# Optimizing a Trainium2 kernel written in Bass

```python
import jax, jax.numpy as jnp
from jax import lax
import numpy as np

D_MODEL = 1024
BATCH = 1
SEQ = 512
DEPTH = 1
DEC_BATCH = 8
DEC_SEQ = 4
PAST_LEN = 512
PAGE_SIZE = 128

HEAD_DIM = 64
HEADS_PER_GROUP = 8
GROUP_WINDOWS = (128, 512, 2048)
GROUP_DILATIONS = (1, 4, 16)
N_GROUPS = 3
ATTN_HEADS = N_GROUPS * HEADS_PER_GROUP
ATTN_WIDTH = ATTN_HEADS * HEAD_DIM
ATTN_OUT_WIDTH = HEADS_PER_GROUP * HEAD_DIM
ROPE_THETA = 10000.0
CONV_DIM = D_MODEL
CONV_WIDTH = 31
N_BRANCHES = 2
IN_COLS = 3 * ATTN_WIDTH + 2 * CONV_DIM + N_BRANCHES * D_MODEL
PEER_HEADS = 8
N_KEYS = 128
N_EXPERTS = N_KEYS * N_KEYS
PEER_TOPK = 16
PEER_QDIM = 256
PEER_HALF = PEER_QDIM // 2
PEER_BLOCK = 256
RMS_EPS = 1e-6
LN_EPS = 1e-5

kernel_name = 'conformer_dilated_peer_hybrid_step'

F32 = jnp.float32

def rms_norm(x, w):
    xf = x.astype(F32)
    y = xf * lax.rsqrt(jnp.mean(xf * xf, axis=-1, keepdims=True) + RMS_EPS)
    return (y * w.astype(F32)).astype(x.dtype)

def layer_norm(x, g, b):
    xf = x.astype(F32)
    mu = jnp.mean(xf, axis=-1, keepdims=True)
    var = jnp.mean(jnp.square(xf - mu), axis=-1, keepdims=True)
    y = (xf - mu) * lax.rsqrt(var + LN_EPS)
    return (y * g.astype(F32) + b.astype(F32)).astype(x.dtype)

def rotary(x, pos):
    half = HEAD_DIM // 2
    inv_freq = ROPE_THETA ** (-jnp.arange(half, dtype=F32) / half)
    ang = pos.astype(F32)[:, None] * inv_freq[None, :]
    cos = jnp.cos(ang)[:, None, :]
    sin = jnp.sin(ang)[:, None, :]
    xf = x.astype(F32)
    x1, x2 = xf[..., :half], xf[..., half:]
    return jnp.concatenate([x1 * cos - x2 * sin, x2 * cos + x1 * sin], axis=-1).astype(x.dtype)

def mixer_inputs(x, pos, norm1_w, w_in, q_norm_w, k_norm_w):
    b, t, _ = x.shape
    h = rms_norm(x, norm1_w)
    z = h @ w_in
    q, k, v, glu_in, gate_in = jnp.split(
        z, [ATTN_WIDTH, 2 * ATTN_WIDTH, 3 * ATTN_WIDTH, 3 * ATTN_WIDTH + 2 * CONV_DIM], axis=-1)
    q = rotary(rms_norm(q.reshape(b, t, ATTN_HEADS, HEAD_DIM), q_norm_w), pos)
    k = rotary(rms_norm(k.reshape(b, t, ATTN_HEADS, HEAD_DIM), k_norm_w), pos)
    v = v.reshape(b, t, ATTN_HEADS, HEAD_DIM)
    a, g = jnp.split(glu_in, 2, axis=-1)
    u = a * jax.nn.sigmoid(g)
    gates = jax.nn.sigmoid(gate_in.astype(F32)).astype(x.dtype).reshape(b, t, N_BRANCHES, D_MODEL)
    return q, k, v, u, gates

def conv_branch(u, left, conv_w, conv_b, ln_g, ln_b, w_conv_proj):
    xp = jnp.concatenate([left, u], axis=1)
    y = lax.conv_general_dilated(
        xp, conv_w[:, None, :], window_strides=(1,), padding='VALID',
        dimension_numbers=('NWC', 'WIO', 'NWC'), feature_group_count=CONV_DIM)
    y = layer_norm(y + conv_b, ln_g, ln_b)
    y = jax.nn.silu(y)
    return y @ w_conv_proj, xp[:, -(CONV_WIDTH - 1):]

def dilated_group_prompt(q, k, v, window, dilation):
    b, t, h, e = q.shape
    m = t // dilation
    steps = window // dilation
    blk = min(steps, m)
    nb = -(-m // blk)
    mp = nb * blk

    def to_res(a):
        a = a.reshape(b, m, dilation, h, e).transpose(0, 2, 1, 3, 4)
        return jnp.pad(a, ((0, 0), (0, 0), (0, mp - m), (0, 0), (0, 0)))

    qr, kr, vr = to_res(q), to_res(k), to_res(v)
    qb = qr.reshape(b, dilation, nb, blk, h, e)

    def band(a):
        prev = jnp.pad(a, ((0, 0), (0, 0), (blk, 0), (0, 0), (0, 0)))[:, :, :mp]
        return jnp.concatenate([prev.reshape(b, dilation, nb, blk, h, e),
                                a.reshape(b, dilation, nb, blk, h, e)], axis=3)

    kb, vb = band(kr), band(vr)
    qi = jnp.arange(blk)[:, None]
    kj = jnp.arange(2 * blk)[None, :]
    diff = blk + qi - kj
    kpos = (jnp.arange(nb)[:, None, None] - 1) * blk + kj[None]
    mask = (diff >= 0)[None] & (diff <= steps)[None] & (kpos >= 0)
    s = jnp.einsum('brnqhe,brnkhe->brnhqk', qb, kb, preferred_element_type=F32) * (HEAD_DIM ** -0.5)
    s = jnp.where(mask[None, None, :, None], s, -jnp.inf)
    lse = jax.nn.logsumexp(s, axis=-1)
    p = jnp.exp(s - lse[..., None]).astype(v.dtype)
    o = jnp.einsum('brnhqk,brnkhe->brnqhe', p, vb).reshape(b, dilation, mp, h, e)[:, :, :m]
    o = o.transpose(0, 2, 1, 3, 4).reshape(b, t, h, e)
    lse = lse.transpose(0, 1, 2, 4, 3).reshape(b, dilation, mp, h)[:, :, :m]
    lse = lse.transpose(0, 2, 1, 3).reshape(b, t, h)
    return o, lse

def dilated_group_sample(q, k_new, v_new, k_buf, v_buf, window, dilation):
    L = k_buf.shape[1]
    s_len = q.shape[1]
    steps = window // dilation
    keys = jnp.concatenate([k_buf, k_new], axis=1)
    vals = jnp.concatenate([v_buf, v_new], axis=1)
    idx = L + jnp.arange(s_len)[:, None] - jnp.arange(steps + 1)[None, :] * dilation
    valid = idx >= 0
    idx = jnp.maximum(idx, 0)
    kg = keys[:, idx]
    vg = vals[:, idx]
    s = jnp.einsum('bshe,bsjhe->bhsj', q, kg, preferred_element_type=F32) * (HEAD_DIM ** -0.5)
    s = jnp.where(valid[None, None], s, -jnp.inf)
    lse = jax.nn.logsumexp(s, axis=-1)
    p = jnp.exp(s - lse[..., None]).astype(v_new.dtype)
    o = jnp.einsum('bhsj,bsjhe->bshe', p, vg)
    return o, lse.transpose(0, 2, 1)

def combine_groups(outs, lses):
    w = jax.nn.softmax(jnp.stack(lses, axis=0), axis=0)
    o = jnp.sum(w[..., None] * jnp.stack(outs, axis=0).astype(F32), axis=0)
    return o.astype(outs[0].dtype)

def attention_prompt(q, k, v):
    outs, lses, states = [], [], []
    t = q.shape[1]
    for g in range(N_GROUPS):
        sl = slice(g * HEADS_PER_GROUP, (g + 1) * HEADS_PER_GROUP)
        o, l = dilated_group_prompt(q[:, :, sl], k[:, :, sl], v[:, :, sl],
                                    GROUP_WINDOWS[g], GROUP_DILATIONS[g])
        outs.append(o)
        lses.append(l)
        keep = min(GROUP_WINDOWS[g], t)
        states.append(jnp.stack([k[:, t - keep:, sl], v[:, t - keep:, sl]], axis=2))
    return combine_groups(outs, lses), states

def attention_sample(q, k, v, caches):
    outs, lses, rows = [], [], []
    for g in range(N_GROUPS):
        sl = slice(g * HEADS_PER_GROUP, (g + 1) * HEADS_PER_GROUP)
        o, l = dilated_group_sample(q[:, :, sl], k[:, :, sl], v[:, :, sl],
                                    caches[g][:, :, 0], caches[g][:, :, 1],
                                    GROUP_WINDOWS[g], GROUP_DILATIONS[g])
        outs.append(o)
        lses.append(l)
        rows.append(jnp.stack([k[:, :, sl], v[:, :, sl]], axis=2))
    return combine_groups(outs, lses), rows

def peer(h, w_peer_q, sub_keys, expert_u, expert_v):
    n = h.shape[0]
    n_pad = -(-n // PEER_BLOCK) * PEER_BLOCK
    hp = jnp.pad(h, ((0, n_pad - n), (0, 0))).reshape(n_pad // PEER_BLOCK, PEER_BLOCK, D_MODEL)

    def block_fn(hb):
        q = (hb @ w_peer_q).reshape(PEER_BLOCK, PEER_HEADS, 2, PEER_HALF)
        s = jnp.einsum('thpc,hpkc->thpk', q, sub_keys, preferred_element_type=F32)
        s1, i1 = lax.top_k(s[:, :, 0], PEER_TOPK)
        s2, i2 = lax.top_k(s[:, :, 1], PEER_TOPK)
        cand = (s1[..., :, None] + s2[..., None, :]).reshape(PEER_BLOCK, PEER_HEADS, PEER_TOPK * PEER_TOPK)
        top_s, top_c = lax.top_k(cand, PEER_TOPK)
        e1 = jnp.take_along_axis(i1, top_c // PEER_TOPK, axis=-1)
        e2 = jnp.take_along_axis(i2, top_c % PEER_TOPK, axis=-1)
        idx = (e1 * N_KEYS + e2).reshape(PEER_BLOCK, PEER_HEADS * PEER_TOPK)
        g = jax.nn.softmax(top_s, axis=-1).reshape(PEER_BLOCK, PEER_HEADS * PEER_TOPK)
        u_rows = jnp.take(expert_u, idx, axis=0)
        a = jnp.einsum('td,tkd->tk', hb, u_rows, preferred_element_type=F32)
        wgt = (g * jax.nn.gelu(a, approximate=False)).astype(hb.dtype)
        v_rows = jnp.take(expert_v, idx, axis=0)
        return jnp.einsum('tk,tkd->td', wgt, v_rows)

    return lax.map(block_fn, hp).reshape(n_pad, D_MODEL)[:n]

def finish_layer(x, heads_out, conv_out, gates, w_attn_proj, w_out, norm2_w,
                 w_peer_q, peer_sub_keys, expert_u, expert_v):
    b, t, _ = x.shape
    attn_out = heads_out.reshape(b, t, ATTN_OUT_WIDTH) @ w_attn_proj
    mixed = gates[:, :, 0] * conv_out + gates[:, :, 1] * attn_out
    x1 = x + mixed @ w_out
    h2 = rms_norm(x1, norm2_w)
    return x1 + peer(h2.reshape(b * t, D_MODEL), w_peer_q, peer_sub_keys,
                     expert_u, expert_v).reshape(b, t, D_MODEL)

def setup_inputs(seed: int = 0) -> dict:
    key = jax.random.key(seed)
    ks = jax.random.split(key, 24)

    def nrm(k, shape, scale):
        return jax.random.normal(k, shape, F32) * scale

    lens = [min(w, PAST_LEN) for w in GROUP_WINDOWS]
    return {
        'x_prompt': nrm(ks[0], (BATCH, SEQ, D_MODEL), 1.0),
        'x_sample': nrm(ks[1], (DEC_BATCH, DEC_SEQ, D_MODEL), 1.0),
        'cache_kv_g1': nrm(ks[2], (DEPTH, DEC_BATCH, lens[0], 2, HEADS_PER_GROUP, HEAD_DIM), 1.0),
        'cache_kv_g2': nrm(ks[3], (DEPTH, DEC_BATCH, lens[1], 2, HEADS_PER_GROUP, HEAD_DIM), 1.0),
        'cache_kv_g3': nrm(ks[4], (DEPTH, DEC_BATCH, lens[2], 2, HEADS_PER_GROUP, HEAD_DIM), 1.0),
        'state_conv': nrm(ks[5], (DEPTH, DEC_BATCH, CONV_WIDTH - 1, CONV_DIM), 0.5),
        'norm1_w': 1.0 + nrm(ks[6], (DEPTH, D_MODEL), 0.02),
        'w_in': nrm(ks[7], (DEPTH, D_MODEL, IN_COLS), D_MODEL ** -0.5),
        'q_norm_w': 1.0 + nrm(ks[8], (DEPTH, HEAD_DIM), 0.02),
        'k_norm_w': 1.0 + nrm(ks[9], (DEPTH, HEAD_DIM), 0.02),
        'conv_w': nrm(ks[10], (DEPTH, CONV_WIDTH, CONV_DIM), CONV_WIDTH ** -0.5),
        'conv_b': nrm(ks[11], (DEPTH, CONV_DIM), 0.02),
        'conv_ln_g': 1.0 + nrm(ks[12], (DEPTH, CONV_DIM), 0.02),
        'conv_ln_b': nrm(ks[13], (DEPTH, CONV_DIM), 0.02),
        'w_conv_proj': nrm(ks[14], (DEPTH, CONV_DIM, D_MODEL), CONV_DIM ** -0.5),
        'w_attn_proj': nrm(ks[15], (DEPTH, ATTN_OUT_WIDTH, D_MODEL), ATTN_OUT_WIDTH ** -0.5),
        'w_out': nrm(ks[16], (DEPTH, D_MODEL, D_MODEL), D_MODEL ** -0.5),
        'norm2_w': 1.0 + nrm(ks[17], (DEPTH, D_MODEL), 0.02),
        'w_peer_q': nrm(ks[18], (DEPTH, D_MODEL, PEER_HEADS * PEER_QDIM), D_MODEL ** -0.5),
        'peer_sub_keys': nrm(ks[19], (DEPTH, PEER_HEADS, 2, N_KEYS, PEER_HALF), PEER_HALF ** -0.5),
        'expert_u': nrm(ks[20], (DEPTH, N_EXPERTS, D_MODEL), D_MODEL ** -0.5),
        'expert_v': nrm(ks[21], (DEPTH, N_EXPERTS, D_MODEL), PEER_HEADS ** -0.5),
    }

def reference(x_prompt, x_sample, cache_kv_g1, cache_kv_g2, cache_kv_g3, state_conv,
              norm1_w, w_in, q_norm_w, k_norm_w, conv_w, conv_b, conv_ln_g, conv_ln_b,
              w_conv_proj, w_attn_proj, w_out, norm2_w, w_peer_q, peer_sub_keys,
              expert_u, expert_v):
    pos_p = jnp.arange(x_prompt.shape[1], dtype=jnp.int32)
    pos_s = PAST_LEN + jnp.arange(x_sample.shape[1], dtype=jnp.int32)
    caches = (cache_kv_g1, cache_kv_g2, cache_kv_g3)
    hp, hs = x_prompt, x_sample
    kv_p = [[], [], []]
    kv_s = [[], [], []]
    conv_p, conv_s = [], []
    for layer in range(DEPTH):
        conv_args = (conv_w[layer], conv_b[layer], conv_ln_g[layer], conv_ln_b[layer], w_conv_proj[layer])
        tail_args = (w_attn_proj[layer], w_out[layer], norm2_w[layer], w_peer_q[layer],
                     peer_sub_keys[layer], expert_u[layer], expert_v[layer])
        q, k, v, u, gates = mixer_inputs(hp, pos_p, norm1_w[layer], w_in[layer], q_norm_w[layer], k_norm_w[layer])
        left = jnp.zeros((hp.shape[0], CONV_WIDTH - 1, CONV_DIM), u.dtype)
        c_out, c_state = conv_branch(u, left, *conv_args)
        a_out, kv_states = attention_prompt(q, k, v)
        hp = finish_layer(hp, a_out, c_out, gates, *tail_args)
        conv_p.append(c_state)
        for g in range(N_GROUPS):
            kv_p[g].append(kv_states[g])
        q, k, v, u, gates = mixer_inputs(hs, pos_s, norm1_w[layer], w_in[layer], q_norm_w[layer], k_norm_w[layer])
        c_out, c_state = conv_branch(u, state_conv[layer], *conv_args)
        a_out, kv_rows = attention_sample(q, k, v, [c[layer] for c in caches])
        hs = finish_layer(hs, a_out, c_out, gates, *tail_args)
        conv_s.append(c_state)
        for g in range(N_GROUPS):
            kv_s[g].append(kv_rows[g])
    return (hp, hs,
            jnp.stack(kv_p[0]), jnp.stack(kv_p[1]), jnp.stack(kv_p[2]), jnp.stack(conv_p),
            jnp.stack(kv_s[0]), jnp.stack(kv_s[1]), jnp.stack(kv_s[2]), jnp.stack(conv_s))


_drawn_inputs = setup_inputs


def setup_inputs(seed=0):
    import zlib

    import numpy as np

    out = dict(_drawn_inputs(seed))
    spreads = {}
    factors = {'q_norm_w': 19.938,
     'k_norm_w': 3.663,
     'conv_ln_g': 7.74,
     'conv_ln_b': 12.724,
     'norm2_w': 8.834}
    for name, (base, spread) in spreads.items():
        noise = np.random.default_rng([zlib.crc32(name.encode()), seed]).standard_normal(out[name].shape)
        drawn = base * np.exp(spread * noise) if base else spread * noise
        out[name] = __import__('jax').numpy.asarray(drawn.astype(out[name].dtype))
    for name, factor in factors.items():
        out[name] = (out[name] * factor).astype(out[name].dtype)
    return out
```

```python
from contextlib import ExitStack

import numpy as np

import concourse.bass as bass
from concourse import mybir

F32 = mybir.dt.float32
U32 = mybir.dt.uint32
ALU = mybir.AluOpType
ACT = mybir.ActivationFunctionType
AX = mybir.AxisListType.X

P = 128
D = 1024
DC = D // P
SEQ = 512
NT = SEQ // P
NB, NS = 8, 4
SMP = NB * NS
TOK = SEQ + SMP
PAST = 512
HD, HG, NG = 64, 8, 3
GW = HG * HD
AW = NG * GW
TAPS = 31
PAD = TAPS - 1
KEYS, TOPK, PH, HALF = 128, 16, 8, 128
WINDOW_ROWS = (128, 512, 512)
RMS_EPS, LN_EPS = 1e-6, 1e-5
NEG = -1.0e30
QK_SCALE = HD ** -0.5
UPT = NT + 1
ACCW = HD + 2

C_ID, C_ONE, C_PREV, C_DIAG, C_STRIDE = 0, 128, 256, 384, 512
C_SELQ = 640
C_SELR = C_SELQ + 2 * SMP - 1
C_NEW1 = C_SELR + 2 * SMP - NS
C_KEEP = C_NEW1 + NS
C_DROP = C_KEEP + NS
C_BACK = C_DROP + NS
C_IOTA = C_BACK + NS
C_FOLD = C_IOTA + TOPK
C_W = C_FOLD + SMP


def shape_constants():
    c = np.zeros((P, C_W), np.float32)
    p, j = np.arange(P)[:, None], np.arange(P)[None, :]
    c[:, C_ID:C_ID + P] = p == j
    c[:, C_ONE:C_ONE + P] = 1.0
    c[:, C_PREV:C_PREV + P] = np.where(j >= p, 0.0, NEG)
    c[:, C_DIAG:C_DIAG + P] = np.where(j <= p, 0.0, NEG)
    c[:, C_STRIDE:C_STRIDE + P] = np.where((j <= p) & ((p - j) % 4 == 0), 0.0, NEG)
    c[:, C_SELQ + SMP - 1] = 1.0
    r = np.arange(P)
    c[r, C_SELR + (SMP - NS) + r % NS] = 1.0
    s = np.arange(NS)[None, :]
    c[:, C_NEW1:C_NEW1 + NS] = np.where(p < s, NEG, 0.0)
    c[:, C_KEEP:C_KEEP + NS] = p % NS == s
    c[:, C_DROP:C_DROP + NS] = np.where(p % NS == s, 0.0, NEG)
    c[:, C_BACK:C_BACK + NS] = np.where(p % NS < s, NEG, 0.0)
    c[:, C_IOTA:C_IOTA + TOPK] = np.arange(TOPK)[None, :]
    c[:, C_FOLD:C_FOLD + SMP] = p % SMP == np.arange(SMP)[None, :]
    half = HD // 2
    freq = (10000.0 ** (-np.arange(half, dtype=np.float64) / half)).astype(np.float32)
    m = np.arange(P)
    pos = [P * i + m for i in range(NT)] + [NT * m + i for i in range(NT)] + [PAST + m % NS]
    ang = (np.stack(pos).astype(np.float32)[:, :, None] * freq).astype(np.float64)
    trig = np.concatenate([np.cos(ang), -np.sin(ang), np.sin(ang)], axis=2).astype(np.float32)
    return c, np.ascontiguousarray(trig.transpose(1, 0, 2))


def tile_rows(i):
    return P if i < NT else SMP


def order_view(rows, g, i):
    return rows[P * i:P * (i + 1)] if g == 0 else rows.rearrange("(m r) x -> r m x", r=NT)[i]


def front(nc, a, sc, cst, yT, trig_d):
    QKV = NG * 3 * UPT
    GLU = 4 * UPT
    UNITS = QKV + 2 * GLU
    SMALL = 7
    VEC = TAPS + 2
    NW = UNITS // UPT
    with ExitStack() as ctx:
        def sb(name, shape, dt=F32):
            return ctx.enter_context(nc.sbuf_tensor("f_" + name, shape, dt))

        def ps(name, shape):
            return ctx.enter_context(nc.psum_tensor("f_" + name, shape, F32))

        def sem(name):
            return ctx.enter_context(nc.semaphore("f_" + name))

        hT = sb("hT", [P, DC, TOK])
        wsb = sb("w", [P, 2, DC, 512])
        trig = sb("trig", [P, 9, 96])
        qkw = sb("qkw", [P, 2, HD])
        rc = sb("rc", [P, 2, 9, HD])
        rs = sb("rs", [P, 2, 9, HD])
        xss = sb("xss", [P, 4])
        half_m = sb("half_m", [P, HG])
        sq = sb("sq", [P, 512])
        ss = sb("ss", [P, 2, HG])
        qn = sb("qn", [P, 512])
        t1 = sb("t1", [P, 512])
        t2 = sb("t2", [P, 512])
        qkr = sb("qkr", [P, 3, 512])
        qT = sb("qT", [P, 2, 4, SEQ])
        kT = sb("kT", [P, 2, 4, SEQ])
        vsb = sb("v", [P, 2, UPT, GW])
        s_sb = sb("s", [P, 4, 512])
        pt = sb("pt", [P, 4, 512])
        nm = sb("nm", [P, 4, 4])
        st = sb("st", [P, 4, 4, ACCW])
        uT = sb("uT", [P, DC, PAD + SEQ])
        uS = sb("uS", [P, DC, NB, PAD + NS])
        sg = sb("sg", [P, 2, 512])
        gst = sb("gst", [P, 2, 512])
        vec = sb("vec", [P, DC, VEC])
        cw, cb, n1 = vec[:, :, 0:TAPS], vec[:, :, TAPS], vec[:, :, TAPS + 1]
        rows33 = gst[0:VEC, :, :].rearrange("p a b -> p (a b)")
        cin = qkr[:, 0:2, :].rearrange("p a b -> p (a b)")

        xt = qT[:, 1, :, :].rearrange("p (a b) c -> p a (b c)", a=2)
        ht = pt[:, 0:2, :].rearrange("p a b -> p (a b)")
        squares = s_sb[:, 0:2, :].rearrange("p a b -> p (a b)")

        zp = [ps("z0", [P, 512]), ps("z1", [P, 512])]
        ap_ = [ps("a0", [P, 512]), ps("a1", [P, 512])]
        tp = ps("t", [P, 512])
        pp = ps("p", [P, 2, 512])
        op = ps("o", [P, 512])
        ident = cst[:, C_ID:C_ID + P]

        small_in = sem("small_in")
        x_in = [sem("x_in0"), sem("x_in1")]
        sq_done = sem("sq_done")
        x_var = sem("x_var")
        h_ready = sem("h_ready")
        hp_ready = sem("hp_ready")
        hT_ready = sem("hT_ready")
        half_ready = sem("half_ready")
        chain = sem("chain")
        w_in = [sem("w_in0"), sem("w_in1")]
        z_ready = sem("z_ready")
        z_free_v = sem("z_free_v")
        z_free_a = sem("z_free_a")
        z_sq = sem("z_sq")
        z_ss = sem("z_ss")
        z_rstd = sem("z_rstd")
        r_ready = sem("r_ready")
        r_out = [sem(f"r_out{i}") for i in range(3)]
        tr_ready = sem("tr_ready")
        tr_out = sem("tr_out")
        v_ready = sem("v_ready")
        v_out = [sem("v_out0"), sem("v_out1")]
        s_ready = sem("s_ready")
        m_ready = sem("m_ready")
        e_ready = sem("e_ready")
        p_ready = sem("p_ready")
        pt_ready = sem("pt_ready")
        o_ready = sem("o_ready")
        st_ready = sem("st_ready")
        st_out = [sem(f"st_out{i}") for i in range(4)]
        sg_ready = sem("sg_ready")
        u_ready = sem("u_ready")
        g_ready = sem("g_ready")
        g_out = [sem("g_out0"), sem("g_out1")]
        cin_in = sem("cin_in")
        cp_ready = sem("cp_ready")
        cs_ready = sem("cs_ready")
        u_zero = sem("u_zero")
        so_ready = sem("so_ready")
        sc_ready = sem("sc_ready")
        so_out = [sem("so_out0"), sem("so_out1")]

        st4 = hT[:, :, 0:NB * PAD].rearrange("p c (b r) -> p c b r", b=NB)
        w_v = a["w_in"][0].rearrange("(k p) c -> p k c", p=P)

        def w_cols(m):
            if m < 9:
                g, c = divmod(m, 3)
                return [(c * AW + g * GW, 512, 0)]
            if m < 13:
                base = 3 * AW + 256 * (m - 9)
                return [(base + D, 256, 0), (base, 256, 256)]
            return [(3 * AW + 2 * D + 512 * (m - 13), 512, 0)]

        def w_count(m):
            return 16 * sum(len(w_cols(j)) for j in range(m % 2, m + 1, 2))

        def unit(n):
            m, i = divmod(n, UPT)
            return m, m // 3, m % 3, i

        def freed_by_scalar(n):
            if n < QKV:
                return False
            if n < QKV + GLU:
                return (n - QKV) % UPT in (0, 1)
            return True

        def wait_bank(eng, n):
            if n >= 2:
                k = sum(freed_by_scalar(j) == freed_by_scalar(n - 2) for j in range(n - 1))
                eng.wait_ge(z_free_a if freed_by_scalar(n - 2) else z_free_v, k)

        qk_units = [n for n in range(QKV) if unit(n)[2] < 2]
        tr_units = [n for n in qk_units if unit(n)[3] < NT]

        def stored(n):
            m, g, c, i = unit(n)
            return i == NT or (c == 1 and (g > 0 or i == NT - 1))

        def r_out_count(e):
            return 16 * sum(stored(qk_units[j]) for j in range(e % 3, e + 1, 3))

        def sub_batches(g, s):
            i, par = divmod(s, 2)
            heads = [par + 2 * j for j in range(4)]
            keys = [i - 1, i] if g == 0 and i else [i]
            return [(heads[:2], keys), (heads[2:], keys)] if g == 0 else [(heads, keys)]

        subs = [(g, s, b) for g in range(NG) for s in range(8) for b in range(len(sub_batches(g, s)))]
        sub_no = {k: q for q, k in enumerate(subs)}

        def attention_steps(n):
            g = n // 15 - 1
            if g < 0 or g >= NG:
                return None
            s = n - 15 * (g + 1)
            return g, (s if s < 8 else None), (s - 1 if 1 <= s < 9 else None), (s - 2 if 2 <= s < 10 else None)

        block = ctx.enter_context(nc.Block())

        @block.sync
        def _(eng):
            eng.dma_start(xt[:, 0, :], a["x_prompt"][0, 0:P, :]).then_inc(x_in[0], 16)
            eng.dma_start(cst[:, :], a["consts"]).then_inc(small_in, 16)
            eng.dma_start(rows33[0:TAPS, :], a["conv_w"][0]).then_inc(small_in, 16)
            eng.dma_start(rows33[TAPS:TAPS + 1, :], a["conv_b"]).then_inc(small_in, 16)
            eng.dma_start(rows33[TAPS + 1:TAPS + 2, :], a["norm1_w"]).then_inc(small_in, 16)
            eng.dma_start(trig[:, :, :], trig_d).then_inc(small_in, 16)
            eng.dma_start(qkw[:, 0, :], a["q_norm_w"].to_broadcast([P, HD])).then_inc(small_in, 16)
            eng.dma_start(qkw[:, 1, :], a["k_norm_w"].to_broadcast([P, HD])).then_inc(small_in, 16)
            for i in range(1, UPT):
                if i >= 2:
                    eng.wait_ge(h_ready, i - 1)
                src = a["x_prompt"][0, P * i:P * (i + 1), :] if i < NT else a["x_sample"].rearrange("b s d -> (b s) d")
                eng.dma_start(xt[0:tile_rows(i), i % 2, :], src).then_inc(x_in[i % 2], 16)
                if i == 1:
                    for j in range(2):
                        eng.dma_start(wsb[:, j, :, :], w_v[:, :, w_cols(j)[0][0]:w_cols(j)[0][0] + 512]).then_inc(w_in[j], 16)
            for m in range(2, NW):
                eng.wait_ge(z_ready, UPT * (m - 1))
                for col, width, at in w_cols(m):
                    eng.dma_start(wsb[:, m % 2, :, at:at + width], w_v[:, :, col:col + width]).then_inc(w_in[m % 2], 16)

        @block.gpsimd
        def _(eng):
            eng.memset(half_m[:, :], -0.5).then_inc(half_ready, 1)
            eng.memset(uT[:, :, 0:PAD], 0.0).then_inc(u_zero, 1)
            eng.wait_ge(half_ready, 1)
            for j in range(2):
                if j:
                    eng.wait_ge(cp_ready, 1)
                eng.dma_start(cin[0:4 * PAD, :], a["state_conv"][0, 4 * j:4 * j + 4].rearrange("b r d -> (b r) d")).then_inc(cin_in, 16)
            for i in range(UPT):
                n = tile_rows(i)
                eng.wait_ge(sq_done, i + 1)
                eng.tensor_scalar(xss[0:n, 1:2], xss[0:n, 0:1], 1.0 / D, RMS_EPS, ALU.mult, ALU.add).then_inc(half_ready, 1)
                eng.wait_ge(half_ready, 2 + i)
                if i:
                    eng.wait_ge(h_ready, i)
                eng.tensor_tensor(xss[0:n, 2:3], xss[0:n, 1:2], half_m[0:n, 0:1], ALU.pow).then_inc(x_var, 1)
                eng.wait_ge(x_var, i + 1)
            own = 1 + UPT
            e = v = 0
            for n in range(QKV + 10):
                if n < QKV:
                    m, g, c, i = unit(n)
                    rows = tile_rows(i)
                if n < QKV and c < 2:
                    eng.wait_ge(z_ss, e + 1)
                    eng.tensor_scalar(ss[0:rows, 1, :], ss[0:rows, 0, :], 1.0 / HD, RMS_EPS, ALU.mult, ALU.add).then_inc(half_ready, 1)
                    own += 1
                    eng.wait_ge(half_ready, own)
                    eng.tensor_tensor(ss[0:rows, 1, :], ss[0:rows, 1, :], half_m[0:rows, :], ALU.pow).then_inc(z_rstd, 1)
                    eng.wait_ge(z_rstd, e + 1)
                    if stored(n):
                        eng.wait_ge(r_ready, e + 1)
                        src = qkr[0:rows, e % 3, :]
                        if i < NT:
                            dst = a[f"kv{g}p"][0, 0].rearrange("t w h e -> t w (h e)")[:, 0, :]
                            dst = dst if g == 0 else order_view(dst, g, i)
                        elif c == 0:
                            dst = sc["q_smp"][g]
                        else:
                            dst = a[f"kv{g}s"][0].rearrange("b s w h e -> (b s) w (h e)")[:, 0, :]
                        eng.dma_start(dst, src).then_inc(r_out[e % 3], 16)
                    e += 1
                elif n < QKV:
                    if g > 0 or i >= NT - 1:
                        eng.wait_ge(v_ready, v + 1)
                        src = vsb[0:rows, g % 2, i, :]
                        if i < NT:
                            dst = a[f"kv{g}p"][0, 0].rearrange("t w h e -> t w (h e)")[:, 1, :]
                            dst = dst if g == 0 else order_view(dst, g, i)
                        else:
                            dst = a[f"kv{g}s"][0].rearrange("b s w h e -> (b s) w (h e)")[:, 1, :]
                        eng.dma_start(dst, src).then_inc(v_out[g % 2], 16)
                    v += 1
                steps = attention_steps(n)
                if steps and steps[3] is not None:
                    g, s = steps[0], steps[3]
                    o = 8 * g + s
                    eng.wait_ge(st_ready, o + 1)
                    dst = order_view(sc["attn"][g][:, (s % 2) * 4 * ACCW:(s % 2 + 1) * 4 * ACCW], g, s // 2)
                    eng.dma_start(dst, st[:, o % 4, :, :].rearrange("p h w -> p (h w)")).then_inc(st_out[o % 4], 16)
            for t in range(GLU):
                eng.wait_ge(g_ready, t + 1)
                m, i = divmod(t, UPT)
                if i < NT:
                    eng.dma_start(sc["gates"][4 * m + i][:, 0:SEQ], gst[:, t % 2, :]).then_inc(g_out[t % 2], 16)
                else:
                    eng.dma_start(sc["gates"][4 * m:4 * m + 4][:, :, SEQ:TOK].rearrange("c p t -> p c t"),
                                  gst[:, t % 2, 0:4 * SMP].rearrange("p (c t) -> p c t", c=4)).then_inc(g_out[t % 2], 16)
            for j in range(3):
                eng.wait_ge(sc_ready, 2 * j + 2)
                if j == 0:
                    eng.dma_start(a["conv_p"][0, 0], xt[0:PAD, 0, :]).then_inc(so_out[0], 16)
                else:
                    eng.dma_start(a["conv_s"][0, 4 * j - 4:4 * j].rearrange("b r d -> (b r) d"), xt[0:4 * PAD, j % 2, :]).then_inc(so_out[j % 2], 16)
            eng.wait_ge(so_out[0], 32)
            eng.wait_ge(so_out[1], 16)
            for j in range(2):
                eng.wait_ge(g_out[j], 16 * GLU // 2)
                eng.wait_ge(v_out[j], 16 * sum(2 if g == 0 else UPT for g in range(j, NG, 2)))
            for j in range(3):
                eng.wait_ge(r_out[j], r_out_count(len(qk_units) - 3 + j))
            for j in range(4):
                eng.wait_ge(st_out[j], 16 * 6)

        @block.tensor
        def _(eng):
            eng.wait_ge(small_in, 16 * SMALL)
            turn = 0
            for j in range(2):
                eng.wait_ge(cin_in, 16 * (j + 1))
                if j:
                    eng.wait_ge(cs_ready, 1)
                for c in range(DC):
                    mm = eng.transpose(pp[:, c // 4, (c % 4) * P:(c % 4) * P + 4 * PAD], cin[0:4 * PAD, c * P:(c + 1) * P], cst[0:4 * PAD, C_ID:C_ID + 4 * PAD])
                mm.then_inc(cp_ready, 1)
            eng.wait_ge(cs_ready, 2)
            for c in range(DC):
                mm = eng.transpose(pp[:, c // 4, (c % 4) * P:(c % 4) * P + VEC], rows33[:, c * P:(c + 1) * P], cst[0:VEC, C_ID:C_ID + VEC])
            mm.then_inc(cp_ready, 1)
            for i in range(UPT):
                n = tile_rows(i)
                eng.wait_ge(h_ready, i + 1)
                eng.wait_ge(*((hT_ready, i) if i else (cs_ready, 3)))
                for c in range(DC):
                    mm = eng.transpose(pp[:, c // 4, (c % 4) * P:(c % 4) * P + n], ht[0:n, c * P:(c + 1) * P], cst[0:n, C_ID:C_ID + n])
                mm.then_inc(hp_ready, 1)
            eng.wait_ge(hT_ready, UPT)
            t = 0
            o = 0
            for n in range(UNITS):
                m, g, c, i = unit(n)
                if i == 0:
                    eng.wait_ge(w_in[m % 2], w_count(m))
                wait_bank(eng, n)
                z = zp[n % 2]
                if n < QKV:
                    for k in range(DC):
                        tok = hT[:, k, SEQ:TOK] if i == NT else hT[:, k, P * i:P * (i + 1)] if g == 0 else hT[:, k, i:SEQ:NT]
                        mm = eng.matmul(z[0:tile_rows(i), :], tok, wsb[:, m % 2, k, :], start=(k == 0), stop=(k == DC - 1))
                elif i < NT:
                    col = i * P
                    for k in range(DC):
                        mm = eng.matmul(z[:, :], wsb[:, m % 2, k, col:col + P], hT[:, k, 0:SEQ], start=(k == 0), stop=(k == DC - 1))
                else:
                    for j in range(4):
                        for k in range(DC):
                            mm = eng.matmul(z[:, SMP * j:SMP * (j + 1)], wsb[:, m % 2, k, P * j:P * (j + 1)], hT[:, k, SEQ:TOK],
                                            start=(k == 0), stop=(k == DC - 1))
                mm.then_inc(z_ready, 1)
                if n - 1 in tr_units:
                    e = qk_units.index(n - 1)
                    eng.wait_ge(r_ready, e + 1)
                    if t:
                        eng.wait_ge(tr_out, t)
                    for j in range(4):
                        mm = eng.transpose(tp[:, P * j:P * (j + 1)], qkr[:, e % 3, P * j:P * (j + 1)], ident)
                    mm.then_inc(tr_ready, 1)
                    t += 1
                steps = attention_steps(n)
                if steps:
                    ga, s_, t_, o_ = steps
                    if s_ is not None:
                        ia = s_ // 2
                        eng.wait_ge(tr_out, 8 * (ga + 1))
                        for b, (heads, keys) in enumerate(sub_batches(ga, s_)):
                            q = sub_no[ga, s_, b]
                            if q >= 2:
                                eng.wait_ge(m_ready, q - 1)
                            nk = len(keys)
                            for j, h in enumerate(heads):
                                r = (h % 2) * HD
                                mm = eng.matmul(ap_[q % 2][:, j * nk * P:(j + 1) * nk * P], qT[r:r + HD, ga % 2, h // 2, P * ia:P * (ia + 1)],
                                                kT[r:r + HD, ga % 2, h // 2, P * keys[0]:P * (keys[-1] + 1)], start=True, stop=True)
                            mm.then_inc(s_ready, 1)
                    if t_ is not None:
                        for b, (heads, keys) in enumerate(sub_batches(ga, t_)):
                            q = sub_no[ga, t_, b]
                            eng.wait_ge(e_ready, q + 1)
                            if q >= 2:
                                eng.wait_ge(pt_ready, q - 1)
                            for j in range(len(heads) * len(keys)):
                                mm = eng.transpose(pp[:, q % 2, P * j:P * (j + 1)], s_sb[:, q % 4, P * j:P * (j + 1)], ident)
                            mm.then_inc(p_ready, 1)
                    if o_ is not None:
                        if o:
                            eng.wait_ge(st_ready, o)
                        eng.wait_ge(v_ready, UPT * (ga + 1))
                        for b, (heads, keys) in enumerate(sub_batches(ga, o_)):
                            q = sub_no[ga, o_, b]
                            eng.wait_ge(pt_ready, q + 1)
                            nk = len(keys)
                            for j, h in enumerate(heads):
                                at = (b * len(heads) + j) * HD
                                for x, key in enumerate(keys):
                                    mm = eng.matmul(op[:, at:at + HD], pt[:, q % 4, (j * nk + x) * P:(j * nk + x + 1) * P],
                                                    vsb[:, ga % 2, key, h * HD:(h + 1) * HD], start=(x == 0), stop=(x == nk - 1))
                        mm.then_inc(o_ready, 1)
                        o += 1
            eng.wait_ge(u_ready, 13)
            eng.wait_ge(pt_ready, len(subs))
            for j in range(3):
                if j:
                    eng.wait_ge(sc_ready, 2 * j)
                w = PAD if j == 0 else 4 * PAD
                for c in range(DC):
                    src = uT[:, c, SEQ:SEQ + PAD] if j == 0 else st4[:, c, 4 * j - 4:4 * j, :].rearrange("p b r -> p (b r)")
                    mm = eng.transpose(pp[0:w, c // 4, (c % 4) * P:(c % 4 + 1) * P], src, ident)
                mm.then_inc(so_ready, 1)

        @block.scalar
        def _(eng):
            for i in range(UPT):
                n = tile_rows(i)
                eng.wait_ge(x_in[i % 2], 16 * (i // 2 + 1))
                if i:
                    eng.wait_ge(h_ready, i)
                eng.activation(squares[0:n, :], xt[0:n, i % 2, :], ACT.Square, accum_out=xss[0:n, 0:1]).then_inc(sq_done, 1)
            t = e = 0
            for n in range(UNITS):
                m, g, c, i = unit(n)
                rows = tile_rows(i)
                if n < QKV and c < 2:
                    eng.wait_ge(z_ready, n + 1)
                    if e:
                        eng.wait_ge(z_ss, e)
                    eng.activation(sq[0:rows, :], zp[n % 2][0:rows, :], ACT.Square).then_inc(z_sq, 1)
                    e += 1
                elif QKV <= n < QKV + GLU:
                    k = (n - QKV) // UPT
                    if i < 2:
                        eng.wait_ge(z_ready, n + 1)
                        if k:
                            eng.wait_ge(u_ready, 3 * k)
                        eng.activation(sg[:, i, :], zp[n % 2][:, :], ACT.Sigmoid).then_inc(z_free_a, 1)
                    elif i == NT:
                        eng.wait_ge(z_ready, n + 1)
                        eng.wait_ge(u_ready, 3 * k + 2)
                        eng.activation(sg[:, 0, 0:2 * SMP], zp[n % 2][:, 0:2 * SMP], ACT.Sigmoid).then_inc(sg_ready, 1)
                elif n >= QKV + GLU:
                    k = n - QKV - GLU
                    w = 512 if i < NT else 4 * SMP
                    eng.wait_ge(z_ready, n + 1)
                    if k >= 2:
                        eng.wait_ge(g_out[k % 2], 16 * (k // 2))
                        eng.wait_ge(g_ready, k - 1)
                    eng.activation(gst[:, k % 2, 0:w], zp[n % 2][:, 0:w], ACT.Sigmoid).then_inc(g_ready, 1)
                    eng.wait_ge(g_ready, k + 1)
                    eng.sem_inc(z_free_a, 1)
                if n - 1 in tr_units:
                    gt, ct, it = unit(n - 1)[1:]
                    eng.wait_ge(tr_ready, t + 1)
                    dst = (qT if ct == 0 else kT)[:, gt % 2, :, P * it:P * (it + 1)]
                    if gt >= 2:
                        eng.wait_ge(s_ready, sub_no[gt - 2, 7, len(sub_batches(gt - 2, 7)) - 1] + 1)
                    eng.activation(dst, tp[:, :].rearrange("p (a b) -> p a b", a=4), ACT.Copy).then_inc(tr_out, 1)
                    t += 1
                steps = attention_steps(n)
                if steps:
                    ga, s_, t_, o_ = steps
                    if t_ is not None:
                        for b, (heads, keys) in enumerate(sub_batches(ga, t_)):
                            q = sub_no[ga, t_, b]
                            w = P * len(heads) * len(keys)
                            eng.wait_ge(p_ready, q + 1)
                            if ga * 8 + t_ >= 2:
                                eng.wait_ge(o_ready, ga * 8 + t_ - 1)
                            eng.activation(pt[:, q % 4, 0:w], pp[:, q % 2, 0:w], ACT.Copy).then_inc(pt_ready, 1)
                    if s_ is not None:
                        for b, (heads, keys) in enumerate(sub_batches(ga, s_)):
                            q = sub_no[ga, s_, b]
                            slot = (8 * ga + s_) % 4
                            w = P * len(keys)
                            eng.wait_ge(m_ready, q + 1)
                            for j in range(len(heads)):
                                ins = eng.activation(s_sb[:, q % 4, j * w:(j + 1) * w], s_sb[:, q % 4, j * w:(j + 1) * w], ACT.Exp,
                                                     bias=nm[:, q % 4, j:j + 1], accum_out=st[:, slot, b * len(heads) + j, HD + 1:HD + 2])
                            ins.then_inc(e_ready, 1)
            for j in range(3):
                w = PAD if j == 0 else 4 * PAD
                eng.wait_ge(so_ready, j + 1)
                if j == 2:
                    eng.wait_ge(so_out[0], 16)
                for b in range(2):
                    eng.activation(xt[0:w, j % 2, 512 * b:512 * (b + 1)], pp[0:w, b, :], ACT.Copy).then_inc(sc_ready, 1)

        @block.vector
        def _(eng):
            count = {"chain": 0}

            def link(ins):
                count["chain"] += 1
                ins.then_inc(chain, 1)
                eng.wait_ge(chain, count["chain"])

            def signal(ins, s, n):
                ins.then_inc(s, 1)
                eng.wait_ge(s, n)

            eng.wait_ge(small_in, 16 * SMALL)
            for w in range(2):
                lo, hi = (qkw[:, w, x:x + 32].unsqueeze(1).to_broadcast([P, 9, 32]) for x in (0, 32))
                link(eng.tensor_tensor(rc[:, w, :, 0:32], trig[:, :, 0:32], lo, ALU.mult))
                link(eng.tensor_tensor(rc[:, w, :, 32:64], trig[:, :, 0:32], hi, ALU.mult))
                link(eng.tensor_tensor(rs[:, w, :, 0:32], trig[:, :, 32:64], hi, ALU.mult))
                link(eng.tensor_tensor(rs[:, w, :, 32:64], trig[:, :, 64:96], lo, ALU.mult))
            for j in range(2):
                eng.wait_ge(cp_ready, j + 1)
                for c2 in range(2):
                    src = pp[:, c2, :].rearrange("p (c x) -> p c x", c=4)[:, :, 0:4 * PAD]
                    for c in range(4):
                        ins = eng.tensor_copy(uS[:, 4 * c2 + c, 4 * j:4 * j + 4, 0:PAD], src[:, c, :].rearrange("p (b r) -> p b r", b=4))
                        if c2 == 1 and c == 3:
                            signal(ins, cs_ready, j + 1)
                        else:
                            link(ins)
            eng.wait_ge(cp_ready, 3)
            for b in range(2):
                ins = eng.tensor_copy(vec[:, 4 * b:4 * b + 4, :], pp[:, b, :].rearrange("p (c x) -> p c x", c=4)[:, :, 0:VEC])
                if b:
                    signal(ins, cs_ready, 3)
                else:
                    link(ins)
            for i in range(UPT):
                n = tile_rows(i)
                eng.wait_ge(x_var, i + 1)
                if i:
                    eng.wait_ge(hp_ready, i)
                signal(eng.tensor_scalar(ht[0:n, :], xt[0:n, i % 2, :], xss[0:n, 2:3], None, ALU.mult), h_ready, i + 1)
                eng.wait_ge(hp_ready, i + 1)
                at = P * i
                for b in range(2):
                    ins = eng.tensor_tensor(hT[:, 4 * b:4 * b + 4, at:at + n], pp[:, b, :].rearrange("p (c x) -> p c x", c=4)[:, :, 0:n],
                                            n1[:, 4 * b:4 * b + 4].unsqueeze(2).to_broadcast([P, 4, n]), ALU.mult)
                    if b:
                        signal(ins, hT_ready, i + 1)
                    else:
                        link(ins)
            e = v = u = o = fv = 0
            for n in range(QKV + GLU):
                m, g, c, i = unit(n)
                rows = tile_rows(i)
                z = zp[n % 2]
                eng.wait_ge(z_ready, n + 1)
                if n < QKV and c < 2:
                    table = 8 if i == NT else i if g == 0 else NT + i
                    eng.wait_ge(z_sq, e + 1)
                    signal(eng.tensor_reduce(ss[0:rows, 0, :], sq[0:rows, :].rearrange("p (h d) -> p h d", h=HG), AX, ALU.add), z_ss, e + 1)
                    eng.wait_ge(z_rstd, e + 1)
                    fv += 1
                    signal(eng.tensor_tensor(qn[0:rows, :].rearrange("p (h d) -> p h d", h=HG), z[0:rows, :].rearrange("p (h d) -> p h d", h=HG),
                                             ss[0:rows, 1, :].unsqueeze(2).to_broadcast([rows, HG, HD]), ALU.mult), z_free_v, fv)
                    x = qn[0:rows, :].rearrange("p (h w d) -> p h w d", h=HG, w=2)
                    y = t2[0:rows, :].rearrange("p (h w d) -> p h w d", h=HG, w=2)
                    link(eng.tensor_tensor(t1[0:rows, :].rearrange("p (h d) -> p h d", h=HG), qn[0:rows, :].rearrange("p (h d) -> p h d", h=HG),
                                           rc[0:rows, c, table, :].unsqueeze(1).to_broadcast([rows, HG, HD]), ALU.mult))
                    for w in range(2):
                        link(eng.tensor_tensor(y[:, :, w, :], x[:, :, 1 - w, :],
                                               rs[0:rows, c, table, 32 * w:32 * w + 32].unsqueeze(1).to_broadcast([rows, HG, 32]), ALU.mult))
                    if e >= 3:
                        eng.wait_ge(tr_ready, sum(j in tr_units for j in qk_units[:e - 2]))
                        if r_out_count(e - 3):
                            eng.wait_ge(r_out[e % 3], r_out_count(e - 3))
                    e += 1
                    signal(eng.tensor_tensor(qkr[0:rows, (e - 1) % 3, :], t1[0:rows, :], t2[0:rows, :], ALU.add), r_ready, e)
                elif n < QKV:
                    if g >= 2:
                        eng.wait_ge(o_ready, 8 * (g - 1))
                        eng.wait_ge(v_out[g % 2], 16 * 2)
                    v += 1
                    ins = eng.tensor_copy(vsb[0:rows, g % 2, i, :], z[0:rows, :])
                    signal(ins, v_ready, v)
                    fv += 1
                    eng.sem_inc(z_free_v, 1)
                else:
                    k = (n - QKV) // UPT
                    if i in (2, 3):
                        ch = 2 * k + i - 2
                        eng.wait_ge(z_free_a, 2 * k + i - 1)
                        u += 1
                        signal(eng.tensor_tensor(uT[:, ch, PAD:PAD + SEQ], z[:, :], sg[:, i - 2, :], ALU.mult), u_ready, u)
                        fv += 1
                        eng.sem_inc(z_free_v, 1)
                    elif i == NT:
                        eng.wait_ge(sg_ready, k + 1)
                        u += 1
                        for ch in range(2):
                            ins = eng.tensor_tensor(uS[:, 2 * k + ch, :, PAD:PAD + NS], z[:, (2 + ch) * SMP:(3 + ch) * SMP].rearrange("p (b s) -> p b s", b=NB),
                                                    sg[:, 0, ch * SMP:(ch + 1) * SMP].rearrange("p (b s) -> p b s", b=NB), ALU.mult)
                            if ch == 0:
                                link(ins)
                        signal(ins, u_ready, u)
                        fv += 1
                        eng.sem_inc(z_free_v, 1)
                steps = attention_steps(n)
                if steps:
                    ga, s_, t_, o_ = steps
                    if s_ is not None:
                        for b, (heads, keys) in enumerate(sub_batches(ga, s_)):
                            q = sub_no[ga, s_, b]
                            so = 8 * ga + s_
                            nh, w = len(heads), P * len(keys)
                            mask = cst[:, C_STRIDE:C_STRIDE + P] if ga == 2 else cst[:, C_DIAG + P - w:C_DIAG + P]
                            eng.wait_ge(s_ready, q + 1)
                            if q >= 4:
                                eng.wait_ge(p_ready, q - 3)
                            if so >= 4:
                                eng.wait_ge(st_out[so % 4], 16 * (so // 4))
                            sv = s_sb[:, q % 4, 0:nh * w].rearrange("p (h k) -> p h k", h=nh)
                            link(eng.scalar_tensor_tensor(out=sv, in0=ap_[q % 2][:, 0:nh * w].rearrange("p (h k) -> p h k", h=nh), scalar=QK_SCALE,
                                                          in1=mask.unsqueeze(1).to_broadcast([P, nh, w]), op0=ALU.mult, op1=ALU.add))
                            mx = st[:, so % 4, b * nh:(b + 1) * nh, HD:HD + 1]
                            link(eng.tensor_reduce(mx, sv, AX, ALU.max))
                            signal(eng.tensor_scalar(nm[:, q % 4, 0:nh], mx.rearrange("p h o -> p (h o)"), -1.0, None, ALU.mult), m_ready, q + 1)
                    if o_ is not None:
                        eng.wait_ge(o_ready, o + 1)
                        eng.wait_ge(e_ready, sub_no[ga, o_, len(sub_batches(ga, o_)) - 1] + 1)
                        signal(eng.tensor_copy(st[:, o % 4, :, 0:HD], op[:, 0:4 * HD].rearrange("p (h d) -> p h d", h=4)), st_ready, o + 1)
                        o += 1
            eng.wait_ge(z_ready, UNITS)
            for c in range(DC):
                ins = eng.tensor_copy(st4[:, c, :, :], uS[:, c, :, NS:NS + PAD])
                if c == DC - 1:
                    signal(ins, u_ready, u + 1)
                else:
                    link(ins)
            eng.wait_ge(u_zero, 1)
            base = count["chain"]
            steps = 0
            for c0 in range(0, DC, 4):
                for tap in range(TAPS):
                    for c in range(c0, c0 + 4):
                        for out, src in ((yT[:, c, 0:SEQ], uT[:, c, tap:tap + SEQ]),
                                         (yT[:, c, SEQ:TOK].rearrange("p (b s) -> p b s", b=NB), uS[:, c, :, tap:tap + NS])):
                            if tap:
                                eng.wait_ge(chain, base + steps - 7)
                                ins = eng.scalar_tensor_tensor(out=out, in0=src, scalar=cw[:, c, tap:tap + 1], in1=out, op0=ALU.mult, op1=ALU.add)
                            else:
                                ins = eng.tensor_scalar(out, src, cw[:, c, 0:1], cb[:, c:c + 1], ALU.mult, ALU.add)
                            ins.then_inc(chain, 1)
                            steps += 1
            eng.wait_ge(chain, base + steps)


def sample_attention(nc, a, sc, cst, hs):
    with ExitStack() as ctx:
        def sb(name, shape, dt=F32):
            return ctx.enter_context(nc.sbuf_tensor("s_" + name, shape, dt))

        def sem(name):
            return ctx.enter_context(nc.semaphore("s_" + name))

        k1 = sb("k1", [P, 2, GW])
        k2 = sb("k2", [P, 2, NS, GW])
        k3 = sb("k3", [P, 2, GW])
        q1 = sb("q1", [P, 2, NS, GW])
        q2 = sb("q2", [P, 2, NS, GW])
        q3 = sb("q3", [P, 2, GW])
        v1 = sb("v1", [P, 2, GW])
        v2 = sb("v2", [P, 2, NS, GW])
        v3 = sb("v3", [P, 2, GW])
        pr1 = sb("pr1", [P, 2, NS, GW])
        pr2 = sb("pr2", [P, 2, NS, GW])
        pr3 = sb("pr3", [P, 2, GW])
        S = sb("S", [P, NG, HG, SMP])
        S3 = sb("S3", [P, HG, NB])
        pw = sb("pw", [P, 2, HG])
        R = sb("R", [SMP, NG * HG, P])
        PT = sb("PT", [P, NG * HG, SMP])
        new = sb("new", [SMP, 6, 2 * GW])
        qn = sb("q", [SMP, NG, GW])
        N = sb("N", [SMP, 6, HG])
        pn = sb("pn", [SMP, 6, GW])
        mx = sb("mx", [SMP, NG * HG])
        M = sb("M", [SMP, 3, HG])
        den = sb("den", [SMP, 3, HG])
        rp = [ctx.enter_context(nc.psum_tensor(f"s_r{i}", [P, 512], F32)) for i in range(6)]
        acc = ctx.enter_context(nc.psum_tensor("s_acc", [P, 512], F32))

        k_in = [sem("k_in0"), sem("k_in1")]
        v_in = [sem("v_in0"), sem("v_in1")]
        new_zero = sem("new_zero")
        new_in = sem("new_in")
        chain = sem("chain")
        pk_ready = sem("pk_ready")
        k_used = sem("k_used")
        S_ready = sem("S_ready")
        r_ready = sem("r_ready")
        x_ready = sem("x_ready")
        e_ready = sem("e_ready")
        b_ready = sem("b_ready")
        PT_ready = sem("PT_ready")
        v_prod = sem("v_prod")
        v_prod2 = sem("v_prod2")
        v_sum = sem("v_sum")

        def cache(g, b, w):
            rows = a[f"cache_kv_g{g + 1}"][0, b].rearrange("l w h e -> l w (h e)")[:, w, :]
            if g == 1:
                return rows.rearrange("(m r) x -> m r x", r=NS)
            if g == 2:
                return rows.rearrange("(m r) x -> m r x", r=16)[:, 0:NS, :]
            return rows

        block = ctx.enter_context(nc.Block())

        @block.sync
        def _(eng):
            for b in range(NB):
                s = b % 2
                if b >= 2:
                    eng.wait_ge(k_used, b - 1)
                eng.dma_start(k1[:, s, :], cache(0, b, 0)).then_inc(k_in[s], 16)
                eng.dma_start(k2[:, s, :, :], cache(1, b, 0)).then_inc(k_in[s], 16)
                eng.dma_start(k3[:, s, :], cache(2, b, 0)).then_inc(k_in[s], 16)
                qrow = [sc["q_smp"][g][NS * b:NS * (b + 1), :] for g in range(NG)]
                eng.dma_start(q1[:, s, :, :], qrow[0].unsqueeze(0).to_broadcast([P, NS, GW])).then_inc(k_in[s], 16)
                eng.dma_start(q2[:, s, :, :], qrow[1].unsqueeze(0).to_broadcast([P, NS, GW])).then_inc(k_in[s], 16)
                eng.dma_start(q3[:, s, :], qrow[2].unsqueeze(0).to_broadcast([P // NS, NS, GW])).then_inc(k_in[s], 16)
            for b in range(NB):
                s = b % 2
                if b >= 2:
                    eng.wait_ge(v_prod, b - 1)
                    eng.wait_ge(v_prod2, b - 1)
                eng.dma_start(v1[:, s, :], cache(0, b, 1)).then_inc(v_in[s], 16)
                eng.dma_start(v2[:, s, :, :], cache(1, b, 1)).then_inc(v_in[s], 16)
                eng.dma_start(v3[:, s, :], cache(2, b, 1)).then_inc(v_in[s], 16)

        @block.gpsimd
        def _(eng):
            eng.memset(new[:, :, :], 0.0).then_inc(new_zero, 1)
            eng.wait_ge(new_zero, 1)
            kv = [a[f"kv{g}s"][0].rearrange("b s w h e -> (b s) (w h e)") for g in range(NG)]
            for d in range(NS):
                eng.dma_start(new[d:SMP, d, :], kv[0][0:SMP - d, :]).then_inc(new_in, 16)
            for g in (1, 2):
                eng.dma_start(new[:, 3 + g, :], kv[g]).then_inc(new_in, 16)
            for g in range(NG):
                eng.dma_start(qn[:, g, :], sc["q_smp"][g]).then_inc(new_in, 16)
            for b in range(NB):
                s = b % 2
                eng.wait_ge(k_in[s], 96 * (b // 2 + 1))
                if b >= 2:
                    eng.wait_ge(k_used, b - 1)
                eng.tensor_tensor(pr2[:, s, :, :], k2[:, s, :, :], q2[:, s, :, :], ALU.mult).then_inc(pk_ready, 1)
            eng.wait_ge(PT_ready, 1)
            for b in range(NB):
                s = b % 2
                eng.wait_ge(v_in[s], 48 * (b // 2 + 1))
                if b >= 2:
                    eng.wait_ge(v_sum, b - 1)
                for t in range(NS):
                    ins = eng.tensor_tensor(pr2[:, s, t, :].rearrange("p (h e) -> p h e", h=HG), v2[:, s, t, :].rearrange("p (h e) -> p h e", h=HG),
                                            PT[:, HG:2 * HG, NS * b + t].unsqueeze(2).to_broadcast([P, HG, HD]), ALU.mult)
                ins.then_inc(v_prod2, 1)

        @block.vector
        def _(eng):
            count = [0]

            def link(ins):
                count[0] += 1
                ins.then_inc(chain, 1)
                eng.wait_ge(chain, count[0])

            def signal(ins, s, n):
                ins.then_inc(s, 1)
                eng.wait_ge(s, n)

            def by_head(x):
                return x.rearrange("p s (h e) -> p s h e", h=HG)

            for b in range(NB):
                s = b % 2
                eng.wait_ge(k_in[s], 96 * (b // 2 + 1))
                link(eng.tensor_tensor(pr1[:, 0, :, :], k1[:, s, :].unsqueeze(1).to_broadcast([P, NS, GW]), q1[:, s, :, :], ALU.mult))
                link(eng.tensor_reduce(S[:, 0, :, NS * b:NS * (b + 1)].rearrange("p h s -> p s h"), by_head(pr1[:, 0, :, :]), AX, ALU.add))
                link(eng.tensor_tensor(pr3[:, 0, :], k3[:, s, :], q3[:, s, :], ALU.mult))
                link(eng.tensor_reduce(S3[:, :, b], pr3[:, 0, :].rearrange("p (h e) -> p h e", h=HG), AX, ALU.add))
                eng.wait_ge(pk_ready, b + 1)
                signal(eng.tensor_reduce(S[:, 1, :, NS * b:NS * (b + 1)].rearrange("p h s -> p s h"), by_head(pr2[:, s, :, :]), AX, ALU.add), k_used, b + 1)
            hb = [S[:, g, :, :].rearrange("p h (b s) -> p (h b) s", s=NS) for g in range(NG)]

            def rowmask(at, rows=HG * NB):
                return cst[:, at:at + NS].unsqueeze(1).to_broadcast([P, rows, NS])

            link(eng.scalar_tensor_tensor(out=hb[0], in0=hb[0], scalar=QK_SCALE, in1=rowmask(C_NEW1), op0=ALU.mult, op1=ALU.add))
            link(eng.tensor_scalar(S[:, 1, :, :], S[:, 1, :, :], QK_SCALE, None, ALU.mult))
            link(eng.tensor_tensor(hb[2], S3[:, :, :].rearrange("p h b -> p (h b)").unsqueeze(2).to_broadcast([P, HG * NB, NS]), rowmask(C_KEEP), ALU.mult))
            signal(eng.scalar_tensor_tensor(out=hb[2], in0=hb[2], scalar=QK_SCALE, in1=rowmask(C_DROP), op0=ALU.mult, op1=ALU.add), S_ready, 1)
            eng.wait_ge(new_in, 16 * 9)
            link(eng.tensor_tensor(pn[:, 0:NS, :], new[:, 0:NS, 0:GW], qn[:, 0:1, :].to_broadcast([SMP, NS, GW]), ALU.mult))
            link(eng.tensor_tensor(pn[:, NS:6, :], new[:, NS:6, 0:GW], qn[:, 1:3, :], ALU.mult))
            link(eng.tensor_reduce(N[:, :, :], by_head(pn[:, :, :]), AX, ALU.add))
            link(eng.tensor_scalar(N[:, NS:6, :], N[:, NS:6, :], QK_SCALE, None, ALU.mult))
            link(eng.scalar_tensor_tensor(out=N[:, 0:NS, :], in0=N[:, 0:NS, :], scalar=QK_SCALE,
                                          in1=cst[0:SMP, C_BACK:C_BACK + NS].unsqueeze(2).to_broadcast([SMP, NS, HG]), op0=ALU.mult, op1=ALU.add))
            eng.wait_ge(r_ready, 1)
            for i in range(6):
                link(eng.tensor_copy(R[:, 4 * i:4 * i + 4, :], rp[i][0:SMP, :].rearrange("p (a k) -> p a k", a=4)))
            link(eng.tensor_reduce(mx[:, :], R[:, :, :], AX, ALU.max))
            link(eng.tensor_reduce(M[:, 0, :], mx[:, :].rearrange("p (g h) -> p h g", g=NG), AX, ALU.max))
            link(eng.tensor_reduce(M[:, 1, :], N[:, :, :].rearrange("p d h -> p h d"), AX, ALU.max))
            link(eng.tensor_tensor(M[:, 2, :], M[:, 0, :], M[:, 1, :], ALU.max))
            for g in range(NG):
                link(eng.tensor_tensor(R[:, HG * g:HG * (g + 1), :], R[:, HG * g:HG * (g + 1), :], M[:, 2, :].unsqueeze(2).to_broadcast([SMP, HG, P]), ALU.subtract))
            signal(eng.tensor_tensor(N[:, :, :], N[:, :, :], M[:, 2:3, :].to_broadcast([SMP, 6, HG]), ALU.subtract), x_ready, 1)
            eng.wait_ge(e_ready, 2)
            link(eng.tensor_reduce(mx[:, :], R[:, :, :], AX, ALU.add))
            link(eng.tensor_reduce(den[:, 0, :], mx[:, :].rearrange("p (g h) -> p h g", g=NG), AX, ALU.add))
            link(eng.tensor_reduce(den[:, 1, :], N[:, :, :].rearrange("p d h -> p h d"), AX, ALU.add))
            link(eng.tensor_tensor(den[:, 0, :], den[:, 0, :], den[:, 1, :], ALU.add))
            link(eng.reciprocal(den[:, 2, :], den[:, 0, :]))
            eng.wait_ge(b_ready, 1)
            link(eng.tensor_copy(PT[:, 0:16, :], rp[0][:, :].rearrange("p (a t) -> p a t", a=16)))
            signal(eng.tensor_copy(PT[:, 16:24, :], rp[1][:, 0:8 * SMP].rearrange("p (a t) -> p a t", a=8)), PT_ready, 1)
            for b in range(NB):
                s = b % 2
                eng.wait_ge(v_in[s], 48 * (b // 2 + 1))
                if b >= 2:
                    eng.wait_ge(v_sum, b - 1)
                link(eng.tensor_reduce(pw[:, s, :], PT[:, 2 * HG:3 * HG, NS * b:NS * (b + 1)], AX, ALU.add))
                for t in range(NS):
                    link(eng.tensor_tensor(pr1[:, s, t, :].rearrange("p (h e) -> p h e", h=HG), v1[:, s, :].rearrange("p (h e) -> p h e", h=HG),
                                           PT[:, 0:HG, NS * b + t].unsqueeze(2).to_broadcast([P, HG, HD]), ALU.mult))
                signal(eng.tensor_tensor(pr3[:, s, :].rearrange("p (h e) -> p h e", h=HG), v3[:, s, :].rearrange("p (h e) -> p h e", h=HG),
                                         pw[:, s, :].unsqueeze(2).to_broadcast([P, HG, HD]), ALU.mult), v_prod, b + 1)
            for d in range(6):
                link(eng.tensor_tensor(pn[:, d, :].rearrange("p (h e) -> p h e", h=HG), new[:, d, GW:2 * GW].rearrange("p (h e) -> p h e", h=HG),
                                       N[:, d, :].unsqueeze(2).to_broadcast([SMP, HG, HD]), ALU.mult))
            for d in range(1, 6):
                link(eng.tensor_tensor(pn[:, 0, :], pn[:, 0, :], pn[:, d, :], ALU.add))
            eng.wait_ge(v_sum, NB)
            link(eng.tensor_tensor(pn[:, 0, :], pn[:, 0, :], acc[0:SMP, :], ALU.add))
            link(eng.tensor_tensor(hs[:, :].rearrange("p (h e) -> p h e", h=HG), pn[:, 0, :].rearrange("p (h e) -> p h e", h=HG),
                                   den[:, 2, :].unsqueeze(2).to_broadcast([SMP, HG, HD]), ALU.mult))

        @block.scalar
        def _(eng):
            eng.wait_ge(x_ready, 1)
            eng.activation(R[:, :, :], R[:, :, :], ACT.Exp).then_inc(e_ready, 1)
            eng.activation(N[:, :, :], N[:, :, :], ACT.Exp).then_inc(e_ready, 1)

        @block.tensor
        def _(eng):
            eng.wait_ge(S_ready, 1)
            for j in range(NG * HG):
                mm = eng.transpose(rp[j // 4][0:SMP, P * (j % 4):P * (j % 4 + 1)], S[:, j // HG, j % HG, :], cst[:, C_ID:C_ID + P])
            mm.then_inc(r_ready, 1)
            eng.wait_ge(e_ready, 2)
            for j in range(NG * HG):
                mm = eng.transpose(rp[j // 16][:, SMP * (j % 16):SMP * (j % 16 + 1)], R[:, j, :], cst[0:SMP, C_ID:C_ID + SMP])
            mm.then_inc(b_ready, 1)
            for b in range(NB):
                s = b % 2
                eng.wait_ge(v_prod, b + 1)
                eng.wait_ge(v_prod2, b + 1)
                for t in range(NS):
                    at = C_SELQ + SMP - 1 - (NS * b + t)
                    for x, pr in enumerate((pr1, pr2)):
                        eng.matmul(acc[0:SMP, :], cst[:, at:at + SMP], pr[:, s, t, :], start=(b == 0 and t == 0 and x == 0), stop=False)
                at = C_SELR + (SMP - NS) - NS * b
                eng.matmul(acc[0:SMP, :], cst[:, at:at + SMP], pr3[:, s, :], start=False, stop=(b == NB - 1)).then_inc(v_sum, 1)


def mix(nc, a, sc, cst, yT, hs):
    HC = 2 * PH
    with ExitStack() as ctx:
        def sb(name, shape, dt=F32, c=ctx):
            return c.enter_context(nc.sbuf_tensor("m_" + name, shape, dt))

        def sem(name):
            return ctx.enter_context(nc.semaphore("m_" + name))

        wcp = sb("wcp", [P, DC, D])
        wap = sb("wap", [P, 4, D])
        wo = sb("wo", [P, DC, D])
        wq = wcp[:, :, :].rearrange("p k c -> p (k c)").rearrange("p (s k c) -> p s k c", s=2, k=DC)
        ag = sb("ag", [P, NG, HG, ACCW])
        cg = sb("cg", [P, 8, HG])
        cw = sb("cw", [P, NG, HG])
        ho = sb("ho", [P, GW])
        tmp = sb("tmp", [P, GW])
        hoT = sb("hoT", [P, 4, TOK])
        stat = sb("stat", [P, 2, TOK])
        sqy = sb("sqy", [P, 2, TOK])
        gt = sb("gt", [P, 2, 2, TOK])
        mT = sb("mT", [P, DC, TOK])
        vec = sb("vec", [P, 3, DC])
        x1 = sb("x1", [P, D])
        h2 = sb("h2", [P, D])
        rms = sb("rms", [P, 4])
        h2T = yT
        sk = sb("sk", [P, HC, HALF])
        skT = sb("skT", [P, HC, KEYS])
        qp = sb("qp", [P, 2, TOK])
        scs = sb("scs", [P, 2, UPT, KEYS])
        bank = [ctx.enter_context(nc.psum_tensor(f"m_b{i}", [P, 512], F32)) for i in range(8)]

        w_in = sem("w_in")
        wo_in = sem("wo_in")
        sk_in = sem("sk_in")
        vec_in = sem("vec_in")
        chain = sem("chain")
        ag_in = sem("ag_in")
        ag_used = sem("ag_used")
        c_max = sem("c_max")
        c_exp = sem("c_exp")
        ho_ready = sem("ho_ready")
        hp_ready = sem("hp_ready")
        hoT_ready = sem("hoT_ready")
        sum_ready = sem("sum_ready")
        d_ready = sem("d_ready")
        sq_ready = sem("sq_ready")
        sq_used = sem("sq_used")
        half_ready = sem("half_ready")
        var_ready = sem("var_ready")
        rstd_ready = sem("rstd_ready")
        yn_ready = sem("yn_ready")
        y_ready = sem("y_ready")
        g_in = [sem("g_in0"), sem("g_in1")]
        pr_ready = sem("pr_ready")
        mix_ready = sem("mix_ready")
        x_in = sem("x_in")
        o_ready = sem("o_ready")
        x1_ready = sem("x1_ready")
        x1_sq = sem("x1_sq")
        x1_rstd = sem("x1_rstd")
        h2_ready = sem("h2_ready")
        x1_out = sem("x1_out")
        ht_ready = sem("ht_ready")
        h2T_ready = sem("h2T_ready")
        kt_ready = sem("kt_ready")
        skT_ready = sem("skT_ready")
        wq_in = [sem("wq_in0"), sem("wq_in1")]
        q_ready = sem("q_ready")
        qs_ready = sem("qs_ready")
        s_ready = sem("s_ready")
        sc_ready = sem("sc_ready")
        sc_out = [sem("sc_out0"), sem("sc_out1")]

        wq_v = a["w_peer_q"][0].rearrange("(k p) c -> p k c", p=P)
        block = ctx.enter_context(nc.Block())

        @block.sync
        def _(eng):
            with nc.allow_non_contiguous_dma("short rows of small inputs"):
                eng.dma_start(vec[:, 0, :], a["conv_ln_g"][0].rearrange("(c p) -> p c", p=P)).then_inc(vec_in, 16)
                eng.dma_start(vec[:, 1, :], a["conv_ln_b"][0].rearrange("(c p) -> p c", p=P)).then_inc(vec_in, 16)
                eng.dma_start(vec[:, 2, :], a["norm2_w"][0].rearrange("(c p) -> p c", p=P)).then_inc(vec_in, 16)
            for i in range(NT):
                if i:
                    eng.wait_ge(ag_used, i)
                for g in range(NG):
                    eng.dma_start(ag[:, g, :, :].rearrange("p h w -> p (h w)"), sc["attn"][g][P * i:P * (i + 1), :]).then_inc(ag_in, 16)
                if i == 0:
                    eng.dma_start(wcp[:, :, :], a["w_conv_proj"][0].rearrange("(k p) c -> p k c", p=P)).then_inc(w_in, 16)
                    eng.dma_start(wap[:, :, :], a["w_attn_proj"][0].rearrange("(k p) c -> p k c", p=P)).then_inc(w_in, 16)
                    eng.dma_start(sk[:, :, :], a["peer_sub_keys"][0].rearrange("h t k c -> k (h t) c")).then_inc(sk_in, 16)
                    eng.dma_start(wo[:, :, :], a["w_out"][0].rearrange("(k p) c -> p k c", p=P)).then_inc(wo_in, 16)
            for c in range(DC):
                if c >= 2:
                    eng.wait_ge(mix_ready, c - 1)
                for w in range(2):
                    eng.dma_start(gt[:, c % 2, w, :], sc["gates"][DC * w + c]).then_inc(g_in[c % 2], 16)
            for i in range(UPT):
                n = tile_rows(i)
                if i:
                    eng.wait_ge(x1_out, 32 * i)
                src = a["x_prompt"][0, P * i:P * (i + 1), :] if i < NT else a["x_sample"].rearrange("b s d -> (b s) d")
                eng.dma_start(x1[0:n, :], src).then_inc(x_in, 16)
                if i == 0:
                    eng.wait_ge(pr_ready, DC)
                    for j in range(2):
                        eng.dma_start(wq[:, j, :, :], wq_v[:, :, 512 * j:512 * (j + 1)]).then_inc(wq_in[j], 16)
            for j in range(2, 4):
                eng.wait_ge(q_ready, 4 * (j - 1))
                eng.dma_start(wq[:, j % 2, :, :], wq_v[:, :, 512 * j:512 * (j + 1)]).then_inc(wq_in[j % 2], 16)

        @block.gpsimd
        def _(eng):
            eng.memset(rms[:, 3:4], -0.5).then_inc(half_ready, 1)
            eng.wait_ge(half_ready, 1)
            eng.wait_ge(var_ready, 1)
            eng.tensor_tensor(stat[:, 1, :], stat[:, 1, :], rms[:, 3:4].to_broadcast([P, TOK]), ALU.pow).then_inc(rstd_ready, 1)
            for i in range(UPT):
                n = tile_rows(i)
                eng.wait_ge(x1_sq, i + 1)
                eng.tensor_scalar(rms[0:n, 1:2], rms[0:n, 0:1], 1.0 / D, RMS_EPS, ALU.mult, ALU.add).then_inc(half_ready, 1)
                eng.wait_ge(half_ready, 2 + i)
                eng.tensor_tensor(rms[0:n, 2:3], rms[0:n, 1:2], rms[0:n, 3:4], ALU.pow).then_inc(x1_rstd, 1)
                eng.wait_ge(x1_rstd, i + 1)
                at = P * i
                eng.dma_start(sc["x1"][at:at + n, :], x1[0:n, :]).then_inc(x1_out, 16)
                eng.wait_ge(h2T_ready, i + 1)
                eng.dma_start(sc["h2"][at:at + n, :], h2[0:n, :]).then_inc(x1_out, 16)
                eng.wait_ge(x1_out, 32 * (i + 1))
            for j in range(HC):
                eng.wait_ge(sc_ready, j + 1)
                for i in range(UPT):
                    n = tile_rows(i)
                    eng.dma_start(sc["scores"][P * i:P * i + n, KEYS * j:KEYS * (j + 1)], scs[0:n, j % 2, i, :]).then_inc(sc_out[j % 2], 16)
            for j in range(2):
                eng.wait_ge(sc_out[j], 16 * UPT * HC // 2)

        @block.tensor
        def _(eng):
            ident = cst[:, C_ID:C_ID + P]
            for i in range(UPT):
                n = tile_rows(i)
                src = ho if i < NT else hs
                if i < NT:
                    eng.wait_ge(ho_ready, i + 1)
                if i:
                    eng.wait_ge(hoT_ready, i)
                for c in range(4):
                    mm = eng.transpose(bank[0][:, P * c:P * c + n], src[0:n, P * c:P * (c + 1)], cst[0:n, C_ID:C_ID + n])
                mm.then_inc(hp_ready, 1)
            eng.wait_ge(sk_in, 16)
            for j in range(4):
                for c in range(4):
                    mm = eng.transpose(bank[4 + j][:, P * c:P * (c + 1)], sk[:, 4 * j + c, :], ident)
            mm.then_inc(kt_ready, 1)
            ones = cst[:, C_ONE:C_ONE + P]
            for k in range(DC):
                eng.matmul(bank[2][:, :], ones, yT[:, k, 0:SEQ], start=(k == 0), stop=(k == DC - 1))
            for k in range(DC):
                mm = eng.matmul(bank[3][:, 0:SMP], ones, yT[:, k, SEQ:TOK], start=(k == 0), stop=(k == DC - 1))
            mm.then_inc(sum_ready, 1)
            eng.wait_ge(d_ready, 1)
            for k in range(DC):
                eng.wait_ge(sq_ready, k + 1)
                eng.matmul(bank[2][:, :], ones, sqy[:, k % 2, 0:SEQ], start=(k == 0), stop=(k == DC - 1))
                eng.matmul(bank[3][:, 0:SMP], ones, sqy[:, k % 2, SEQ:TOK], start=(k == 0), stop=(k == DC - 1)).then_inc(sq_used, 1)
            eng.wait_ge(w_in, 32)
            eng.wait_ge(hoT_ready, UPT)
            eng.wait_ge(skT_ready, 1)
            eng.wait_ge(var_ready, 1)
            for c in range(DC):
                bc, ba, bs = (bank[3 * (c % 2) + 2 + x] for x in range(3))
                if c >= 2:
                    eng.wait_ge(mix_ready, c - 1)
                for k in range(4):
                    w = wap[:, k, P * c:P * (c + 1)]
                    eng.matmul(ba[:, :], w, hoT[:, k, 0:SEQ], start=(k == 0), stop=(k == 3))
                for k in range(4):
                    w = wap[:, k, P * c:P * (c + 1)]
                    eng.matmul(bs[:, SMP:2 * SMP], w, hoT[:, k, SEQ:TOK], start=(k == 0), stop=(k == 3))
                if c == 0:
                    eng.wait_ge(y_ready, DC)
                for k in range(DC):
                    eng.matmul(bc[:, :], wcp[:, k, P * c:P * (c + 1)], yT[:, k, 0:SEQ], start=(k == 0), stop=(k == DC - 1))
                for k in range(DC):
                    mm = eng.matmul(bs[:, 0:SMP], wcp[:, k, P * c:P * (c + 1)], yT[:, k, SEQ:TOK], start=(k == 0), stop=(k == DC - 1))
                mm.then_inc(pr_ready, 1)
            eng.wait_ge(wo_in, 16)
            eng.wait_ge(mix_ready, DC)

            def out_proj(i):
                n = tile_rows(i)
                if i:
                    eng.wait_ge(x1_ready, i)
                for h in range(2):
                    for k in range(DC):
                        mm = eng.matmul(bank[h][0:n, :], mT[:, k, P * i:P * i + n], wo[:, k, 512 * h:512 * (h + 1)], start=(k == 0), stop=(k == DC - 1))
                mm.then_inc(o_ready, 1)

            out_proj(0)
            for i in range(UPT):
                n = tile_rows(i)
                if i + 1 < UPT:
                    out_proj(i + 1)
                eng.wait_ge(h2_ready, i + 1)
                if i:
                    eng.wait_ge(h2T_ready, i)
                for c in range(DC):
                    mm = eng.transpose(bank[2 + c // 4][:, P * (c % 4):P * (c % 4) + n], h2[0:n, P * c:P * (c + 1)], cst[0:n, C_ID:C_ID + n])
                mm.then_inc(ht_ready, 1)
            eng.wait_ge(h2T_ready, UPT)

            def query(j):
                if j % 4 == 0:
                    eng.wait_ge(wq_in[(j // 4) % 2], 16 * (j // 8 + 1))
                if j >= 2:
                    eng.wait_ge(qs_ready, j - 1)
                bm, bs = bank[2 * (j % 2)], bank[2 * (j % 2) + 1]
                for k in range(DC):
                    eng.matmul(bm[:, :], wq[:, (j // 4) % 2, k, P * (j % 4):P * (j % 4 + 1)], h2T[:, k, 0:SEQ], start=(k == 0), stop=(k == DC - 1))
                for k in range(DC):
                    mm = eng.matmul(bs[:, 0:SMP], wq[:, (j // 4) % 2, k, P * (j % 4):P * (j % 4 + 1)], h2T[:, k, SEQ:TOK], start=(k == 0), stop=(k == DC - 1))
                mm.then_inc(q_ready, 1)

            query(0)
            for j in range(HC):
                if j + 1 < HC:
                    query(j + 1)
                eng.wait_ge(qs_ready, j + 1)
                if j >= 2:
                    eng.wait_ge(sc_ready, j - 1)
                for i in range(UPT):
                    n = tile_rows(i)
                    b = bank[4 + 2 * (j % 2) + i // 4]
                    mm = eng.matmul(b[0:n, P * (i % 4):P * (i % 4 + 1)], qp[:, j % 2, P * i:P * i + n], skT[:, j, :], start=True, stop=True)
                mm.then_inc(s_ready, 1)

        @block.scalar
        def _(eng):
            for i in range(NT):
                eng.wait_ge(c_max, i + 1)
                eng.activation(cw[:, :, :], cw[:, :, :], ACT.Exp).then_inc(c_exp, 1)
            for k in range(DC):
                eng.wait_ge(d_ready, k + 1)
                if k >= 2:
                    eng.wait_ge(sq_used, k - 1)
                eng.activation(sqy[:, k % 2, :], yT[:, k, :], ACT.Square).then_inc(sq_ready, 1)
            eng.wait_ge(vec_in, 48)
            for k in range(DC):
                eng.wait_ge(yn_ready, k + 1)
                eng.activation(yT[:, k, :], yT[:, k, :], ACT.Silu, scale=vec[:, 0, k:k + 1], bias=vec[:, 1, k:k + 1]).then_inc(y_ready, 1)
            for i in range(UPT):
                n = tile_rows(i)
                eng.wait_ge(x1_ready, i + 1)
                if i:
                    eng.wait_ge(h2T_ready, i)
                    eng.wait_ge(x1_out, 32 * i)
                eng.activation(h2[0:n, :], x1[0:n, :], ACT.Square, accum_out=rms[0:n, 0:1]).then_inc(x1_sq, 1)
            for j in range(HC):
                eng.wait_ge(q_ready, j + 1)
                if j >= 2:
                    eng.wait_ge(s_ready, j - 1)
                eng.activation(qp[:, j % 2, 0:SEQ], bank[2 * (j % 2)][:, :], ACT.Copy)
                eng.activation(qp[:, j % 2, SEQ:TOK], bank[2 * (j % 2) + 1][:, 0:SMP], ACT.Copy).then_inc(qs_ready, 1)

        @block.vector
        def _(eng):
            count = [0]

            def link(ins):
                count[0] += 1
                ins.then_inc(chain, 1)
                eng.wait_ge(chain, count[0])

            def signal(ins, s, n):
                ins.then_inc(s, 1)
                eng.wait_ge(s, n)

            for i in range(NT):
                eng.wait_ge(ag_in, 48 * (i + 1))
                mxs = [ag[:, g, :, HD] for g in range(NG)]
                dns = [ag[:, g, :, HD + 1] for g in range(NG)]
                link(eng.tensor_tensor(cg[:, 0, :], mxs[0], mxs[1], ALU.max))
                link(eng.tensor_tensor(cg[:, 0, :], cg[:, 0, :], mxs[2], ALU.max))
                for g in range(NG):
                    ins = eng.tensor_tensor(cw[:, g, :], mxs[g], cg[:, 0, :], ALU.subtract)
                    if g == NG - 1:
                        signal(ins, c_max, i + 1)
                    else:
                        link(ins)
                eng.wait_ge(c_exp, i + 1)
                for g in range(NG):
                    link(eng.tensor_tensor(cg[:, 1 + g, :], cw[:, g, :], dns[g], ALU.mult))
                link(eng.tensor_tensor(cg[:, 1, :], cg[:, 1, :], cg[:, 2, :], ALU.add))
                link(eng.tensor_tensor(cg[:, 1, :], cg[:, 1, :], cg[:, 3, :], ALU.add))
                link(eng.reciprocal(cg[:, 4, :], cg[:, 1, :]))
                if i:
                    eng.wait_ge(hp_ready, i)
                hv = ho[:, :].rearrange("p (j w e) -> p w j e", w=2, e=HD)
                tv = tmp[:, :].rearrange("p (j w e) -> p w j e", w=2, e=HD)
                for g in range(NG):
                    link(eng.tensor_tensor(cg[:, 5 + g, :], cw[:, g, :], cg[:, 4, :], ALU.mult))
                    for w in range(2):
                        link(eng.tensor_tensor((tv if g else hv)[:, w, :, :], ag[:, g, 4 * w:4 * w + 4, 0:HD],
                                               cg[:, 5 + g, 4 * w:4 * w + 4].unsqueeze(2).to_broadcast([P, 4, HD]), ALU.mult))
                    if g:
                        ins = eng.tensor_tensor(ho[:, :], ho[:, :], tmp[:, :], ALU.add)
                        if g == NG - 1:
                            signal(ins, ho_ready, i + 1)
                            eng.sem_inc(ag_used, 1)
                        else:
                            link(ins)
                eng.wait_ge(hp_ready, i + 1)
                signal(eng.tensor_copy(hoT[:, :, P * i:P * (i + 1)], bank[0][:, :].rearrange("p (c t) -> p c t", c=4)), hoT_ready, i + 1)
            eng.wait_ge(hp_ready, UPT)
            signal(eng.tensor_copy(hoT[:, :, SEQ:TOK], bank[0][:, :].rearrange("p (c t) -> p c t", c=4)[:, :, 0:SMP]), hoT_ready, UPT)
            eng.wait_ge(kt_ready, 1)
            for j in range(4):
                ins = eng.tensor_copy(skT[:, 4 * j:4 * j + 4, :], bank[4 + j][:, :].rearrange("p (c t) -> p c t", c=4))
                if j == 3:
                    signal(ins, skT_ready, 1)
                else:
                    link(ins)
            eng.wait_ge(sum_ready, 1)
            link(eng.tensor_scalar(stat[:, 0, 0:SEQ], bank[2][:, :], 1.0 / D, None, ALU.mult))
            link(eng.tensor_scalar(stat[:, 0, SEQ:TOK], bank[3][:, 0:SMP], 1.0 / D, None, ALU.mult))
            for k in range(DC):
                eng.tensor_tensor(yT[:, k, :], yT[:, k, :], stat[:, 0, :], ALU.subtract).then_inc(d_ready, 1)
            eng.wait_ge(d_ready, DC)
            eng.wait_ge(sq_used, DC)
            link(eng.tensor_scalar(stat[:, 1, 0:SEQ], bank[2][:, :], 1.0 / D, LN_EPS, ALU.mult, ALU.add))
            signal(eng.tensor_scalar(stat[:, 1, SEQ:TOK], bank[3][:, 0:SMP], 1.0 / D, LN_EPS, ALU.mult, ALU.add), var_ready, 1)
            eng.wait_ge(rstd_ready, 1)
            for k in range(DC):
                eng.tensor_tensor(yT[:, k, :], yT[:, k, :], stat[:, 1, :], ALU.mult).then_inc(yn_ready, 1)
            for c in range(DC):
                bc, ba, bs = (bank[3 * (c % 2) + 2 + x] for x in range(3))
                eng.wait_ge(pr_ready, c + 1)
                eng.wait_ge(g_in[c % 2], 32 * (c // 2 + 1))
                link(eng.tensor_tensor(gt[:, c % 2, 0, 0:SEQ], gt[:, c % 2, 0, 0:SEQ], bc[:, :], ALU.mult))
                link(eng.tensor_tensor(gt[:, c % 2, 0, SEQ:TOK], gt[:, c % 2, 0, SEQ:TOK], bs[:, 0:SMP], ALU.mult))
                link(eng.tensor_tensor(gt[:, c % 2, 1, 0:SEQ], gt[:, c % 2, 1, 0:SEQ], ba[:, :], ALU.mult))
                link(eng.tensor_tensor(gt[:, c % 2, 1, SEQ:TOK], gt[:, c % 2, 1, SEQ:TOK], bs[:, SMP:2 * SMP], ALU.mult))
                signal(eng.tensor_tensor(mT[:, c, :], gt[:, c % 2, 0, :], gt[:, c % 2, 1, :], ALU.add), mix_ready, c + 1)
            for i in range(UPT):
                n = tile_rows(i)
                eng.wait_ge(o_ready, i + 1)
                eng.wait_ge(x_in, 16 * (i + 1))
                for h in range(2):
                    ins = eng.tensor_tensor(x1[0:n, 512 * h:512 * (h + 1)], x1[0:n, 512 * h:512 * (h + 1)], bank[h][0:n, :], ALU.add)
                    if h:
                        signal(ins, x1_ready, i + 1)
                    else:
                        link(ins)
                eng.wait_ge(x1_rstd, i + 1)
                signal(eng.tensor_scalar(h2[0:n, :], x1[0:n, :], rms[0:n, 2:3], None, ALU.mult), h2_ready, i + 1)
                eng.wait_ge(ht_ready, i + 1)
                for b in range(2):
                    ins = eng.tensor_tensor(h2T[:, 4 * b:4 * b + 4, P * i:P * i + n], bank[2 + b][:, :].rearrange("p (c t) -> p c t", c=4)[:, :, 0:n],
                                            vec[:, 2, 4 * b:4 * b + 4].unsqueeze(2).to_broadcast([P, 4, n]), ALU.mult)
                    if b:
                        signal(ins, h2T_ready, i + 1)
                    else:
                        link(ins)
            for j in range(HC):
                eng.wait_ge(s_ready, j + 1)
                if j >= 2:
                    eng.wait_ge(sc_out[j % 2], 16 * UPT * (j // 2))
                link(eng.tensor_copy(scs[:, j % 2, 0:NT, :], bank[4 + 2 * (j % 2)][:, :].rearrange("p (i k) -> p i k", i=NT)))
                signal(eng.tensor_copy(scs[0:SMP, j % 2, NT, :], bank[5 + 2 * (j % 2)][0:SMP, 0:KEYS]), sc_ready, j + 1)


def peer(nc, a, sc, cst):
    SLOTS = PH * TOPK
    STEPS = NT * SLOTS + SLOTS // 4
    RING, LAG = 8, 2
    LOW = -3.0e38
    with ExitStack() as ctx:
        def sb(name, shape, dt=F32):
            return ctx.enter_context(nc.sbuf_tensor("p_" + name, shape, dt))

        def sem(name):
            return ctx.enter_context(nc.semaphore("p_" + name))

        ring = sb("ring", [P, RING, 2 * D])
        y = sb("y", [P, 2, D])
        h2 = sb("h2", [P, 2, D])
        w2 = sb("w2", [P, D])
        sco = sb("sco", [P, 2, 2 * PH * KEYS])
        idx = sb("idx", [P, 2, SLOTS], U32)
        gw = sb("gw", [P, 2, SLOTS])
        dots = sb("dots", [P, 4])
        gel = sb("gel", [P, 4])
        wgt = sb("wgt", [P, 4])
        tv = sb("tv", [P, 2, TOPK])
        ti = sb("ti", [P, 2, TOPK], U32)
        tif = sb("tif", [P, 2, TOPK])
        cand = sb("cand", [P, TOPK, TOPK])
        cv = sb("cv", [P, TOPK])
        ci = sb("ci", [P, TOPK], U32)
        ca = sb("ca", [P, 2, TOPK], U32)
        caf = sb("caf", [P, 2, TOPK])
        eq = sb("eq", [P, TOPK, TOPK])
        e12 = sb("e12", [P, 2, TOPK])
        nmx = sb("nmx", [P, 1])
        ex = sb("ex", [P, TOPK])
        exs = sb("exs", [P, 2])
        idx4 = sb("idx4", [P, SLOTS // 4], U32)
        gw4 = sb("gw4", [P, SLOTS // 4])
        out4 = sb("out4", [SMP, D])
        fold = [ctx.enter_context(nc.psum_tensor(f"p_f{i}", [P, 512], F32)) for i in range(2)]

        w2_in = sem("w2_in")
        sc_in = [sem("sc_in0"), sem("sc_in1")]
        y_in = [sem("y_in0"), sem("y_in1")]
        y4_zero = sem("y4_zero")
        top_ready = sem("top_ready")
        ex_ready = sem("ex_ready")
        idx_ready = sem("idx_ready")
        quad_in = sem("quad_in")
        h2_ready = sem("h2_ready")
        chain = sem("chain")
        row_in = [sem(f"row_in{i}") for i in range(RING)]
        dot_ready = sem("dot_ready")
        gel_ready = sem("gel_ready")
        wgt_ready = sem("wgt_ready")
        v_used = sem("v_used")
        y_out = [sem("y_out0"), sem("y_out1")]
        fold_ready = sem("fold_ready")
        f_ready = sem("f_ready")

        def step_tile(t):
            return min(t // SLOTS, NT)

        def step_no(t):
            return step_tile(t), t - SLOTS * step_tile(t)

        def end_of(tile):
            return SLOTS * (tile + 1) if tile < NT else STEPS

        block = ctx.enter_context(nc.Block())

        @block.sync
        def _(eng):
            for i in range(UPT):
                n, s, at = tile_rows(i), i % 2, P * i
                if i >= 2:
                    eng.wait_ge(idx_ready, PH * (i - 1))
                eng.dma_start(sco[0:n, s, :], sc["scores"][at:at + n, :]).then_inc(sc_in[s], 16)
                if i == 0:
                    eng.dma_start(w2[:, :], a["norm2_w"].to_broadcast([P, D])).then_inc(w2_in, 16)
                if i >= 2:
                    eng.wait_ge(v_used, end_of(i - 2))
                    eng.dma_start(a["y_p"][0, P * (i - 2):P * (i - 1), :], y[:, s, :]).then_inc(y_out[s], 16)
                    eng.wait_ge(y_out[s], 16 * (i // 2))
                if i < NT:
                    eng.dma_start(y[:, s, :], sc["x1"][at:at + n, :]).then_inc(y_in[s], 16)
                    eng.dma_start(h2[:, s, :], sc["h2"][at:at + n, :]).then_inc(y_in[s], 16)
                else:
                    eng.wait_ge(y4_zero, 1)
                    eng.dma_start(y[0:n, s, :], sc["x1"][at:at + n, :]).then_inc(y_in[s], 16)
                    for r in range(4):
                        eng.dma_start(h2[n * r:n * (r + 1), s, :], sc["h2"][at:at + n, :]).then_inc(y_in[s], 16)
            eng.wait_ge(idx_ready, PH * UPT)
            for r in range(4):
                for dst, src in ((idx4, idx), (gw4, gw)):
                    eng.dma_start(dst[SMP * r:SMP * (r + 1), :], src[0:SMP, NT % 2, 32 * r:32 * (r + 1)]).then_inc(quad_in, 16)
            eng.wait_ge(v_used, end_of(NT - 1))
            eng.dma_start(a["y_p"][0, P * (NT - 1):P * NT, :], y[:, (NT - 1) % 2, :]).then_inc(y_out[1], 16)
            eng.wait_ge(f_ready, 2)
            eng.dma_start(a["y_s"].rearrange("b s d -> (b s) d"), out4[:, :]).then_inc(y_out[0], 16)
            eng.wait_ge(y_out[0], 48)
            eng.wait_ge(y_out[1], 32)

        @block.gpsimd
        def _(eng):
            for t in range(STEPS):
                tile, k = step_no(t)
                if tile < NT and k % TOPK == 0:
                    eng.wait_ge(idx_ready, PH * tile + k // TOPK + 1)
                if tile == NT and k == 0:
                    eng.wait_ge(quad_in, 128)
                if t == end_of(NT - 2) + LAG:
                    eng.wait_ge(y_out[0], 32)
                    eng.memset(y[:, 0, :], 0.0).then_inc(y4_zero, 1)
                if t >= RING:
                    eng.wait_ge(v_used, t - RING + 1)
                col = idx[:, tile % 2, k:k + 1] if tile < NT else idx4[:, k:k + 1]
                eng.indirect_dma_start(ring[:, t % RING, :], None, a["expert_uv"], bass.IndirectOffsetOnAxis(col, 0)).then_inc(row_in[t % RING], 16)

        @block.scalar
        def _(eng):
            def head_exp(i, h):
                n = tile_rows(i)
                eng.wait_ge(top_ready, PH * i + h + 1)
                eng.activation(ex[0:n, :], cv[0:n, :], ACT.Exp, bias=nmx[0:n, :], accum_out=exs[0:n, 0:1]).then_inc(ex_ready, 1)

            for h in range(PH):
                head_exp(0, h)
            for t in range(STEPS):
                tile, k = step_no(t)
                if k == 0 and tile == NT:
                    eng.wait_ge(quad_in, 128)
                w = gw[:, tile % 2, k:k + 1] if tile < NT else gw4[:, k:k + 1]
                eng.wait_ge(dot_ready, t + 1)
                if t >= 4:
                    eng.wait_ge(v_used, t - 3)
                eng.activation(gel[:, t % 4:t % 4 + 1], dots[:, t % 4:t % 4 + 1], ACT.Gelu).then_inc(gel_ready, 1)
                eng.wait_ge(gel_ready, t + 1)
                eng.activation(wgt[:, t % 4:t % 4 + 1], gel[:, t % 4:t % 4 + 1], ACT.Copy, scale=w).then_inc(wgt_ready, 1)
                if tile < NT and k % TOPK == TOPK - 1:
                    head_exp(tile + 1, k // TOPK)

        @block.vector
        def _(eng):
            count = [0]

            def link(ins):
                count[0] += 1
                ins.then_inc(chain, 1)
                eng.wait_ge(chain, count[0])

            def signal(ins, s, n):
                ins.then_inc(s, 1)
                eng.wait_ge(s, n)

            def top16(values, index, x):
                link(eng.max(values[:, 0:8], x))
                link(eng.max_index(index[:, 0:8], values[:, 0:8], x))
                link(eng.match_replace(x, values[:, 0:8], x, LOW))
                link(eng.max(values[:, 8:16], x))
                link(eng.max_index(index[:, 8:16], values[:, 8:16], x))

            def retrieve(i, h):
                n, s = tile_rows(i), i % 2
                if h == 0:
                    eng.wait_ge(sc_in[s], 16 * (i // 2 + 1))
                for p in range(2):
                    at = (2 * h + p) * KEYS
                    top16(tv[0:n, p, :], ti[0:n, p, :], sco[0:n, s, at:at + KEYS])
                link(eng.tensor_copy(tif[0:n, :, :], ti[0:n, :, :]))
                link(eng.tensor_tensor(cand[0:n, :, :], tv[0:n, 0, :].unsqueeze(2).to_broadcast([n, TOPK, TOPK]),
                                       tv[0:n, 1, :].unsqueeze(1).to_broadcast([n, TOPK, TOPK]), ALU.add))
                flat = cand[0:n, :, :].rearrange("p a b -> p (a b)")
                top16(cv[0:n, :], ci[0:n, :], flat)
                signal(eng.tensor_scalar(nmx[0:n, :], cv[0:n, 0:1], -1.0, None, ALU.mult), top_ready, PH * i + h + 1)
                link(eng.tensor_scalar(ca[0:n, 0, :], ci[0:n, :], 4, None, ALU.logical_shift_right))
                link(eng.tensor_scalar(ca[0:n, 1, :], ci[0:n, :], TOPK - 1, None, ALU.bitwise_and))
                link(eng.tensor_copy(caf[0:n, :, :], ca[0:n, :, :]))
                for p in range(2):
                    link(eng.tensor_tensor(eq[0:n, :, :], caf[0:n, p, :].unsqueeze(2).to_broadcast([n, TOPK, TOPK]),
                                           cst[0:n, C_IOTA:C_IOTA + TOPK].unsqueeze(1).to_broadcast([n, TOPK, TOPK]), ALU.is_equal))
                    link(eng.tensor_tensor(eq[0:n, :, :], eq[0:n, :, :], tif[0:n, p, :].unsqueeze(1).to_broadcast([n, TOPK, TOPK]), ALU.mult))
                    link(eng.tensor_reduce(e12[0:n, p, :], eq[0:n, :, :], AX, ALU.add))
                link(eng.scalar_tensor_tensor(out=e12[0:n, 0, :], in0=e12[0:n, 0, :], scalar=float(KEYS), in1=e12[0:n, 1, :], op0=ALU.mult, op1=ALU.add))
                link(eng.tensor_copy(idx[0:n, s, TOPK * h:TOPK * (h + 1)], e12[0:n, 0, :]))
                eng.wait_ge(ex_ready, PH * i + h + 1)
                link(eng.reciprocal(exs[0:n, 1:2], exs[0:n, 0:1]))
                signal(eng.tensor_scalar(gw[0:n, s, TOPK * h:TOPK * (h + 1)], ex[0:n, :], exs[0:n, 1:2], None, ALU.mult), idx_ready, PH * i + h + 1)

            def weigh(i):
                s = i % 2
                eng.wait_ge(y_in[s], 32 * (i // 2 + 1) if i < NT else 32 * 2 + 80)
                signal(eng.tensor_tensor(h2[:, s, :], h2[:, s, :], w2[:, :], ALU.mult), h2_ready, i + 1)

            def add_v(t):
                s = step_tile(t) % 2
                eng.wait_ge(wgt_ready, t + 1)
                if t:
                    eng.wait_ge(v_used, t)
                eng.scalar_tensor_tensor(out=y[:, s, :], in0=ring[:, t % RING, D:2 * D], scalar=wgt[:, t % 4:t % 4 + 1], in1=y[:, s, :],
                                         op0=ALU.mult, op1=ALU.add).then_inc(v_used, 1)

            for h in range(PH):
                retrieve(0, h)
            eng.wait_ge(w2_in, 16)
            for t in range(STEPS):
                tile, k = step_no(t)
                if k == 0:
                    weigh(tile)
                eng.wait_ge(row_in[t % RING], 16 * (t // RING + 1))
                u = ring[:, t % RING, 0:D]
                eng.tensor_tensor_reduce(u, u, h2[:, tile % 2, :], 1.0, 0.0, ALU.mult, ALU.add, dots[:, t % 4:t % 4 + 1]).then_inc(dot_ready, 1)
                if t >= LAG:
                    add_v(t - LAG)
                if tile < NT and k % TOPK == TOPK - 1:
                    retrieve(tile + 1, k // TOPK)
            for t in range(STEPS - LAG, STEPS):
                add_v(t)
            for h in range(2):
                eng.wait_ge(fold_ready, 1)
                signal(eng.tensor_copy(out4[:, 512 * h:512 * (h + 1)], fold[h][0:SMP, :]), f_ready, h + 1)

        @block.tensor
        def _(eng):
            eng.wait_ge(v_used, STEPS)
            for h in range(2):
                mm = eng.matmul(fold[h][0:SMP, :], cst[:, C_FOLD:C_FOLD + SMP], y[:, NT % 2, 512 * h:512 * (h + 1)], start=True, stop=True)
            mm.then_inc(fold_ready, 1)


_IN = ["x_prompt", "x_sample", "cache_kv_g1", "cache_kv_g2", "cache_kv_g3", "state_conv", "norm1_w", "w_in", "q_norm_w", "k_norm_w",
       "conv_w", "conv_b", "conv_ln_g", "conv_ln_b", "w_conv_proj", "w_attn_proj", "w_out", "norm2_w", "w_peer_q", "peer_sub_keys"]
_OUT = [("y_p", (1, SEQ, D)), ("y_s", (NB, NS, D)),
        ("kv0p", (1, 1, 128, 2, HG, HD)), ("kv1p", (1, 1, SEQ, 2, HG, HD)), ("kv2p", (1, 1, SEQ, 2, HG, HD)), ("conv_p", (1, 1, PAD, D)),
        ("kv0s", (1, NB, NS, 2, HG, HD)), ("kv1s", (1, NB, NS, 2, HG, HD)), ("kv2s", (1, NB, NS, 2, HG, HD)), ("conv_s", (1, NB, PAD, D))]


def program(nc, a):
    def scratch(name, shape):
        return nc.dram_tensor("x_" + name, shape, F32, kind="Internal").ap()

    sc = {"attn": [scratch(f"attn{g}", [SEQ, HG * ACCW]) for g in range(NG)],
          "q_smp": [scratch(f"q{g}", [SMP, GW]) for g in range(NG)],
          "gates": scratch("gates", [2 * DC, P, TOK]),
          "x1": scratch("x1", [TOK, D]), "h2": scratch("h2", [TOK, D]), "scores": scratch("scores", [TOK, 2 * PH * KEYS])}
    with ExitStack() as ctx:
        cst = ctx.enter_context(nc.sbuf_tensor("cst", [P, C_W], F32))
        with ExitStack() as inner:
            yT = inner.enter_context(nc.sbuf_tensor("yT", [P, DC, TOK], F32))
            hs = inner.enter_context(nc.sbuf_tensor("hs", [SMP, GW], F32))
            front(nc, a, sc, cst, yT, a["trig"])
            sample_attention(nc, a, sc, cst, hs)
            mix(nc, a, sc, cst, yT, hs)
        peer(nc, a, sc, cst)


def kernel(**inputs):
    import concourse.bacc as _bacc
    from concourse.bass_utils import run_bass_kernel_spmd as _run

    nc = _bacc.Bacc("TRN2", target_bir_lowering=False, num_devices=1)
    arrays = {name: np.ascontiguousarray(inputs[name]) for name in _IN}
    arrays["expert_uv"] = np.concatenate([inputs["expert_u"][0], inputs["expert_v"][0]], axis=1)
    arrays["consts"], arrays["trig"] = shape_constants()
    a = {name: nc.dram_tensor("in_" + name, x.shape, mybir.dt.from_np(x.dtype), kind="ExternalInput").ap() for name, x in arrays.items()}
    a |= {name: nc.dram_tensor("out_" + name, shape, F32, kind="ExternalOutput").ap() for name, shape in _OUT}
    program(nc, a)
    r = _run(nc, [{"in_" + name: x for name, x in arrays.items()}], core_ids=[0])
    return tuple(r.results[0]["out_" + name] for name, _ in _OUT)
```

```python
from contextlib import ExitStack

import numpy as np

import concourse.bass as bass
from concourse import mybir

F32 = mybir.dt.float32
U32 = mybir.dt.uint32
ALU = mybir.AluOpType
ACT = mybir.ActivationFunctionType
AX = mybir.AxisListType.X

P = 128
D = 1024
DC = D // P
SEQ = 512
NT = SEQ // P
NB, NS = 8, 4
SMP = NB * NS
TOK = SEQ + SMP
PAST = 512
HD, HG, NG = 64, 8, 3
GW = HG * HD
AW = NG * GW
TAPS = 31
PAD = TAPS - 1
KEYS, TOPK, PH, HALF = 128, 16, 8, 128
WINDOW_ROWS = (128, 512, 512)
RMS_EPS, LN_EPS = 1e-6, 1e-5
NEG = -1.0e30
QK_SCALE = HD ** -0.5
UPT = NT + 1
ACCW = HD + 2

C_ID, C_ONE, C_PREV, C_DIAG, C_STRIDE = 0, 128, 256, 384, 512
C_SELQ = 640
C_SELR = C_SELQ + 2 * SMP - 1
C_NEW1 = C_SELR + 2 * SMP - NS
C_KEEP = C_NEW1 + NS
C_DROP = C_KEEP + NS
C_BACK = C_DROP + NS
C_IOTA = C_BACK + NS
C_FOLD = C_IOTA + TOPK
C_W = C_FOLD + SMP


def shape_constants():
    c = np.zeros((P, C_W), np.float32)
    p, j = np.arange(P)[:, None], np.arange(P)[None, :]
    c[:, C_ID:C_ID + P] = p == j
    c[:, C_ONE:C_ONE + P] = 1.0
    c[:, C_PREV:C_PREV + P] = np.where(j >= p, 0.0, NEG)
    c[:, C_DIAG:C_DIAG + P] = np.where(j <= p, 0.0, NEG)
    c[:, C_STRIDE:C_STRIDE + P] = np.where((j <= p) & ((p - j) % 4 == 0), 0.0, NEG)
    c[:, C_SELQ + SMP - 1] = 1.0
    r = np.arange(P)
    c[r, C_SELR + (SMP - NS) + r % NS] = 1.0
    s = np.arange(NS)[None, :]
    c[:, C_NEW1:C_NEW1 + NS] = np.where(p < s, NEG, 0.0)
    c[:, C_KEEP:C_KEEP + NS] = p % NS == s
    c[:, C_DROP:C_DROP + NS] = np.where(p % NS == s, 0.0, NEG)
    c[:, C_BACK:C_BACK + NS] = np.where(p % NS < s, NEG, 0.0)
    c[:, C_IOTA:C_IOTA + TOPK] = np.arange(TOPK)[None, :]
    c[:, C_FOLD:C_FOLD + SMP] = p % SMP == np.arange(SMP)[None, :]
    half = HD // 2
    freq = (10000.0 ** (-np.arange(half, dtype=np.float64) / half)).astype(np.float32)
    m = np.arange(P)
    pos = [P * i + m for i in range(NT)] + [NT * m + i for i in range(NT)] + [PAST + m % NS]
    ang = (np.stack(pos).astype(np.float32)[:, :, None] * freq).astype(np.float64)
    trig = np.concatenate([np.cos(ang), -np.sin(ang), np.sin(ang)], axis=2).astype(np.float32)
    return c, np.ascontiguousarray(trig.transpose(1, 0, 2))


def tile_rows(i):
    return P if i < NT else SMP


def order_view(rows, g, i):
    return rows[P * i:P * (i + 1)] if g == 0 else rows.rearrange("(m r) x -> r m x", r=NT)[i]


def front(nc, a, sc, cst, yT, trig_d):
    GLU = 4 * UPT
    QKV = NG * 3 * UPT
    Q0, G0 = GLU, GLU + QKV
    UNITS = QKV + 2 * GLU
    SMALL = 7
    VEC = TAPS + 2
    NW = UNITS // UPT
    with ExitStack() as ctx:
        def sb(name, shape, dt=F32):
            return ctx.enter_context(nc.sbuf_tensor("f_" + name, shape, dt))

        def ps(name, shape):
            return ctx.enter_context(nc.psum_tensor("f_" + name, shape, F32))

        def sem(name):
            return ctx.enter_context(nc.semaphore("f_" + name))

        hT = sb("hT", [P, DC, TOK])
        wsb = sb("w", [P, 2, DC, 512])
        trig = sb("trig", [P, 9, 96])
        qkw = sb("qkw", [P, 2, HD])
        rc = sb("rc", [P, 2, 9, HD])
        rs = sb("rs", [P, 2, 9, HD])
        xss = sb("xss", [P, 4])
        half_m = sb("half_m", [P, HG])
        sq = sb("sq", [P, 512])
        ss = sb("ss", [P, 2, HG])
        qn = sb("qn", [P, 512])
        t1 = sb("t1", [P, 512])
        t2 = sb("t2", [P, 512])
        qkr = sb("qkr", [P, 3, 512])
        qT = sb("qT", [P, 2, 4, SEQ])
        kT = sb("kT", [P, 2, 4, SEQ])
        vsb = sb("v", [P, 2, UPT, GW])
        s_sb = sb("s", [P, 4, 512])
        pt = sb("pt", [P, 4, 512])
        nm = sb("nm", [P, 4, 4])
        st = sb("st", [P, 4, 4, ACCW])
        uT = sb("uT", [P, DC, PAD + SEQ])
        uS = sb("uS", [P, DC, NB, PAD + NS])
        sg = sb("sg", [P, 2, 512])
        gst = sb("gst", [P, 2, 512])
        vec = sb("vec", [P, DC, VEC])
        cw, cb, n1 = vec[:, :, 0:TAPS], vec[:, :, TAPS], vec[:, :, TAPS + 1]
        rows33 = gst[0:VEC, :, :].rearrange("p a b -> p (a b)")
        cin = qkr[:, 0:2, :].rearrange("p a b -> p (a b)")

        xt = qT[:, 1, :, :].rearrange("p (a b) c -> p a (b c)", a=2)
        ht = pt[:, 0:2, :].rearrange("p a b -> p (a b)")
        squares = s_sb[:, 0:2, :].rearrange("p a b -> p (a b)")

        zp = [ps("z0", [P, 512]), ps("z1", [P, 512])]
        ap_ = [ps("a0", [P, 512]), ps("a1", [P, 512])]
        tp = ps("t", [P, 512])
        pp = ps("p", [P, 2, 512])
        op = ps("o", [P, 512])
        ident = cst[:, C_ID:C_ID + P]

        small_in = sem("small_in")
        x_in = [sem("x_in0"), sem("x_in1")]
        sq_done = sem("sq_done")
        x_var = sem("x_var")
        h_ready = sem("h_ready")
        hp_ready = sem("hp_ready")
        hT_ready = sem("hT_ready")
        half_ready = sem("half_ready")
        chain = sem("chain")
        w_in = [sem("w_in0"), sem("w_in1")]
        z_ready = sem("z_ready")
        z_free_v = sem("z_free_v")
        z_free_a = sem("z_free_a")
        z_sq = sem("z_sq")
        z_ss = sem("z_ss")
        z_rstd = sem("z_rstd")
        r_ready = sem("r_ready")
        r_out = [sem(f"r_out{i}") for i in range(3)]
        tr_ready = sem("tr_ready")
        tr_out = sem("tr_out")
        v_ready = sem("v_ready")
        v_out = [sem("v_out0"), sem("v_out1")]
        s_ready = sem("s_ready")
        m_ready = sem("m_ready")
        e_ready = sem("e_ready")
        p_ready = sem("p_ready")
        pt_ready = sem("pt_ready")
        o_ready = sem("o_ready")
        st_ready = sem("st_ready")
        st_out = [sem(f"st_out{i}") for i in range(4)]
        sg_ready = sem("sg_ready")
        u_ready = sem("u_ready")
        g_ready = sem("g_ready")
        g_out = [sem("g_out0"), sem("g_out1")]
        cin_in = sem("cin_in")
        cp_ready = sem("cp_ready")
        cs_ready = sem("cs_ready")
        u_zero = sem("u_zero")
        conv_done = sem("conv_done")
        so_ready = sem("so_ready")
        sc_ready = sem("sc_ready")
        so_out = [sem("so_out0"), sem("so_out1")]

        st4 = hT[:, :, 0:NB * PAD].rearrange("p c (b r) -> p c b r", b=NB)
        w_v = a["w_in"][0].rearrange("(k p) c -> p k c", p=P)

        def w_cols(m):
            if m < 4:
                base = 3 * AW + 256 * m
                return [(base + D, 256, 0), (base, 256, 256)]
            if m < 13:
                g, c = divmod(m - 4, 3)
                return [(c * AW + g * GW, 512, 0)]
            return [(3 * AW + 2 * D + 512 * (m - 13), 512, 0)]

        def w_count(m):
            return 16 * sum(len(w_cols(j)) for j in range(m % 2, m + 1, 2))

        def unit(n):
            m, i = divmod(n, UPT)
            return m, (m - 4) // 3, (m - 4) % 3, i

        def freed_by_scalar(n):
            if n < Q0:
                return n % UPT in (0, 1)
            return n >= G0

        def wait_bank(eng, n):
            if n >= 2:
                k = sum(freed_by_scalar(j) == freed_by_scalar(n - 2) for j in range(n - 1))
                eng.wait_ge(z_free_a if freed_by_scalar(n - 2) else z_free_v, k)

        qk_units = [n for n in range(Q0, G0) if unit(n)[2] < 2]
        tr_units = [n for n in qk_units if unit(n)[3] < NT]

        def stored(n):
            m, g, c, i = unit(n)
            return i == NT or (c == 1 and (g > 0 or i == NT - 1))

        def r_out_count(e):
            return 16 * sum(stored(qk_units[j]) for j in range(e % 3, e + 1, 3))

        def sub_batches(g, s):
            i, par = divmod(s, 2)
            heads = [par + 2 * j for j in range(4)]
            keys = [i - 1, i] if g == 0 and i else [i]
            return [(heads[:2], keys), (heads[2:], keys)] if g == 0 else [(heads, keys)]

        subs = [(g, s, b) for g in range(NG) for s in range(8) for b in range(len(sub_batches(g, s)))]
        sub_no = {k: q for q, k in enumerate(subs)}

        def attention_steps(n):
            g = (n - Q0) // 15 - 1
            if g < 0 or g >= NG:
                return None
            s = n - Q0 - 15 * (g + 1)
            return g, (s if s < 8 else None), (s - 1 if 1 <= s < 9 else None), (s - 2 if 2 <= s < 10 else None)

        CONV = 2 * DC * TAPS
        CONV_AT = [0 if n < 2 * UPT else min(CONV // 2, CONV * (n - 2 * UPT) // 70) if n < Q0 else CONV * (n - 2 * UPT) // 70
                   for n in range(UNITS)]
        CONV_AT = [min(x, CONV) for x in CONV_AT]

        block = ctx.enter_context(nc.Block())

        @block.sync
        def _(eng):
            eng.dma_start(xt[:, 0, :], a["x_prompt"][0, 0:P, :]).then_inc(x_in[0], 16)
            eng.dma_start(cst[:, :], a["consts"]).then_inc(small_in, 16)
            eng.dma_start(rows33[0:TAPS, :], a["conv_w"][0]).then_inc(small_in, 16)
            eng.dma_start(rows33[TAPS:TAPS + 1, :], a["conv_b"]).then_inc(small_in, 16)
            eng.dma_start(rows33[TAPS + 1:TAPS + 2, :], a["norm1_w"]).then_inc(small_in, 16)
            eng.dma_start(trig[:, :, :], trig_d).then_inc(small_in, 16)
            eng.dma_start(qkw[:, 0, :], a["q_norm_w"].to_broadcast([P, HD])).then_inc(small_in, 16)
            eng.dma_start(qkw[:, 1, :], a["k_norm_w"].to_broadcast([P, HD])).then_inc(small_in, 16)
            for i in range(1, UPT):
                if i >= 2:
                    eng.wait_ge(h_ready, i - 1)
                src = a["x_prompt"][0, P * i:P * (i + 1), :] if i < NT else a["x_sample"].rearrange("b s d -> (b s) d")
                eng.dma_start(xt[0:tile_rows(i), i % 2, :], src).then_inc(x_in[i % 2], 16)
                if i == 1:
                    for j in range(2):
                        for col, width, at in w_cols(j):
                            eng.dma_start(wsb[:, j, :, at:at + width], w_v[:, :, col:col + width]).then_inc(w_in[j], 16)
            for m in range(2, NW):
                eng.wait_ge(z_ready, UPT * (m - 1))
                for col, width, at in w_cols(m):
                    eng.dma_start(wsb[:, m % 2, :, at:at + width], w_v[:, :, col:col + width]).then_inc(w_in[m % 2], 16)

        @block.gpsimd
        def _(eng):
            eng.memset(half_m[:, :], -0.5).then_inc(half_ready, 1)
            eng.memset(uT[:, :, 0:PAD], 0.0).then_inc(u_zero, 1)
            eng.wait_ge(half_ready, 1)
            for j in range(2):
                if j:
                    eng.wait_ge(cp_ready, 1)
                eng.dma_start(cin[0:4 * PAD, :], a["state_conv"][0, 4 * j:4 * j + 4].rearrange("b r d -> (b r) d")).then_inc(cin_in, 16)
            for i in range(UPT):
                n = tile_rows(i)
                eng.wait_ge(sq_done, i + 1)
                eng.tensor_scalar(xss[0:n, 1:2], xss[0:n, 0:1], 1.0 / D, RMS_EPS, ALU.mult, ALU.add).then_inc(half_ready, 1)
                eng.wait_ge(half_ready, 2 + i)
                if i:
                    eng.wait_ge(h_ready, i)
                eng.tensor_tensor(xss[0:n, 2:3], xss[0:n, 1:2], half_m[0:n, 0:1], ALU.pow).then_inc(x_var, 1)
                eng.wait_ge(x_var, i + 1)
            own = 1 + UPT
            e = v = 0
            for n in range(Q0, UNITS):
                m, g, c, i = unit(n)
                rows = tile_rows(i)
                if n >= G0:
                    t = n - G0
                    eng.wait_ge(g_ready, t + 1)
                    gm = t // UPT
                    if i < NT:
                        eng.dma_start(sc["gates"][4 * gm + i][:, 0:SEQ], gst[:, t % 2, :]).then_inc(g_out[t % 2], 16)
                    else:
                        eng.dma_start(sc["gates"][4 * gm:4 * gm + 4][:, :, SEQ:TOK].rearrange("c p t -> p c t"),
                                      gst[:, t % 2, 0:4 * SMP].rearrange("p (c t) -> p c t", c=4)).then_inc(g_out[t % 2], 16)
                elif c < 2:
                    eng.wait_ge(z_ss, e + 1)
                    eng.tensor_scalar(ss[0:rows, 1, :], ss[0:rows, 0, :], 1.0 / HD, RMS_EPS, ALU.mult, ALU.add).then_inc(half_ready, 1)
                    own += 1
                    eng.wait_ge(half_ready, own)
                    eng.tensor_tensor(ss[0:rows, 1, :], ss[0:rows, 1, :], half_m[0:rows, :], ALU.pow).then_inc(z_rstd, 1)
                    eng.wait_ge(z_rstd, e + 1)
                    if stored(n):
                        eng.wait_ge(r_ready, e + 1)
                        src = qkr[0:rows, e % 3, :]
                        if i < NT:
                            dst = a[f"kv{g}p"][0, 0].rearrange("t w h e -> t w (h e)")[:, 0, :]
                            dst = dst if g == 0 else order_view(dst, g, i)
                        elif c == 0:
                            dst = sc["q_smp"][g]
                        else:
                            dst = a[f"kv{g}s"][0].rearrange("b s w h e -> (b s) w (h e)")[:, 0, :]
                        eng.dma_start(dst, src).then_inc(r_out[e % 3], 16)
                    e += 1
                else:
                    if g > 0 or i >= NT - 1:
                        eng.wait_ge(v_ready, v + 1)
                        src = vsb[0:rows, g % 2, i, :]
                        if i < NT:
                            dst = a[f"kv{g}p"][0, 0].rearrange("t w h e -> t w (h e)")[:, 1, :]
                            dst = dst if g == 0 else order_view(dst, g, i)
                        else:
                            dst = a[f"kv{g}s"][0].rearrange("b s w h e -> (b s) w (h e)")[:, 1, :]
                        eng.dma_start(dst, src).then_inc(v_out[g % 2], 16)
                    v += 1
                steps = attention_steps(n)
                if steps and steps[3] is not None:
                    g, s = steps[0], steps[3]
                    o = 8 * g + s
                    eng.wait_ge(st_ready, o + 1)
                    dst = order_view(sc["attn"][g][:, (s % 2) * 4 * ACCW:(s % 2 + 1) * 4 * ACCW], g, s // 2)
                    eng.dma_start(dst, st[:, o % 4, :, :].rearrange("p h w -> p (h w)")).then_inc(st_out[o % 4], 16)
            for j in range(3):
                eng.wait_ge(sc_ready, 2 * j + 2)
                if j == 0:
                    eng.dma_start(a["conv_p"][0, 0], xt[0:PAD, 0, :]).then_inc(so_out[0], 16)
                else:
                    eng.dma_start(a["conv_s"][0, 4 * j - 4:4 * j].rearrange("b r d -> (b r) d"), xt[0:4 * PAD, j % 2, :]).then_inc(so_out[j % 2], 16)
            eng.wait_ge(so_out[0], 32)
            eng.wait_ge(so_out[1], 16)
            for j in range(2):
                eng.wait_ge(g_out[j], 16 * GLU // 2)
                eng.wait_ge(v_out[j], 16 * sum(2 if g == 0 else UPT for g in range(j, NG, 2)))
            for j in range(3):
                eng.wait_ge(r_out[j], r_out_count(len(qk_units) - 3 + j))
            for j in range(4):
                eng.wait_ge(st_out[j], 16 * 6)

        @block.tensor
        def _(eng):
            eng.wait_ge(small_in, 16 * SMALL)
            turn = 0
            for j in range(2):
                eng.wait_ge(cin_in, 16 * (j + 1))
                if j:
                    eng.wait_ge(cs_ready, 1)
                for c in range(DC):
                    mm = eng.transpose(pp[:, c // 4, (c % 4) * P:(c % 4) * P + 4 * PAD], cin[0:4 * PAD, c * P:(c + 1) * P], cst[0:4 * PAD, C_ID:C_ID + 4 * PAD])
                mm.then_inc(cp_ready, 1)
            eng.wait_ge(cs_ready, 2)
            for c in range(DC):
                mm = eng.transpose(pp[:, c // 4, (c % 4) * P:(c % 4) * P + VEC], rows33[:, c * P:(c + 1) * P], cst[0:VEC, C_ID:C_ID + VEC])
            mm.then_inc(cp_ready, 1)
            for i in range(UPT):
                n = tile_rows(i)
                eng.wait_ge(h_ready, i + 1)
                eng.wait_ge(*((hT_ready, i) if i else (cs_ready, 3)))
                for c in range(DC):
                    mm = eng.transpose(pp[:, c // 4, (c % 4) * P:(c % 4) * P + n], ht[0:n, c * P:(c + 1) * P], cst[0:n, C_ID:C_ID + n])
                mm.then_inc(hp_ready, 1)
            eng.wait_ge(hT_ready, UPT)
            t = 0
            o = 0
            for n in range(UNITS):
                m, g, c, i = unit(n)
                if i == 0:
                    eng.wait_ge(w_in[m % 2], w_count(m))
                wait_bank(eng, n)
                z = zp[n % 2]
                if Q0 <= n < G0:
                    for k in range(DC):
                        tok = hT[:, k, SEQ:TOK] if i == NT else hT[:, k, P * i:P * (i + 1)] if g == 0 else hT[:, k, i:SEQ:NT]
                        mm = eng.matmul(z[0:tile_rows(i), :], tok, wsb[:, m % 2, k, :], start=(k == 0), stop=(k == DC - 1))
                elif i < NT:
                    col = i * P
                    for k in range(DC):
                        mm = eng.matmul(z[:, :], wsb[:, m % 2, k, col:col + P], hT[:, k, 0:SEQ], start=(k == 0), stop=(k == DC - 1))
                else:
                    for j in range(4):
                        for k in range(DC):
                            mm = eng.matmul(z[:, SMP * j:SMP * (j + 1)], wsb[:, m % 2, k, P * j:P * (j + 1)], hT[:, k, SEQ:TOK],
                                            start=(k == 0), stop=(k == DC - 1))
                mm.then_inc(z_ready, 1)
                if n - 1 in tr_units:
                    e = qk_units.index(n - 1)
                    eng.wait_ge(r_ready, e + 1)
                    if t:
                        eng.wait_ge(tr_out, t)
                    for j in range(4):
                        mm = eng.transpose(tp[:, P * j:P * (j + 1)], qkr[:, e % 3, P * j:P * (j + 1)], ident)
                    mm.then_inc(tr_ready, 1)
                    t += 1
                steps = attention_steps(n)
                if steps:
                    ga, s_, t_, o_ = steps
                    if s_ is not None:
                        ia = s_ // 2
                        eng.wait_ge(tr_out, 8 * (ga + 1))
                        for b, (heads, keys) in enumerate(sub_batches(ga, s_)):
                            q = sub_no[ga, s_, b]
                            if q >= 2:
                                eng.wait_ge(m_ready, q - 1)
                            nk = len(keys)
                            for j, h in enumerate(heads):
                                r = (h % 2) * HD
                                mm = eng.matmul(ap_[q % 2][:, j * nk * P:(j + 1) * nk * P], qT[r:r + HD, ga % 2, h // 2, P * ia:P * (ia + 1)],
                                                kT[r:r + HD, ga % 2, h // 2, P * keys[0]:P * (keys[-1] + 1)], start=True, stop=True)
                            mm.then_inc(s_ready, 1)
                    if t_ is not None:
                        for b, (heads, keys) in enumerate(sub_batches(ga, t_)):
                            q = sub_no[ga, t_, b]
                            eng.wait_ge(e_ready, q + 1)
                            if q >= 2:
                                eng.wait_ge(pt_ready, q - 1)
                            for j in range(len(heads) * len(keys)):
                                mm = eng.transpose(pp[:, q % 2, P * j:P * (j + 1)], s_sb[:, q % 4, P * j:P * (j + 1)], ident)
                            mm.then_inc(p_ready, 1)
                    if o_ is not None:
                        if o:
                            eng.wait_ge(st_ready, o)
                        eng.wait_ge(v_ready, UPT * (ga + 1))
                        for b, (heads, keys) in enumerate(sub_batches(ga, o_)):
                            q = sub_no[ga, o_, b]
                            eng.wait_ge(pt_ready, q + 1)
                            nk = len(keys)
                            for j, h in enumerate(heads):
                                at = (b * len(heads) + j) * HD
                                for x, key in enumerate(keys):
                                    mm = eng.matmul(op[:, at:at + HD], pt[:, q % 4, (j * nk + x) * P:(j * nk + x + 1) * P],
                                                    vsb[:, ga % 2, key, h * HD:(h + 1) * HD], start=(x == 0), stop=(x == nk - 1))
                        mm.then_inc(o_ready, 1)
                        o += 1
            eng.wait_ge(u_ready, 13)
            eng.wait_ge(pt_ready, len(subs))
            for j in range(3):
                if j:
                    eng.wait_ge(sc_ready, 2 * j)
                w = PAD if j == 0 else 4 * PAD
                for c in range(DC):
                    src = uT[:, c, SEQ:SEQ + PAD] if j == 0 else st4[:, c, 4 * j - 4:4 * j, :].rearrange("p b r -> p (b r)")
                    mm = eng.transpose(pp[0:w, c // 4, (c % 4) * P:(c % 4 + 1) * P], src, ident)
                mm.then_inc(so_ready, 1)

        @block.scalar
        def _(eng):
            for i in range(UPT):
                n = tile_rows(i)
                eng.wait_ge(x_in[i % 2], 16 * (i // 2 + 1))
                if i:
                    eng.wait_ge(h_ready, i)
                eng.activation(squares[0:n, :], xt[0:n, i % 2, :], ACT.Square, accum_out=xss[0:n, 0:1]).then_inc(sq_done, 1)
            t = e = 0
            for n in range(UNITS):
                m, g, c, i = unit(n)
                rows = tile_rows(i)
                if Q0 <= n < G0 and c < 2:
                    eng.wait_ge(z_ready, n + 1)
                    if e:
                        eng.wait_ge(z_ss, e)
                    eng.activation(sq[0:rows, :], zp[n % 2][0:rows, :], ACT.Square).then_inc(z_sq, 1)
                    e += 1
                elif n < Q0:
                    k = n // UPT
                    if i < 2:
                        eng.wait_ge(z_ready, n + 1)
                        if k:
                            eng.wait_ge(u_ready, 3 * k)
                        eng.activation(sg[:, i, :], zp[n % 2][:, :], ACT.Sigmoid).then_inc(z_free_a, 1)
                    elif i == NT:
                        eng.wait_ge(z_ready, n + 1)
                        eng.wait_ge(u_ready, 3 * k + 2)
                        eng.activation(sg[:, 0, 0:2 * SMP], zp[n % 2][:, 0:2 * SMP], ACT.Sigmoid).then_inc(sg_ready, 1)
                elif n >= G0:
                    k = n - G0
                    w = 512 if i < NT else 4 * SMP
                    eng.wait_ge(z_ready, n + 1)
                    if k >= 2:
                        eng.wait_ge(g_out[k % 2], 16 * (k // 2))
                        eng.wait_ge(g_ready, k - 1)
                    eng.activation(gst[:, k % 2, 0:w], zp[n % 2][:, 0:w], ACT.Sigmoid).then_inc(g_ready, 1)
                    eng.wait_ge(g_ready, k + 1)
                    eng.sem_inc(z_free_a, 1)
                if n - 1 in tr_units:
                    gt, ct, it = unit(n - 1)[1:]
                    eng.wait_ge(tr_ready, t + 1)
                    dst = (qT if ct == 0 else kT)[:, gt % 2, :, P * it:P * (it + 1)]
                    if gt >= 2:
                        eng.wait_ge(s_ready, sub_no[gt - 2, 7, len(sub_batches(gt - 2, 7)) - 1] + 1)
                    eng.activation(dst, tp[:, :].rearrange("p (a b) -> p a b", a=4), ACT.Copy).then_inc(tr_out, 1)
                    t += 1
                steps = attention_steps(n)
                if steps:
                    ga, s_, t_, o_ = steps
                    if t_ is not None:
                        for b, (heads, keys) in enumerate(sub_batches(ga, t_)):
                            q = sub_no[ga, t_, b]
                            w = P * len(heads) * len(keys)
                            eng.wait_ge(p_ready, q + 1)
                            if ga * 8 + t_ >= 2:
                                eng.wait_ge(o_ready, ga * 8 + t_ - 1)
                            eng.activation(pt[:, q % 4, 0:w], pp[:, q % 2, 0:w], ACT.Copy).then_inc(pt_ready, 1)
                    if s_ is not None:
                        for b, (heads, keys) in enumerate(sub_batches(ga, s_)):
                            q = sub_no[ga, s_, b]
                            slot = (8 * ga + s_) % 4
                            w = P * len(keys)
                            eng.wait_ge(m_ready, q + 1)
                            for j in range(len(heads)):
                                ins = eng.activation(s_sb[:, q % 4, j * w:(j + 1) * w], s_sb[:, q % 4, j * w:(j + 1) * w], ACT.Exp,
                                                     bias=nm[:, q % 4, j:j + 1], accum_out=st[:, slot, b * len(heads) + j, HD + 1:HD + 2])
                            ins.then_inc(e_ready, 1)
            for j in range(3):
                w = PAD if j == 0 else 4 * PAD
                eng.wait_ge(so_ready, j + 1)
                if j == 2:
                    eng.wait_ge(so_out[0], 16)
                for b in range(2):
                    eng.activation(xt[0:w, j % 2, 512 * b:512 * (b + 1)], pp[0:w, b, :], ACT.Copy).then_inc(sc_ready, 1)

        @block.vector
        def _(eng):
            count = {"chain": 0}

            def link(ins):
                count["chain"] += 1
                ins.then_inc(chain, 1)
                eng.wait_ge(chain, count["chain"])

            def signal(ins, s, n):
                ins.then_inc(s, 1)
                eng.wait_ge(s, n)

            eng.wait_ge(small_in, 16 * SMALL)
            for w in range(2):
                lo, hi = (qkw[:, w, x:x + 32].unsqueeze(1).to_broadcast([P, 9, 32]) for x in (0, 32))
                link(eng.tensor_tensor(rc[:, w, :, 0:32], trig[:, :, 0:32], lo, ALU.mult))
                link(eng.tensor_tensor(rc[:, w, :, 32:64], trig[:, :, 0:32], hi, ALU.mult))
                link(eng.tensor_tensor(rs[:, w, :, 0:32], trig[:, :, 32:64], hi, ALU.mult))
                link(eng.tensor_tensor(rs[:, w, :, 32:64], trig[:, :, 64:96], lo, ALU.mult))
            for j in range(2):
                eng.wait_ge(cp_ready, j + 1)
                for c2 in range(2):
                    src = pp[:, c2, :].rearrange("p (c x) -> p c x", c=4)[:, :, 0:4 * PAD]
                    for c in range(4):
                        ins = eng.tensor_copy(uS[:, 4 * c2 + c, 4 * j:4 * j + 4, 0:PAD], src[:, c, :].rearrange("p (b r) -> p b r", b=4))
                        if c2 == 1 and c == 3:
                            signal(ins, cs_ready, j + 1)
                        else:
                            link(ins)
            eng.wait_ge(cp_ready, 3)
            for b in range(2):
                ins = eng.tensor_copy(vec[:, 4 * b:4 * b + 4, :], pp[:, b, :].rearrange("p (c x) -> p c x", c=4)[:, :, 0:VEC])
                if b:
                    signal(ins, cs_ready, 3)
                else:
                    link(ins)
            for i in range(UPT):
                n = tile_rows(i)
                eng.wait_ge(x_var, i + 1)
                if i:
                    eng.wait_ge(hp_ready, i)
                signal(eng.tensor_scalar(ht[0:n, :], xt[0:n, i % 2, :], xss[0:n, 2:3], None, ALU.mult), h_ready, i + 1)
                eng.wait_ge(hp_ready, i + 1)
                at = P * i
                for b in range(2):
                    ins = eng.tensor_tensor(hT[:, 4 * b:4 * b + 4, at:at + n], pp[:, b, :].rearrange("p (c x) -> p c x", c=4)[:, :, 0:n],
                                            n1[:, 4 * b:4 * b + 4].unsqueeze(2).to_broadcast([P, 4, n]), ALU.mult)
                    if b:
                        signal(ins, hT_ready, i + 1)
                    else:
                        link(ins)
            done = [0]

            def conv_upto(last):
                for step in range(done[0], last):
                    half, rest = divmod(step, 8 * TAPS)
                    tap, (c, smp) = rest // 8, divmod(rest % 8, 2)
                    c += 4 * half
                    if smp:
                        out, src = yT[:, c, SEQ:TOK].rearrange("p (b s) -> p b s", b=NB), uS[:, c, :, tap:tap + NS]
                    else:
                        out, src = yT[:, c, 0:SEQ], uT[:, c, tap:tap + SEQ]
                    if tap:
                        eng.wait_ge(conv_done, step - 7)
                        ins = eng.scalar_tensor_tensor(out=out, in0=src, scalar=cw[:, c, tap:tap + 1], in1=out, op0=ALU.mult, op1=ALU.add)
                    else:
                        ins = eng.tensor_scalar(out, src, cw[:, c, 0:1], cb[:, c:c + 1], ALU.mult, ALU.add)
                    ins.then_inc(conv_done, 1)
                done[0] = max(done[0], last)

            eng.wait_ge(u_zero, 1)
            e = v = u = o = fv = 0
            for n in range(UNITS):
                m, g, c, i = unit(n)
                rows = tile_rows(i)
                z = zp[n % 2]
                if n < G0:
                    eng.wait_ge(z_ready, n + 1)
                if Q0 <= n < G0 and c < 2:
                    table = 8 if i == NT else i if g == 0 else NT + i
                    eng.wait_ge(z_sq, e + 1)
                    signal(eng.tensor_reduce(ss[0:rows, 0, :], sq[0:rows, :].rearrange("p (h d) -> p h d", h=HG), AX, ALU.add), z_ss, e + 1)
                    eng.wait_ge(z_rstd, e + 1)
                    fv += 1
                    signal(eng.tensor_tensor(qn[0:rows, :].rearrange("p (h d) -> p h d", h=HG), z[0:rows, :].rearrange("p (h d) -> p h d", h=HG),
                                             ss[0:rows, 1, :].unsqueeze(2).to_broadcast([rows, HG, HD]), ALU.mult), z_free_v, fv)
                    x = qn[0:rows, :].rearrange("p (h w d) -> p h w d", h=HG, w=2)
                    y = t2[0:rows, :].rearrange("p (h w d) -> p h w d", h=HG, w=2)
                    link(eng.tensor_tensor(t1[0:rows, :].rearrange("p (h d) -> p h d", h=HG), qn[0:rows, :].rearrange("p (h d) -> p h d", h=HG),
                                           rc[0:rows, c, table, :].unsqueeze(1).to_broadcast([rows, HG, HD]), ALU.mult))
                    for w in range(2):
                        link(eng.tensor_tensor(y[:, :, w, :], x[:, :, 1 - w, :],
                                               rs[0:rows, c, table, 32 * w:32 * w + 32].unsqueeze(1).to_broadcast([rows, HG, 32]), ALU.mult))
                    if e >= 3:
                        eng.wait_ge(tr_ready, sum(j in tr_units for j in qk_units[:e - 2]))
                        if r_out_count(e - 3):
                            eng.wait_ge(r_out[e % 3], r_out_count(e - 3))
                    e += 1
                    signal(eng.tensor_tensor(qkr[0:rows, (e - 1) % 3, :], t1[0:rows, :], t2[0:rows, :], ALU.add), r_ready, e)
                elif Q0 <= n < G0:
                    if g >= 2:
                        eng.wait_ge(o_ready, 8 * (g - 1))
                        eng.wait_ge(v_out[g % 2], 16 * 2)
                    v += 1
                    ins = eng.tensor_copy(vsb[0:rows, g % 2, i, :], z[0:rows, :])
                    signal(ins, v_ready, v)
                    fv += 1
                    eng.sem_inc(z_free_v, 1)
                elif n < Q0:
                    k = n // UPT
                    if i in (2, 3):
                        ch = 2 * k + i - 2
                        eng.wait_ge(z_free_a, 2 * k + i - 1)
                        u += 1
                        signal(eng.tensor_tensor(uT[:, ch, PAD:PAD + SEQ], z[:, :], sg[:, i - 2, :], ALU.mult), u_ready, u)
                        fv += 1
                        eng.sem_inc(z_free_v, 1)
                    elif i == NT:
                        eng.wait_ge(sg_ready, k + 1)
                        u += 1
                        for ch in range(2):
                            ins = eng.tensor_tensor(uS[:, 2 * k + ch, :, PAD:PAD + NS], z[:, (2 + ch) * SMP:(3 + ch) * SMP].rearrange("p (b s) -> p b s", b=NB),
                                                    sg[:, 0, ch * SMP:(ch + 1) * SMP].rearrange("p (b s) -> p b s", b=NB), ALU.mult)
                            if ch == 0:
                                link(ins)
                        signal(ins, u_ready, u)
                        fv += 1
                        eng.sem_inc(z_free_v, 1)
                conv_upto(CONV_AT[n])
                steps = attention_steps(n)
                if steps:
                    ga, s_, t_, o_ = steps
                    if s_ is not None:
                        for b, (heads, keys) in enumerate(sub_batches(ga, s_)):
                            q = sub_no[ga, s_, b]
                            so = 8 * ga + s_
                            nh, w = len(heads), P * len(keys)
                            mask = cst[:, C_STRIDE:C_STRIDE + P] if ga == 2 else cst[:, C_DIAG + P - w:C_DIAG + P]
                            eng.wait_ge(s_ready, q + 1)
                            if q >= 4:
                                eng.wait_ge(p_ready, q - 3)
                            if so >= 4:
                                eng.wait_ge(st_out[so % 4], 16 * (so // 4))
                            sv = s_sb[:, q % 4, 0:nh * w].rearrange("p (h k) -> p h k", h=nh)
                            link(eng.scalar_tensor_tensor(out=sv, in0=ap_[q % 2][:, 0:nh * w].rearrange("p (h k) -> p h k", h=nh), scalar=QK_SCALE,
                                                          in1=mask.unsqueeze(1).to_broadcast([P, nh, w]), op0=ALU.mult, op1=ALU.add))
                            mx = st[:, so % 4, b * nh:(b + 1) * nh, HD:HD + 1]
                            link(eng.tensor_reduce(mx, sv, AX, ALU.max))
                            signal(eng.tensor_scalar(nm[:, q % 4, 0:nh], mx.rearrange("p h o -> p (h o)"), -1.0, None, ALU.mult), m_ready, q + 1)
                    if o_ is not None:
                        eng.wait_ge(o_ready, o + 1)
                        eng.wait_ge(e_ready, sub_no[ga, o_, len(sub_batches(ga, o_)) - 1] + 1)
                        signal(eng.tensor_copy(st[:, o % 4, :, 0:HD], op[:, 0:4 * HD].rearrange("p (h d) -> p h d", h=4)), st_ready, o + 1)
                        o += 1
            eng.wait_ge(z_ready, UNITS)
            for c in range(DC):
                ins = eng.tensor_copy(st4[:, c, :, :], uS[:, c, :, NS:NS + PAD])
                if c == DC - 1:
                    signal(ins, u_ready, u + 1)
                else:
                    link(ins)
            eng.wait_ge(conv_done, CONV)


def sample_attention(nc, a, sc, cst, hs):
    with ExitStack() as ctx:
        def sb(name, shape, dt=F32):
            return ctx.enter_context(nc.sbuf_tensor("s_" + name, shape, dt))

        def sem(name):
            return ctx.enter_context(nc.semaphore("s_" + name))

        k1 = sb("k1", [P, 2, GW])
        k2 = sb("k2", [P, 2, NS, GW])
        k3 = sb("k3", [P, 2, GW])
        q1 = sb("q1", [P, 2, NS, GW])
        q2 = sb("q2", [P, 2, NS, GW])
        q3 = sb("q3", [P, 2, GW])
        v1 = sb("v1", [P, 2, GW])
        v2 = sb("v2", [P, 2, NS, GW])
        v3 = sb("v3", [P, 2, GW])
        pr1 = sb("pr1", [P, 2, NS, GW])
        pr2 = sb("pr2", [P, 2, NS, GW])
        pr3 = sb("pr3", [P, 2, GW])
        S = sb("S", [P, NG, HG, SMP])
        S3 = sb("S3", [P, HG, NB])
        pw = sb("pw", [P, 2, HG])
        R = sb("R", [SMP, NG * HG, P])
        PT = sb("PT", [P, NG * HG, SMP])
        new = sb("new", [SMP, 6, 2 * GW])
        qn = sb("q", [SMP, NG, GW])
        N = sb("N", [SMP, 6, HG])
        pn = sb("pn", [SMP, 6, GW])
        mx = sb("mx", [SMP, NG * HG])
        M = sb("M", [SMP, 3, HG])
        den = sb("den", [SMP, 3, HG])
        rp = [ctx.enter_context(nc.psum_tensor(f"s_r{i}", [P, 512], F32)) for i in range(6)]
        acc = ctx.enter_context(nc.psum_tensor("s_acc", [P, 512], F32))

        k_in = [sem("k_in0"), sem("k_in1")]
        v_in = [sem("v_in0"), sem("v_in1")]
        new_zero = sem("new_zero")
        new_in = sem("new_in")
        chain = sem("chain")
        pk_ready = sem("pk_ready")
        k_used = sem("k_used")
        S_ready = sem("S_ready")
        r_ready = sem("r_ready")
        x_ready = sem("x_ready")
        e_ready = sem("e_ready")
        b_ready = sem("b_ready")
        PT_ready = sem("PT_ready")
        v_prod = sem("v_prod")
        v_prod2 = sem("v_prod2")
        v_sum = sem("v_sum")

        def cache(g, b, w):
            rows = a[f"cache_kv_g{g + 1}"][0, b].rearrange("l w h e -> l w (h e)")[:, w, :]
            if g == 1:
                return rows.rearrange("(m r) x -> m r x", r=NS)
            if g == 2:
                return rows.rearrange("(m r) x -> m r x", r=16)[:, 0:NS, :]
            return rows

        block = ctx.enter_context(nc.Block())

        @block.sync
        def _(eng):
            for b in range(NB):
                s = b % 2
                if b >= 2:
                    eng.wait_ge(k_used, b - 1)
                eng.dma_start(k1[:, s, :], cache(0, b, 0)).then_inc(k_in[s], 16)
                eng.dma_start(k2[:, s, :, :], cache(1, b, 0)).then_inc(k_in[s], 16)
                eng.dma_start(k3[:, s, :], cache(2, b, 0)).then_inc(k_in[s], 16)
                qrow = [sc["q_smp"][g][NS * b:NS * (b + 1), :] for g in range(NG)]
                eng.dma_start(q1[:, s, :, :], qrow[0].unsqueeze(0).to_broadcast([P, NS, GW])).then_inc(k_in[s], 16)
                eng.dma_start(q2[:, s, :, :], qrow[1].unsqueeze(0).to_broadcast([P, NS, GW])).then_inc(k_in[s], 16)
                eng.dma_start(q3[:, s, :], qrow[2].unsqueeze(0).to_broadcast([P // NS, NS, GW])).then_inc(k_in[s], 16)
            for b in range(NB):
                s = b % 2
                if b >= 2:
                    eng.wait_ge(v_prod, b - 1)
                    eng.wait_ge(v_prod2, b - 1)
                eng.dma_start(v1[:, s, :], cache(0, b, 1)).then_inc(v_in[s], 16)
                eng.dma_start(v2[:, s, :, :], cache(1, b, 1)).then_inc(v_in[s], 16)
                eng.dma_start(v3[:, s, :], cache(2, b, 1)).then_inc(v_in[s], 16)

        @block.gpsimd
        def _(eng):
            eng.memset(new[:, :, :], 0.0).then_inc(new_zero, 1)
            eng.wait_ge(new_zero, 1)
            kv = [a[f"kv{g}s"][0].rearrange("b s w h e -> (b s) (w h e)") for g in range(NG)]
            for d in range(NS):
                eng.dma_start(new[d:SMP, d, :], kv[0][0:SMP - d, :]).then_inc(new_in, 16)
            for g in (1, 2):
                eng.dma_start(new[:, 3 + g, :], kv[g]).then_inc(new_in, 16)
            for g in range(NG):
                eng.dma_start(qn[:, g, :], sc["q_smp"][g]).then_inc(new_in, 16)
            for b in range(NB):
                s = b % 2
                eng.wait_ge(k_in[s], 96 * (b // 2 + 1))
                if b >= 2:
                    eng.wait_ge(k_used, b - 1)
                eng.tensor_tensor(pr2[:, s, :, :], k2[:, s, :, :], q2[:, s, :, :], ALU.mult).then_inc(pk_ready, 1)
            eng.wait_ge(PT_ready, 1)
            for b in range(NB):
                s = b % 2
                eng.wait_ge(v_in[s], 48 * (b // 2 + 1))
                if b >= 2:
                    eng.wait_ge(v_sum, b - 1)
                for t in range(NS):
                    ins = eng.tensor_tensor(pr2[:, s, t, :].rearrange("p (h e) -> p h e", h=HG), v2[:, s, t, :].rearrange("p (h e) -> p h e", h=HG),
                                            PT[:, HG:2 * HG, NS * b + t].unsqueeze(2).to_broadcast([P, HG, HD]), ALU.mult)
                ins.then_inc(v_prod2, 1)

        @block.vector
        def _(eng):
            count = [0]

            def link(ins):
                count[0] += 1
                ins.then_inc(chain, 1)
                eng.wait_ge(chain, count[0])

            def signal(ins, s, n):
                ins.then_inc(s, 1)
                eng.wait_ge(s, n)

            def by_head(x):
                return x.rearrange("p s (h e) -> p s h e", h=HG)

            for b in range(NB):
                s = b % 2
                eng.wait_ge(k_in[s], 96 * (b // 2 + 1))
                link(eng.tensor_tensor(pr1[:, 0, :, :], k1[:, s, :].unsqueeze(1).to_broadcast([P, NS, GW]), q1[:, s, :, :], ALU.mult))
                link(eng.tensor_reduce(S[:, 0, :, NS * b:NS * (b + 1)].rearrange("p h s -> p s h"), by_head(pr1[:, 0, :, :]), AX, ALU.add))
                link(eng.tensor_tensor(pr3[:, 0, :], k3[:, s, :], q3[:, s, :], ALU.mult))
                link(eng.tensor_reduce(S3[:, :, b], pr3[:, 0, :].rearrange("p (h e) -> p h e", h=HG), AX, ALU.add))
                eng.wait_ge(pk_ready, b + 1)
                signal(eng.tensor_reduce(S[:, 1, :, NS * b:NS * (b + 1)].rearrange("p h s -> p s h"), by_head(pr2[:, s, :, :]), AX, ALU.add), k_used, b + 1)
            hb = [S[:, g, :, :].rearrange("p h (b s) -> p (h b) s", s=NS) for g in range(NG)]

            def rowmask(at, rows=HG * NB):
                return cst[:, at:at + NS].unsqueeze(1).to_broadcast([P, rows, NS])

            link(eng.scalar_tensor_tensor(out=hb[0], in0=hb[0], scalar=QK_SCALE, in1=rowmask(C_NEW1), op0=ALU.mult, op1=ALU.add))
            link(eng.tensor_scalar(S[:, 1, :, :], S[:, 1, :, :], QK_SCALE, None, ALU.mult))
            link(eng.tensor_tensor(hb[2], S3[:, :, :].rearrange("p h b -> p (h b)").unsqueeze(2).to_broadcast([P, HG * NB, NS]), rowmask(C_KEEP), ALU.mult))
            signal(eng.scalar_tensor_tensor(out=hb[2], in0=hb[2], scalar=QK_SCALE, in1=rowmask(C_DROP), op0=ALU.mult, op1=ALU.add), S_ready, 1)
            eng.wait_ge(new_in, 16 * 9)
            link(eng.tensor_tensor(pn[:, 0:NS, :], new[:, 0:NS, 0:GW], qn[:, 0:1, :].to_broadcast([SMP, NS, GW]), ALU.mult))
            link(eng.tensor_tensor(pn[:, NS:6, :], new[:, NS:6, 0:GW], qn[:, 1:3, :], ALU.mult))
            link(eng.tensor_reduce(N[:, :, :], by_head(pn[:, :, :]), AX, ALU.add))
            link(eng.tensor_scalar(N[:, NS:6, :], N[:, NS:6, :], QK_SCALE, None, ALU.mult))
            link(eng.scalar_tensor_tensor(out=N[:, 0:NS, :], in0=N[:, 0:NS, :], scalar=QK_SCALE,
                                          in1=cst[0:SMP, C_BACK:C_BACK + NS].unsqueeze(2).to_broadcast([SMP, NS, HG]), op0=ALU.mult, op1=ALU.add))
            eng.wait_ge(r_ready, 1)
            for i in range(6):
                link(eng.tensor_copy(R[:, 4 * i:4 * i + 4, :], rp[i][0:SMP, :].rearrange("p (a k) -> p a k", a=4)))
            link(eng.tensor_reduce(mx[:, :], R[:, :, :], AX, ALU.max))
            link(eng.tensor_reduce(M[:, 0, :], mx[:, :].rearrange("p (g h) -> p h g", g=NG), AX, ALU.max))
            link(eng.tensor_reduce(M[:, 1, :], N[:, :, :].rearrange("p d h -> p h d"), AX, ALU.max))
            link(eng.tensor_tensor(M[:, 2, :], M[:, 0, :], M[:, 1, :], ALU.max))
            for g in range(NG):
                link(eng.tensor_tensor(R[:, HG * g:HG * (g + 1), :], R[:, HG * g:HG * (g + 1), :], M[:, 2, :].unsqueeze(2).to_broadcast([SMP, HG, P]), ALU.subtract))
            signal(eng.tensor_tensor(N[:, :, :], N[:, :, :], M[:, 2:3, :].to_broadcast([SMP, 6, HG]), ALU.subtract), x_ready, 1)
            eng.wait_ge(e_ready, 2)
            link(eng.tensor_reduce(mx[:, :], R[:, :, :], AX, ALU.add))
            link(eng.tensor_reduce(den[:, 0, :], mx[:, :].rearrange("p (g h) -> p h g", g=NG), AX, ALU.add))
            link(eng.tensor_reduce(den[:, 1, :], N[:, :, :].rearrange("p d h -> p h d"), AX, ALU.add))
            link(eng.tensor_tensor(den[:, 0, :], den[:, 0, :], den[:, 1, :], ALU.add))
            link(eng.reciprocal(den[:, 2, :], den[:, 0, :]))
            eng.wait_ge(b_ready, 1)
            link(eng.tensor_copy(PT[:, 0:16, :], rp[0][:, :].rearrange("p (a t) -> p a t", a=16)))
            signal(eng.tensor_copy(PT[:, 16:24, :], rp[1][:, 0:8 * SMP].rearrange("p (a t) -> p a t", a=8)), PT_ready, 1)
            for b in range(NB):
                s = b % 2
                eng.wait_ge(v_in[s], 48 * (b // 2 + 1))
                if b >= 2:
                    eng.wait_ge(v_sum, b - 1)
                link(eng.tensor_reduce(pw[:, s, :], PT[:, 2 * HG:3 * HG, NS * b:NS * (b + 1)], AX, ALU.add))
                for t in range(NS):
                    link(eng.tensor_tensor(pr1[:, s, t, :].rearrange("p (h e) -> p h e", h=HG), v1[:, s, :].rearrange("p (h e) -> p h e", h=HG),
                                           PT[:, 0:HG, NS * b + t].unsqueeze(2).to_broadcast([P, HG, HD]), ALU.mult))
                signal(eng.tensor_tensor(pr3[:, s, :].rearrange("p (h e) -> p h e", h=HG), v3[:, s, :].rearrange("p (h e) -> p h e", h=HG),
                                         pw[:, s, :].unsqueeze(2).to_broadcast([P, HG, HD]), ALU.mult), v_prod, b + 1)
            for d in range(6):
                link(eng.tensor_tensor(pn[:, d, :].rearrange("p (h e) -> p h e", h=HG), new[:, d, GW:2 * GW].rearrange("p (h e) -> p h e", h=HG),
                                       N[:, d, :].unsqueeze(2).to_broadcast([SMP, HG, HD]), ALU.mult))
            for d in range(1, 6):
                link(eng.tensor_tensor(pn[:, 0, :], pn[:, 0, :], pn[:, d, :], ALU.add))
            eng.wait_ge(v_sum, NB)
            link(eng.tensor_tensor(pn[:, 0, :], pn[:, 0, :], acc[0:SMP, :], ALU.add))
            link(eng.tensor_tensor(hs[:, :].rearrange("p (h e) -> p h e", h=HG), pn[:, 0, :].rearrange("p (h e) -> p h e", h=HG),
                                   den[:, 2, :].unsqueeze(2).to_broadcast([SMP, HG, HD]), ALU.mult))

        @block.scalar
        def _(eng):
            eng.wait_ge(x_ready, 1)
            eng.activation(R[:, :, :], R[:, :, :], ACT.Exp).then_inc(e_ready, 1)
            eng.activation(N[:, :, :], N[:, :, :], ACT.Exp).then_inc(e_ready, 1)

        @block.tensor
        def _(eng):
            eng.wait_ge(S_ready, 1)
            for j in range(NG * HG):
                mm = eng.transpose(rp[j // 4][0:SMP, P * (j % 4):P * (j % 4 + 1)], S[:, j // HG, j % HG, :], cst[:, C_ID:C_ID + P])
            mm.then_inc(r_ready, 1)
            eng.wait_ge(e_ready, 2)
            for j in range(NG * HG):
                mm = eng.transpose(rp[j // 16][:, SMP * (j % 16):SMP * (j % 16 + 1)], R[:, j, :], cst[0:SMP, C_ID:C_ID + SMP])
            mm.then_inc(b_ready, 1)
            for b in range(NB):
                s = b % 2
                eng.wait_ge(v_prod, b + 1)
                eng.wait_ge(v_prod2, b + 1)
                for t in range(NS):
                    at = C_SELQ + SMP - 1 - (NS * b + t)
                    for x, pr in enumerate((pr1, pr2)):
                        eng.matmul(acc[0:SMP, :], cst[:, at:at + SMP], pr[:, s, t, :], start=(b == 0 and t == 0 and x == 0), stop=False)
                at = C_SELR + (SMP - NS) - NS * b
                eng.matmul(acc[0:SMP, :], cst[:, at:at + SMP], pr3[:, s, :], start=False, stop=(b == NB - 1)).then_inc(v_sum, 1)


def mix(nc, a, sc, cst, yT, hs, late):
    HC = 2 * PH
    wo, wq, skT, mT = late["wo"], late["wq"], late["skT"], late["mT"]
    wo_in, wq_in = late["wo_in"], late["wq_in"]
    with ExitStack() as ctx:
        def sb(name, shape, dt=F32, c=ctx):
            return c.enter_context(nc.sbuf_tensor("m_" + name, shape, dt))

        def sem(name):
            return ctx.enter_context(nc.semaphore("m_" + name))

        wcp = wq[:, :, D:2 * D]
        wap = sb("wap", [P, 4, D])
        ag = sb("ag", [P, NG, HG, ACCW])
        cg = sb("cg", [P, 8, HG])
        cw = sb("cw", [P, NG, HG])
        ho = sb("ho", [P, GW])
        tmp = sb("tmp", [P, GW])
        hoT = sb("hoT", [P, 4, TOK])
        stat = sb("stat", [P, 2, TOK])
        sqy = sb("sqy", [P, 2, TOK])
        gt = sb("gt", [P, 2, 2, TOK])
        vec = sb("vec", [P, 2, DC])
        half_m = sb("half_m", [P, 1])
        sk = sb("sk", [P, HC, HALF])
        bank = [ctx.enter_context(nc.psum_tensor(f"m_b{i}", [P, 512], F32)) for i in range(8)]

        w_in = sem("w_in")
        sk_in = sem("sk_in")
        vec_in = sem("vec_in")
        chain = sem("chain")
        ag_in = sem("ag_in")
        ag_used = sem("ag_used")
        c_max = sem("c_max")
        c_exp = sem("c_exp")
        ho_ready = sem("ho_ready")
        hp_ready = sem("hp_ready")
        hoT_ready = sem("hoT_ready")
        sum_ready = sem("sum_ready")
        d_ready = sem("d_ready")
        sq_ready = sem("sq_ready")
        sq_used = sem("sq_used")
        half_ready = sem("half_ready")
        var_ready = sem("var_ready")
        rstd_ready = sem("rstd_ready")
        yn_ready = sem("yn_ready")
        y_ready = sem("y_ready")
        g_in = [sem("g_in0"), sem("g_in1")]
        pr_ready = sem("pr_ready")
        mix_ready = sem("mix_ready")
        kt_ready = sem("kt_ready")
        skT_ready = sem("skT_ready")

        wq_v = a["w_peer_q"][0].rearrange("(k p) c -> p k c", p=P)
        block = ctx.enter_context(nc.Block())

        @block.sync
        def _(eng):
            with nc.allow_non_contiguous_dma("short rows of small inputs"):
                eng.dma_start(vec[:, 0, :], a["conv_ln_g"][0].rearrange("(c p) -> p c", p=P)).then_inc(vec_in, 16)
                eng.dma_start(vec[:, 1, :], a["conv_ln_b"][0].rearrange("(c p) -> p c", p=P)).then_inc(vec_in, 16)
            for i in range(NT):
                if i:
                    eng.wait_ge(ag_used, i)
                for g in range(NG):
                    eng.dma_start(ag[:, g, :, :].rearrange("p h w -> p (h w)"), sc["attn"][g][P * i:P * (i + 1), :]).then_inc(ag_in, 16)
                if i == 0:
                    eng.dma_start(wcp[:, :, :], a["w_conv_proj"][0].rearrange("(k p) c -> p k c", p=P)).then_inc(w_in, 16)
                    eng.dma_start(wap[:, :, :], a["w_attn_proj"][0].rearrange("(k p) c -> p k c", p=P)).then_inc(w_in, 16)
                    eng.dma_start(sk[:, :, :], a["peer_sub_keys"][0].rearrange("h t k c -> k (h t) c")).then_inc(sk_in, 16)
                    eng.dma_start(wo[:, :, :], a["w_out"][0].rearrange("(k p) c -> p k c", p=P)).then_inc(wo_in, 16)
                    eng.dma_start(wq[:, :, 0:D], wq_v[:, :, 0:D]).then_inc(wq_in[0], 16)
            for c in range(DC):
                if c >= 2:
                    eng.wait_ge(mix_ready, c - 1)
                for w in range(2):
                    eng.dma_start(gt[:, c % 2, w, :], sc["gates"][DC * w + c]).then_inc(g_in[c % 2], 16)
            eng.wait_ge(pr_ready, DC)
            eng.dma_start(wq[:, :, D:2 * D], wq_v[:, :, D:2 * D]).then_inc(wq_in[1], 16)

        @block.gpsimd
        def _(eng):
            eng.memset(half_m[:, :], -0.5).then_inc(half_ready, 1)
            eng.wait_ge(half_ready, 1)
            eng.wait_ge(var_ready, 1)
            eng.tensor_tensor(stat[:, 1, :], stat[:, 1, :], half_m[:, :].to_broadcast([P, TOK]), ALU.pow).then_inc(rstd_ready, 1)

        @block.tensor
        def _(eng):
            ident = cst[:, C_ID:C_ID + P]
            for i in range(UPT):
                n = tile_rows(i)
                src = ho if i < NT else hs
                if i < NT:
                    eng.wait_ge(ho_ready, i + 1)
                if i:
                    eng.wait_ge(hoT_ready, i)
                for c in range(4):
                    mm = eng.transpose(bank[0][:, P * c:P * c + n], src[0:n, P * c:P * (c + 1)], cst[0:n, C_ID:C_ID + n])
                mm.then_inc(hp_ready, 1)
            eng.wait_ge(sk_in, 16)
            for j in range(4):
                for c in range(4):
                    mm = eng.transpose(bank[4 + j][:, P * c:P * (c + 1)], sk[:, 4 * j + c, :], ident)
            mm.then_inc(kt_ready, 1)
            ones = cst[:, C_ONE:C_ONE + P]
            for k in range(DC):
                eng.matmul(bank[2][:, :], ones, yT[:, k, 0:SEQ], start=(k == 0), stop=(k == DC - 1))
            for k in range(DC):
                mm = eng.matmul(bank[3][:, 0:SMP], ones, yT[:, k, SEQ:TOK], start=(k == 0), stop=(k == DC - 1))
            mm.then_inc(sum_ready, 1)
            eng.wait_ge(d_ready, 1)
            for k in range(DC):
                eng.wait_ge(sq_ready, k + 1)
                eng.matmul(bank[2][:, :], ones, sqy[:, k % 2, 0:SEQ], start=(k == 0), stop=(k == DC - 1))
                eng.matmul(bank[3][:, 0:SMP], ones, sqy[:, k % 2, SEQ:TOK], start=(k == 0), stop=(k == DC - 1)).then_inc(sq_used, 1)
            eng.wait_ge(w_in, 32)
            eng.wait_ge(hoT_ready, UPT)
            eng.wait_ge(skT_ready, 1)
            eng.wait_ge(var_ready, 1)
            for c in range(DC):
                bc, ba, bs = (bank[3 * (c % 2) + 2 + x] for x in range(3))
                if c >= 2:
                    eng.wait_ge(mix_ready, c - 1)
                for k in range(4):
                    w = wap[:, k, P * c:P * (c + 1)]
                    eng.matmul(ba[:, :], w, hoT[:, k, 0:SEQ], start=(k == 0), stop=(k == 3))
                for k in range(4):
                    w = wap[:, k, P * c:P * (c + 1)]
                    eng.matmul(bs[:, SMP:2 * SMP], w, hoT[:, k, SEQ:TOK], start=(k == 0), stop=(k == 3))
                if c == 0:
                    eng.wait_ge(y_ready, DC)
                for k in range(DC):
                    eng.matmul(bc[:, :], wcp[:, k, P * c:P * (c + 1)], yT[:, k, 0:SEQ], start=(k == 0), stop=(k == DC - 1))
                for k in range(DC):
                    mm = eng.matmul(bs[:, 0:SMP], wcp[:, k, P * c:P * (c + 1)], yT[:, k, SEQ:TOK], start=(k == 0), stop=(k == DC - 1))
                mm.then_inc(pr_ready, 1)

        @block.scalar
        def _(eng):
            for i in range(NT):
                eng.wait_ge(c_max, i + 1)
                eng.activation(cw[:, :, :], cw[:, :, :], ACT.Exp).then_inc(c_exp, 1)
            for k in range(DC):
                eng.wait_ge(d_ready, k + 1)
                if k >= 2:
                    eng.wait_ge(sq_used, k - 1)
                eng.activation(sqy[:, k % 2, :], yT[:, k, :], ACT.Square).then_inc(sq_ready, 1)
            eng.wait_ge(vec_in, 32)
            for k in range(DC):
                eng.wait_ge(yn_ready, k + 1)
                eng.activation(yT[:, k, :], yT[:, k, :], ACT.Silu, scale=vec[:, 0, k:k + 1], bias=vec[:, 1, k:k + 1]).then_inc(y_ready, 1)

        @block.vector
        def _(eng):
            count = [0]

            def link(ins):
                count[0] += 1
                ins.then_inc(chain, 1)
                eng.wait_ge(chain, count[0])

            def signal(ins, s, n):
                ins.then_inc(s, 1)
                eng.wait_ge(s, n)

            for i in range(NT):
                eng.wait_ge(ag_in, 48 * (i + 1))
                mxs = [ag[:, g, :, HD] for g in range(NG)]
                dns = [ag[:, g, :, HD + 1] for g in range(NG)]
                link(eng.tensor_tensor(cg[:, 0, :], mxs[0], mxs[1], ALU.max))
                link(eng.tensor_tensor(cg[:, 0, :], cg[:, 0, :], mxs[2], ALU.max))
                for g in range(NG):
                    ins = eng.tensor_tensor(cw[:, g, :], mxs[g], cg[:, 0, :], ALU.subtract)
                    if g == NG - 1:
                        signal(ins, c_max, i + 1)
                    else:
                        link(ins)
                eng.wait_ge(c_exp, i + 1)
                for g in range(NG):
                    link(eng.tensor_tensor(cg[:, 1 + g, :], cw[:, g, :], dns[g], ALU.mult))
                link(eng.tensor_tensor(cg[:, 1, :], cg[:, 1, :], cg[:, 2, :], ALU.add))
                link(eng.tensor_tensor(cg[:, 1, :], cg[:, 1, :], cg[:, 3, :], ALU.add))
                link(eng.reciprocal(cg[:, 4, :], cg[:, 1, :]))
                if i:
                    eng.wait_ge(hp_ready, i)
                hv = ho[:, :].rearrange("p (j w e) -> p w j e", w=2, e=HD)
                tv = tmp[:, :].rearrange("p (j w e) -> p w j e", w=2, e=HD)
                for g in range(NG):
                    link(eng.tensor_tensor(cg[:, 5 + g, :], cw[:, g, :], cg[:, 4, :], ALU.mult))
                    for w in range(2):
                        link(eng.tensor_tensor((tv if g else hv)[:, w, :, :], ag[:, g, 4 * w:4 * w + 4, 0:HD],
                                               cg[:, 5 + g, 4 * w:4 * w + 4].unsqueeze(2).to_broadcast([P, 4, HD]), ALU.mult))
                    if g:
                        ins = eng.tensor_tensor(ho[:, :], ho[:, :], tmp[:, :], ALU.add)
                        if g == NG - 1:
                            signal(ins, ho_ready, i + 1)
                            eng.sem_inc(ag_used, 1)
                        else:
                            link(ins)
                eng.wait_ge(hp_ready, i + 1)
                signal(eng.tensor_copy(hoT[:, :, P * i:P * (i + 1)], bank[0][:, :].rearrange("p (c t) -> p c t", c=4)), hoT_ready, i + 1)
            eng.wait_ge(hp_ready, UPT)
            signal(eng.tensor_copy(hoT[:, :, SEQ:TOK], bank[0][:, :].rearrange("p (c t) -> p c t", c=4)[:, :, 0:SMP]), hoT_ready, UPT)
            eng.wait_ge(kt_ready, 1)
            for j in range(4):
                ins = eng.tensor_copy(skT[:, 4 * j:4 * j + 4, :], bank[4 + j][:, :].rearrange("p (c t) -> p c t", c=4))
                if j == 3:
                    signal(ins, skT_ready, 1)
                else:
                    link(ins)
            eng.wait_ge(sum_ready, 1)
            link(eng.tensor_scalar(stat[:, 0, 0:SEQ], bank[2][:, :], 1.0 / D, None, ALU.mult))
            link(eng.tensor_scalar(stat[:, 0, SEQ:TOK], bank[3][:, 0:SMP], 1.0 / D, None, ALU.mult))
            for k in range(DC):
                eng.tensor_tensor(yT[:, k, :], yT[:, k, :], stat[:, 0, :], ALU.subtract).then_inc(d_ready, 1)
            eng.wait_ge(d_ready, DC)
            eng.wait_ge(sq_used, DC)
            link(eng.tensor_scalar(stat[:, 1, 0:SEQ], bank[2][:, :], 1.0 / D, LN_EPS, ALU.mult, ALU.add))
            signal(eng.tensor_scalar(stat[:, 1, SEQ:TOK], bank[3][:, 0:SMP], 1.0 / D, LN_EPS, ALU.mult, ALU.add), var_ready, 1)
            eng.wait_ge(rstd_ready, 1)
            for k in range(DC):
                eng.tensor_tensor(yT[:, k, :], yT[:, k, :], stat[:, 1, :], ALU.mult).then_inc(yn_ready, 1)
            for c in range(DC):
                bc, ba, bs = (bank[3 * (c % 2) + 2 + x] for x in range(3))
                eng.wait_ge(pr_ready, c + 1)
                eng.wait_ge(g_in[c % 2], 32 * (c // 2 + 1))
                link(eng.tensor_tensor(gt[:, c % 2, 0, 0:SEQ], gt[:, c % 2, 0, 0:SEQ], bc[:, :], ALU.mult))
                link(eng.tensor_tensor(gt[:, c % 2, 0, SEQ:TOK], gt[:, c % 2, 0, SEQ:TOK], bs[:, 0:SMP], ALU.mult))
                link(eng.tensor_tensor(gt[:, c % 2, 1, 0:SEQ], gt[:, c % 2, 1, 0:SEQ], ba[:, :], ALU.mult))
                link(eng.tensor_tensor(gt[:, c % 2, 1, SEQ:TOK], gt[:, c % 2, 1, SEQ:TOK], bs[:, SMP:2 * SMP], ALU.mult))
                signal(eng.tensor_tensor(mT[:, c, :], gt[:, c % 2, 0, :], gt[:, c % 2, 1, :], ALU.add), mix_ready, c + 1)


def peer(nc, a, cst, late, yT):
    SLOTS = PH * TOPK
    STEPS = NT * SLOTS + SLOTS // 4
    RING = 6
    LOW = -3.0e38
    QUADS = PH // 2

    OUT_AT = (2, 4, 6, 8)
    SUM_AT = 12
    POW_AT = SUM_AT + RING + 4
    NORM_AT = POW_AT + 2
    TURN_AT = NORM_AT + 2

    def quad_at(i, m):
        return TURN_AT + 4 + 18 * m if i else (3, 13)[m - 2]

    def head_at(i, h):
        return quad_at(i, 0) + 10 + 9 * h if i else 1 + 6 * (h - 1)

    def heads_at(tile, k, lag=0):
        return [(i, h) for i in (tile, tile + 1) for h in range(PH)
                if i <= NT and (i == tile + 1 or (i == 0 and h)) and head_at(i, h) + lag == k]

    def quads_at(tile, k, lag=0):
        return [(i, m) for i in (tile, tile + 1) for m in range(QUADS)
                if i <= NT and (i == tile + 1 or (i == 0 and m >= 2)) and quad_at(i, m) + lag == k]

    wo, wq, skT, mT = late["wo"], late["wq"], late["skT"], late["mT"]
    with ExitStack() as ctx:
        def sb(name, shape, dt=F32):
            return ctx.enter_context(nc.sbuf_tensor("p_" + name, shape, dt))

        def sem(name):
            return ctx.enter_context(nc.semaphore("p_" + name))

        rows = yT[:, :, :].rearrange("p c t -> p (c t)")[:, 0:4 * D].rearrange("p (w s d) -> p w s d", w=2, s=2)
        y, h2 = rows[:, 0], rows[:, 1]
        h2T = mT
        ring = sb("ring", [P, RING, 2 * D])
        w2 = sb("w2", [P, D])
        rms = sb("rms", [P, 4])
        qp = sb("qp", [P, 4, P])
        sco = sb("sco", [P, 2, 4, KEYS])
        idx = sb("idx", [P, 2, SLOTS], U32)
        gw = sb("gw", [P, 2, SLOTS])
        dots = sb("dots", [P, 4])
        gel = sb("gel", [P, 4])
        wgt = sb("wgt", [P, 4])
        diag = sb("diag", [P, 4, P])
        tv = sb("tv", [P, 2, TOPK])
        ti = sb("ti", [P, 2, TOPK], U32)
        tif = sb("tif", [P, 2, TOPK])
        cand = sb("cand", [P, TOPK, TOPK])
        cv = sb("cv", [P, TOPK])
        ci = sb("ci", [P, TOPK], U32)
        ca = sb("ca", [P, 2, TOPK], U32)
        caf = sb("caf", [P, 2, TOPK])
        eq = cand
        e12 = sb("e12", [P, 2, TOPK])
        nmx = sb("nmx", [P, 1])
        ex = sb("ex", [P, TOPK])
        exs = sb("exs", [P, 2])
        idx4 = sb("idx4", [P, SLOTS // 4], U32)
        gw4 = sb("gw4", [P, SLOTS // 4])
        acc, ob, tb = ([ctx.enter_context(nc.psum_tensor(f"p_{w}{i}", [P, 512], F32)) for i in range(2)] for w in ("acc", "o", "t"))
        qb, kb = (ctx.enter_context(nc.psum_tensor("p_" + w, [P, 512], F32)) for w in ("q", "k"))

        w2_in = sem("w2_in")
        x_in = [sem("x_in0"), sem("x_in1")]
        o_ready = sem("o_ready")
        x1_ready = sem("x1_ready")
        x1_sq = sem("x1_sq")
        half_ready = sem("half_ready")
        x1_rstd = sem("x1_rstd")
        h2_ready = sem("h2_ready")
        h2_rep = sem("h2_rep")
        ht_ready = sem("ht_ready")
        h2T_ready = sem("h2T_ready")
        q_ready = sem("q_ready")
        qp_ready = sem("qp_ready")
        s_ready = sem("s_ready")
        sco_ready = sem("sco_ready")
        top_ready = sem("top_ready")
        ex_ready = sem("ex_ready")
        idx_ready = sem("idx_ready")
        quad_in = sem("quad_in")
        chain = sem("chain")
        row_in = [sem(f"row_in{i}") for i in range(RING)]
        dot_ready = sem("dot_ready")
        gel_ready = sem("gel_ready")
        wgt_ready = sem("wgt_ready")
        diag_ready = sem("diag_ready")
        v_used = sem("v_used")
        y_ready = sem("y_ready")
        y_out = [sem("y_out0"), sem("y_out1")]

        def step_tile(t):
            return min(t // SLOTS, NT)

        def step_no(t):
            return step_tile(t), t - SLOTS * step_tile(t)

        def end_of(tile):
            return SLOTS * (tile + 1) if tile < NT else STEPS

        block = ctx.enter_context(nc.Block())

        @block.sync
        def _(eng):
            xs, ys = a["x_sample"].rearrange("b s d -> (b s) d"), a["y_s"].rearrange("b s d -> (b s) d")
            for i in range(2):
                eng.dma_start(y[:, i, :], a["x_prompt"][0, P * i:P * (i + 1), :]).then_inc(x_in[i], 16)
                if i == 0:
                    eng.dma_start(w2[:, :], a["norm2_w"].to_broadcast([P, D])).then_inc(w2_in, 16)
            for i in range(NT):
                s = i % 2
                eng.wait_ge(y_ready, i + 1)
                eng.dma_start(a["y_p"][0, P * i:P * (i + 1), :], y[:, s, :]).then_inc(y_out[s], 16)
                if i + 2 <= NT:
                    n = tile_rows(i + 2)
                    eng.wait_ge(y_out[s], 16 * (i // 2 + 1))
                    src = a["x_prompt"][0, P * (i + 2):P * (i + 3), :] if i + 2 < NT else xs
                    eng.dma_start(y[0:n, s, :], src).then_inc(x_in[s], 16)
                if i + 2 == NT:
                    eng.wait_ge(h2_ready, UPT)
                    for r in range(1, 4):
                        eng.dma_start(h2[SMP * r:SMP * (r + 1), NT % 2, :], h2[0:SMP, NT % 2, :]).then_inc(h2_rep, 16)
                    eng.wait_ge(idx_ready, PH * UPT)
                    for r in range(4):
                        for dst, src in ((idx4, idx), (gw4, gw)):
                            eng.dma_start(dst[SMP * r:SMP * (r + 1), :], src[0:SMP, NT % 2, 32 * r:32 * (r + 1)]).then_inc(quad_in, 16)
            eng.wait_ge(y_ready, UPT)
            eng.dma_start(ys, y[0:SMP, NT % 2, :]).then_inc(y_out[0], 16)
            eng.wait_ge(y_out[0], 48)
            eng.wait_ge(y_out[1], 32)

        @block.gpsimd
        def _(eng):
            def rstd(i):
                n = tile_rows(i)
                eng.wait_ge(x1_sq, i + 1)
                eng.tensor_scalar(rms[0:n, 1:2], rms[0:n, 0:1], 1.0 / D, RMS_EPS, ALU.mult, ALU.add).then_inc(half_ready, 1)
                eng.wait_ge(half_ready, 2 + i)
                eng.tensor_tensor(rms[0:n, 2:3], rms[0:n, 1:2], rms[0:n, 3:4], ALU.pow).then_inc(x1_rstd, 1)

            eng.memset(rms[:, 3:4], -0.5).then_inc(half_ready, 1)
            eng.wait_ge(half_ready, 1)
            rstd(0)
            for t in range(STEPS):
                tile, k = step_no(t)
                if tile < NT and k % TOPK == 0:
                    eng.wait_ge(idx_ready, PH * tile + k // TOPK + 1)
                if tile == NT and k == 0:
                    eng.wait_ge(quad_in, 128)
                if t >= RING:
                    eng.wait_ge(v_used, t - RING + 1)
                col = idx[:, tile % 2, k:k + 1] if tile < NT else idx4[:, k:k + 1]
                eng.indirect_dma_start(ring[:, t % RING, :], None, a["expert_uv"], bass.IndirectOffsetOnAxis(col, 0)).then_inc(row_in[t % RING], 16)
                if tile < NT and k == POW_AT:
                    rstd(tile + 1)

        @block.tensor
        def _(eng):
            def out_quarter(i, r):
                n, h, lo = tile_rows(i), r // 2, (r % 2) * 4
                if r == 0 and i:
                    eng.wait_ge(x1_ready, i)
                for k in range(lo, lo + 4):
                    mm = eng.matmul(ob[h][0:n, :], mT[:, k, P * i:P * i + n], wo[:, k, 512 * h:512 * (h + 1)], start=(k == 0), stop=(k == DC - 1))
                if r == 3:
                    mm.then_inc(o_ready, 1)

            def turn(i):
                n = tile_rows(i)
                eng.wait_ge(h2_ready, i + 1)
                if i:
                    eng.wait_ge(h2T_ready, i)
                for c in range(DC):
                    mm = eng.transpose(tb[c // 4][:, P * (c % 4):P * (c % 4) + n], h2[0:n, i % 2, P * c:P * (c + 1)], cst[0:n, C_ID:C_ID + n])
                mm.then_inc(ht_ready, 1)

            def query(i, m, j):
                n, at = tile_rows(i), 4 * m + j
                if j == 0:
                    eng.wait_ge(h2T_ready, i + 1)
                    eng.wait_ge(late["wq_in"][m // 2], 16)
                    if i or m:
                        eng.wait_ge(qp_ready, QUADS * i + m)
                for k in range(DC):
                    mm = eng.matmul(qb[:, P * j:P * j + n], wq[:, k, P * at:P * (at + 1)], h2T[:, k, P * i:P * i + n], start=(k == 0), stop=(k == DC - 1))
                if j == 3:
                    mm.then_inc(q_ready, 1)

            def scores(i, m):
                n, q = tile_rows(i), QUADS * i + m
                eng.wait_ge(qp_ready, q + 1)
                if q:
                    eng.wait_ge(sco_ready, q)
                for j in range(4):
                    mm = eng.matmul(kb[0:n, P * j:P * (j + 1)], qp[:, j, 0:n], skT[:, 4 * m + j, :], start=True, stop=True)
                mm.then_inc(s_ready, 1)

            eng.wait_ge(late["wo_in"], 16)
            for r in range(4):
                out_quarter(0, r)
            turn(0)
            for m in range(2):
                for j in range(4):
                    query(0, m, j)
                scores(0, m)
            for t in range(STEPS):
                tile, k = step_no(t)
                n = tile_rows(tile)
                eng.wait_ge(row_in[t % RING], 16 * (t // RING + 1))
                if k == 0 and tile:
                    eng.wait_ge(y_ready, tile)
                eng.wait_ge(diag_ready, t + 1)
                for h in range(2):
                    mm = eng.matmul(acc[h][0:n, :], diag[:, t % 4, 0:n], ring[:, t % RING, D + 512 * h:D + 512 * (h + 1)],
                                    start=(k == 0), stop=(t == end_of(tile) - 1))
                mm.then_inc(v_used, 1)
                if tile < NT:
                    if k in OUT_AT:
                        out_quarter(tile + 1, OUT_AT.index(k))
                    if k == TURN_AT:
                        turn(tile + 1)
                    for j in range(4):
                        for i, m in quads_at(tile, k, 2 * j):
                            query(i, m, j)
                    for i, m in quads_at(tile, k, 8):
                        scores(i, m)

        @block.scalar
        def _(eng):
            def square(i):
                n = tile_rows(i)
                eng.wait_ge(x1_ready, i + 1)
                if i >= 2:
                    eng.wait_ge(dot_ready, end_of(i - 2))
                eng.activation(h2[0:n, i % 2, :], y[0:n, i % 2, :], ACT.Square, accum_out=rms[0:n, 0:1]).then_inc(x1_sq, 1)

            def keep_turned(i):
                n = tile_rows(i)
                eng.wait_ge(ht_ready, i + 1)
                for b in range(2):
                    ins = eng.activation(h2T[:, 4 * b:4 * b + 4, P * i:P * i + n], tb[b][:, :].rearrange("p (c t) -> p c t", c=4)[:, :, 0:n], ACT.Copy)
                ins.then_inc(h2T_ready, 1)

            def keep_queries(i, m):
                n, q = tile_rows(i), QUADS * i + m
                eng.wait_ge(q_ready, q + 1)
                if q:
                    eng.wait_ge(s_ready, q)
                eng.activation(qp[:, :, 0:n], qb[:, :].rearrange("p (c t) -> p c t", c=4)[:, :, 0:n], ACT.Copy).then_inc(qp_ready, 1)

            def keep_scores(i, m):
                n, q = tile_rows(i), QUADS * i + m
                eng.wait_ge(s_ready, q + 1)
                if q >= 2:
                    eng.wait_ge(idx_ready, 2 * (q - 1))
                eng.activation(sco[0:n, q % 2, :, :], kb[0:n, :].rearrange("p (c t) -> p c t", c=4), ACT.Copy).then_inc(sco_ready, 1)

            def head_exp(i, h):
                n = tile_rows(i)
                eng.wait_ge(top_ready, PH * i + h + 1)
                eng.activation(ex[0:n, :], cv[0:n, :], ACT.Exp, bias=nmx[0:n, :], accum_out=exs[0:n, 0:1]).then_inc(ex_ready, 1)

            square(0)
            keep_turned(0)
            for m in range(2):
                keep_queries(0, m)
                keep_scores(0, m)
            head_exp(0, 0)
            for t in range(STEPS):
                tile, k = step_no(t)
                n = tile_rows(tile)
                if k == 0 and tile == NT:
                    eng.wait_ge(quad_in, 128)
                w = gw[:, tile % 2, k:k + 1] if tile < NT else gw4[:, k:k + 1]
                shape = cst[:, C_ID:C_ID + P] if tile < NT else cst[:, C_FOLD:C_FOLD + SMP]
                eng.wait_ge(dot_ready, t + 1)
                if t >= 4:
                    eng.wait_ge(v_used, t - 3)
                eng.activation(gel[:, t % 4:t % 4 + 1], dots[:, t % 4:t % 4 + 1], ACT.Gelu).then_inc(gel_ready, 1)
                eng.wait_ge(gel_ready, t + 1)
                eng.activation(wgt[:, t % 4:t % 4 + 1], gel[:, t % 4:t % 4 + 1], ACT.Copy, scale=w).then_inc(wgt_ready, 1)
                eng.wait_ge(wgt_ready, t + 1)
                eng.activation(diag[:, t % 4, 0:n], shape, ACT.Copy, scale=wgt[:, t % 4:t % 4 + 1]).then_inc(diag_ready, 1)
                if tile < NT:
                    if k == SUM_AT:
                        square(tile + 1)
                    if k == TURN_AT:
                        keep_turned(tile + 1)
                    for i, m in quads_at(tile, k, 7):
                        keep_queries(i, m)
                    for i, m in quads_at(tile, k, 9):
                        keep_scores(i, m)
                    for i, h in heads_at(tile, k):
                        head_exp(i, h)

        @block.vector
        def _(eng):
            count = [0]

            def link(ins):
                count[0] += 1
                ins.then_inc(chain, 1)
                eng.wait_ge(chain, count[0])

            def signal(ins, s, n):
                ins.then_inc(s, 1)
                eng.wait_ge(s, n)

            def residual(i):
                n, s = tile_rows(i), i % 2
                eng.wait_ge(o_ready, i + 1)
                eng.wait_ge(x_in[s], 16 * (i // 2 + 1))
                for h in range(2):
                    ins = eng.tensor_tensor(y[0:n, s, 512 * h:512 * (h + 1)], y[0:n, s, 512 * h:512 * (h + 1)], ob[h][0:n, :], ALU.add)
                    if h:
                        signal(ins, x1_ready, i + 1)
                    else:
                        link(ins)

            def norm(i):
                n, s = tile_rows(i), i % 2
                eng.wait_ge(x1_rstd, i + 1)
                if i == 0:
                    eng.wait_ge(w2_in, 16)
                signal(eng.scalar_tensor_tensor(out=h2[0:n, s, :], in0=y[0:n, s, :], scalar=rms[0:n, 2:3], in1=w2[0:n, :],
                                                op0=ALU.mult, op1=ALU.mult), h2_ready, i + 1)

            def top16(values, index, x):
                link(eng.max(values[:, 0:8], x))
                link(eng.max_index(index[:, 0:8], values[:, 0:8], x))
                link(eng.match_replace(x, values[:, 0:8], x, LOW))
                link(eng.max(values[:, 8:16], x))
                link(eng.max_index(index[:, 8:16], values[:, 8:16], x))

            def candidates(i, h):
                n, q = tile_rows(i), QUADS * i + h // 2
                eng.wait_ge(sco_ready, q + 1)
                for p in range(2):
                    top16(tv[0:n, p, :], ti[0:n, p, :], sco[0:n, q % 2, 2 * (h % 2) + p, :])
                link(eng.tensor_copy(tif[0:n, :, :], ti[0:n, :, :]))
                link(eng.tensor_tensor(cand[0:n, :, :], tv[0:n, 0, :].unsqueeze(2).to_broadcast([n, TOPK, TOPK]),
                                       tv[0:n, 1, :].unsqueeze(1).to_broadcast([n, TOPK, TOPK]), ALU.add))
                flat = cand[0:n, :, :].rearrange("p a b -> p (a b)")
                top16(cv[0:n, :], ci[0:n, :], flat)
                signal(eng.tensor_scalar(nmx[0:n, :], cv[0:n, 0:1], -1.0, None, ALU.mult), top_ready, PH * i + h + 1)

            def experts(i, h):
                n, s = tile_rows(i), i % 2
                link(eng.tensor_scalar(ca[0:n, 0, :], ci[0:n, :], 4, None, ALU.logical_shift_right))
                link(eng.tensor_scalar(ca[0:n, 1, :], ci[0:n, :], TOPK - 1, None, ALU.bitwise_and))
                link(eng.tensor_copy(caf[0:n, :, :], ca[0:n, :, :]))
                for p in range(2):
                    link(eng.tensor_tensor(eq[0:n, :, :], caf[0:n, p, :].unsqueeze(2).to_broadcast([n, TOPK, TOPK]),
                                           cst[0:n, C_IOTA:C_IOTA + TOPK].unsqueeze(1).to_broadcast([n, TOPK, TOPK]), ALU.is_equal))
                    link(eng.tensor_tensor(eq[0:n, :, :], eq[0:n, :, :], tif[0:n, p, :].unsqueeze(1).to_broadcast([n, TOPK, TOPK]), ALU.mult))
                    link(eng.tensor_reduce(e12[0:n, p, :], eq[0:n, :, :], AX, ALU.add))
                link(eng.scalar_tensor_tensor(out=e12[0:n, 0, :], in0=e12[0:n, 0, :], scalar=float(KEYS), in1=e12[0:n, 1, :], op0=ALU.mult, op1=ALU.add))
                link(eng.tensor_copy(idx[0:n, s, TOPK * h:TOPK * (h + 1)], e12[0:n, 0, :]))
                eng.wait_ge(ex_ready, PH * i + h + 1)
                link(eng.reciprocal(exs[0:n, 1:2], exs[0:n, 0:1]))
                signal(eng.tensor_scalar(gw[0:n, s, TOPK * h:TOPK * (h + 1)], ex[0:n, :], exs[0:n, 1:2], None, ALU.mult), idx_ready, PH * i + h + 1)

            def finish(i):
                n, s = tile_rows(i), i % 2
                eng.wait_ge(v_used, end_of(i))
                for h in range(2):
                    ins = eng.tensor_tensor(y[0:n, s, 512 * h:512 * (h + 1)], y[0:n, s, 512 * h:512 * (h + 1)], acc[h][0:n, :], ALU.add)
                    if h:
                        signal(ins, y_ready, i + 1)
                    else:
                        link(ins)

            residual(0)
            norm(0)
            candidates(0, 0)
            experts(0, 0)
            for t in range(STEPS):
                tile, k = step_no(t)
                if tile == NT and k == 0:
                    eng.wait_ge(h2_rep, 48)
                eng.wait_ge(row_in[t % RING], 16 * (t // RING + 1))
                if t >= 4:
                    eng.wait_ge(gel_ready, t - 3)
                u = ring[:, t % RING, 0:D]
                eng.tensor_tensor_reduce(u, u, h2[:, tile % 2, :], 1.0, 0.0, ALU.mult, ALU.add, dots[:, t % 4:t % 4 + 1]).then_inc(dot_ready, 1)
                if tile and k == 1:
                    finish(tile - 1)
                if tile < NT:
                    if k == SUM_AT:
                        residual(tile + 1)
                    if k == NORM_AT:
                        norm(tile + 1)
                    for i, h in heads_at(tile, k, 3):
                        experts(i, h)
                    for i, h in heads_at(tile, k):
                        candidates(i, h)
            finish(NT)


_IN = ["x_prompt", "x_sample", "cache_kv_g1", "cache_kv_g2", "cache_kv_g3", "state_conv", "norm1_w", "w_in", "q_norm_w", "k_norm_w",
       "conv_w", "conv_b", "conv_ln_g", "conv_ln_b", "w_conv_proj", "w_attn_proj", "w_out", "norm2_w", "w_peer_q", "peer_sub_keys"]
_OUT = [("y_p", (1, SEQ, D)), ("y_s", (NB, NS, D)),
        ("kv0p", (1, 1, 128, 2, HG, HD)), ("kv1p", (1, 1, SEQ, 2, HG, HD)), ("kv2p", (1, 1, SEQ, 2, HG, HD)), ("conv_p", (1, 1, PAD, D)),
        ("kv0s", (1, NB, NS, 2, HG, HD)), ("kv1s", (1, NB, NS, 2, HG, HD)), ("kv2s", (1, NB, NS, 2, HG, HD)), ("conv_s", (1, NB, PAD, D))]


def program(nc, a):
    def scratch(name, shape):
        return nc.dram_tensor("x_" + name, shape, F32, kind="Internal").ap()

    sc = {"attn": [scratch(f"attn{g}", [SEQ, HG * ACCW]) for g in range(NG)],
          "q_smp": [scratch(f"q{g}", [SMP, GW]) for g in range(NG)],
          "gates": scratch("gates", [2 * DC, P, TOK])}
    with ExitStack() as ctx:
        cst = ctx.enter_context(nc.sbuf_tensor("cst", [P, C_W], F32))
        late = {"wo_in": ctx.enter_context(nc.semaphore("wo_in")),
                "wq_in": [ctx.enter_context(nc.semaphore(f"wq_in{i}")) for i in range(2)]}
        with nc.sbuf_tensor("yT", [P, DC, TOK], F32) as yT, nc.sbuf_tensor("hs", [SMP, GW], F32) as hs:
            front(nc, a, sc, cst, yT, a["trig"])
            sample_attention(nc, a, sc, cst, hs)
            with ExitStack() as inner:
                def sb(name, shape):
                    late[name] = inner.enter_context(nc.sbuf_tensor(name, shape, F32))

                sb("mT", [P, DC, TOK])
                sb("wo", [P, DC, D])
                sb("wq", [P, DC, 2 * PH * HALF])
                sb("skT", [P, 2 * PH, KEYS])
                mix(nc, a, sc, cst, yT, hs, late)
                peer(nc, a, cst, late, yT)


def kernel(**inputs):
    import concourse.bacc as _bacc
    from concourse.bass_utils import run_bass_kernel_spmd as _run

    nc = _bacc.Bacc("TRN2", target_bir_lowering=False, num_devices=1)
    arrays = {name: np.ascontiguousarray(inputs[name]) for name in _IN}
    arrays["expert_uv"] = np.concatenate([inputs["expert_u"][0], inputs["expert_v"][0]], axis=1)
    arrays["consts"], arrays["trig"] = shape_constants()
    a = {name: nc.dram_tensor("in_" + name, x.shape, mybir.dt.from_np(x.dtype), kind="ExternalInput").ap() for name, x in arrays.items()}
    a |= {name: nc.dram_tensor("out_" + name, shape, F32, kind="ExternalOutput").ap() for name, shape in _OUT}
    program(nc, a)
    r = _run(nc, [{"in_" + name: x for name, x in arrays.items()}], core_ids=[0])
    return tuple(r.results[0]["out_" + name] for name, _ in _OUT)
```

```python
from contextlib import ExitStack

import numpy as np

import concourse.bass as bass
from concourse import mybir

F32 = mybir.dt.float32
U32 = mybir.dt.uint32
ALU = mybir.AluOpType
ACT = mybir.ActivationFunctionType
AX = mybir.AxisListType.X

P = 128
D = 1024
DC = D // P
SEQ = 512
NT = SEQ // P
NB, NS = 8, 4
SMP = NB * NS
TOK = SEQ + SMP
PAST = 512
HD, HG, NG = 64, 8, 3
GW = HG * HD
AW = NG * GW
TAPS = 31
PAD = TAPS - 1
KEYS, TOPK, PH, HALF = 128, 16, 8, 128
WINDOW_ROWS = (128, 512, 512)
RMS_EPS, LN_EPS = 1e-6, 1e-5
NEG = -1.0e30
QK_SCALE = HD ** -0.5
UPT = NT + 1
ACCW = HD + 2

C_ID, C_ONE, C_PREV, C_DIAG, C_STRIDE = 0, 128, 256, 384, 512
C_HEAD = 640
C_SUM = C_HEAD + HG
C_NEW1 = C_SUM + SMP // 2
C_KEEP = C_NEW1 + NS
C_DROP = C_KEEP + NS
C_BACK = C_DROP + NS
C_IOTA = C_BACK + NS
C_FOLD = C_IOTA + TOPK
C_W = C_FOLD + SMP


def shape_constants():
    c = np.zeros((P, C_W), np.float32)
    p, j = np.arange(P)[:, None], np.arange(P)[None, :]
    c[:, C_ID:C_ID + P] = p == j
    c[:, C_ONE:C_ONE + P] = 1.0
    c[:, C_PREV:C_PREV + P] = np.where(j >= p, 0.0, NEG)
    c[:, C_DIAG:C_DIAG + P] = np.where(j <= p, 0.0, NEG)
    c[:, C_STRIDE:C_STRIDE + P] = np.where((j <= p) & ((p - j) % 4 == 0), 0.0, NEG)
    r = np.arange(P)[:, None]
    c[:, C_HEAD:C_HEAD + HG] = r // NS % HG == np.arange(HG)[None, :]
    j = np.arange(SMP // 2)[None, :]
    c[:, C_SUM:C_SUM + SMP // 2] = (r // (NS * HG) == j // NS) & (r % NS == j % NS)
    s = np.arange(NS)[None, :]
    c[:, C_NEW1:C_NEW1 + NS] = np.where(p < s, NEG, 0.0)
    c[:, C_KEEP:C_KEEP + NS] = p % NS == s
    c[:, C_DROP:C_DROP + NS] = np.where(p % NS == s, 0.0, NEG)
    c[:, C_BACK:C_BACK + NS] = np.where(p % NS < s, NEG, 0.0)
    c[:, C_IOTA:C_IOTA + TOPK] = np.arange(TOPK)[None, :]
    c[:, C_FOLD:C_FOLD + SMP] = p % SMP == np.arange(SMP)[None, :]
    half = HD // 2
    freq = (10000.0 ** (-np.arange(half, dtype=np.float64) / half)).astype(np.float32)
    m = np.arange(P)
    pos = [P * i + m for i in range(NT)] + [NT * m + i for i in range(NT)] + [PAST + m % NS]
    ang = (np.stack(pos).astype(np.float32)[:, :, None] * freq).astype(np.float64)
    trig = np.concatenate([np.cos(ang), -np.sin(ang), np.sin(ang)], axis=2).astype(np.float32)
    return c, np.ascontiguousarray(trig.transpose(1, 0, 2))


def tile_rows(i):
    return P if i < NT else SMP


def order_view(rows, g, i):
    return rows[P * i:P * (i + 1)] if g == 0 else rows.rearrange("(m r) x -> r m x", r=NT)[i]


def front(nc, a, sc, cst, yT, hT, wsb, w_in, qk, S, trig_d):
    GLU, GATES = 4 * UPT, 2 * UPT
    QKV = NG * 3 * UPT
    Q0, G0 = GLU, GLU + QKV
    UNITS = QKV + GLU + GATES
    VEC_IN, ROPE_IN = 4, 3
    VEC = TAPS + 2
    NW = UNITS // UPT
    with ExitStack() as ctx:
        def sb(name, shape, dt=F32):
            return ctx.enter_context(nc.sbuf_tensor("f_" + name, shape, dt))

        def ps(name, shape):
            return ctx.enter_context(nc.psum_tensor("f_" + name, shape, F32))

        def sem(name):
            return ctx.enter_context(nc.semaphore("f_" + name))

        trig = sb("trig", [P, 9, 96])
        qkw = sb("qkw", [P, 2, HD])
        rc = sb("rc", [P, 2, 9, HD])
        rs = sb("rs", [P, 2, 9, HD])
        xss = sb("xss", [P, UPT, 3])
        half_m = sb("half_m", [P, HG])
        sq = sb("sq", [P, 512])
        ss = sb("ss", [P, 2, HG])
        qn = sb("qn", [P, 512])
        t1 = sb("t1", [P, 512])
        t2 = sb("t2", [P, 512])
        qkr = sb("qkr", [P, 3, 512])
        qT, kT = qk[:, :, 0], qk[:, :, 1]
        vsb = sb("v", [P, 2, UPT, GW])
        s_sb = sb("s", [P, 4, 512])
        pt = sb("pt", [P, 4, 512])
        nm = sb("nm", [P, 4, 4])
        st = sb("st", [P, 4, 4, ACCW])
        uT = sb("uT", [P, DC, PAD + SEQ])
        uS = sb("uS", [P, DC, NB, PAD + NS])
        sg = sb("sg", [P, 2, 512])
        gst = sb("gst", [P, 2, 512])
        vec = sb("vec", [P, DC, VEC])
        cw, cb, n1 = vec[:, :, 0:TAPS], vec[:, :, TAPS], vec[:, :, TAPS + 1]
        rows33 = gst[0:VEC, :, :].rearrange("p a b -> p (a b)")

        qk_rows = qk[:, :, :, :, :].rearrange("p a b c t -> p (a b c t)").rearrange("p (s d) -> p s d", d=D)
        xt, cin, state_rows = qk_rows[:, 0:UPT], qk_rows[:, UPT:UPT + 2], qk_rows[:, 4:6]
        ht = pt[:, :, :].rearrange("p (s a) b -> p s (a b)", s=2)
        squares = s_sb[:, 0:2, :].rearrange("p a b -> p (a b)")

        zp = [ps("z0", [P, 512]), ps("z1", [P, 512])]
        ap_ = [ps("a0", [P, 512]), ps("a1", [P, 512])]
        tp = ps("t", [P, 512])
        pp = ps("p", [P, 2, 512])
        op = ps("o", [P, 512])
        ident = cst[:, C_ID:C_ID + P]

        vec_in = sem("vec_in")
        rope_in = sem("rope_in")
        x_in = [sem("x_in0"), sem("x_in1")]
        sq_done = sem("sq_done")
        x_var = sem("x_var")
        h_ready = sem("h_ready")
        hp_ready = sem("hp_ready")
        hT_ready = sem("hT_ready")
        half_ready = sem("half_ready")
        chain = sem("chain")
        z_ready = sem("z_ready")
        z_free_v = sem("z_free_v")
        z_free_a = sem("z_free_a")
        z_sq = sem("z_sq")
        z_ss = sem("z_ss")
        z_rstd = sem("z_rstd")
        r_ready = sem("r_ready")
        r_out = [sem(f"r_out{i}") for i in range(3)]
        tr_ready = sem("tr_ready")
        tr_out = sem("tr_out")
        v_ready = sem("v_ready")
        v_out = [sem("v_out0"), sem("v_out1")]
        s_ready = sem("s_ready")
        m_ready = sem("m_ready")
        e_ready = sem("e_ready")
        p_ready = sem("p_ready")
        pt_ready = sem("pt_ready")
        o_ready = sem("o_ready")
        st_ready = sem("st_ready")
        st_out = [sem(f"st_out{i}") for i in range(4)]
        sg_ready = sem("sg_ready")
        u_ready = sem("u_ready")
        g_ready = sem("g_ready")
        g_out = [sem("g_out0"), sem("g_out1")]
        cin_in = sem("cin_in")
        cp_ready = sem("cp_ready")
        cs_ready = sem("cs_ready")
        u_zero = sem("u_zero")
        conv_done = sem("conv_done")
        so_ready = sem("so_ready")
        sc_ready = sem("sc_ready")
        so_out = [sem("so_out0"), sem("so_out1")]
        c_in = sem("c_in")
        c_prod = sem("c_prod")
        c_used = sem("c_used")

        st4 = kT[:, 1, :, :].rearrange("p a b -> p (a b)")[:, 0:DC * NB * PAD].rearrange("p (c b r) -> p c b r", c=DC, b=NB)
        w_v = a["w_in"][0].rearrange("(k p) c -> p k c", p=P)

        def w_cols(m):
            if m < 4:
                base = 3 * AW + 256 * m
                return [(base + D, 256, 0), (base, 256, 256)]
            if m < 13:
                g, c = divmod(m - 4, 3)
                return [(c * AW + g * GW, 512, 0)]
            return [(3 * AW + 2 * D + 512 * (m - 13), 512, 0)]

        def w_count(m):
            return 16 * sum(len(w_cols(j)) for j in range(m % 2, m + 1, 2))

        def unit(n):
            m, i = divmod(n, UPT)
            return m, (m - 4) // 3, (m - 4) % 3, i

        def freed_by_scalar(n):
            if n < Q0:
                return n % UPT in (0, 1)
            return n >= G0

        def z_of(n):
            return (zp + ap_)[n % 4] if n < Q0 + 15 else zp[n % 2]

        def wait_bank(eng, n):
            before = [j for j in range(n) if z_of(j) is z_of(n)]
            if before:
                wait_read(eng, before[-1])

        def wait_read(eng, n):
            k = sum(freed_by_scalar(j) == freed_by_scalar(n) for j in range(n + 1))
            eng.wait_ge(z_free_a if freed_by_scalar(n) else z_free_v, k)

        qk_units = [n for n in range(Q0, G0) if unit(n)[2] < 2]
        tr_units = [n for n in qk_units if unit(n)[3] < NT]

        def stored(n):
            m, g, c, i = unit(n)
            return i == NT or (c == 1 and (g > 0 or i == NT - 1))

        def r_out_count(e):
            return 16 * sum(stored(qk_units[j]) for j in range(e % 3, e + 1, 3))

        def sub_batches(g, s):
            i, par = divmod(s, 2)
            heads = [par + 2 * j for j in range(4)]
            keys = [i - 1, i] if g == 0 and i else [i]
            return [(heads[:2], keys), (heads[2:], keys)] if g == 0 else [(heads, keys)]

        subs = [(g, s, b) for g in range(NG) for s in range(8) for b in range(len(sub_batches(g, s)))]
        sub_no = {k: q for q, k in enumerate(subs)}

        def attention_steps(n):
            g = (n - Q0) // 15 - 1
            if g < 0 or g >= NG:
                return None
            s = n - Q0 - 15 * (g + 1)
            return g, (s if s < 8 else None), (s - 1 if 1 <= s < 9 else None), (s - 2 if 2 <= s < 10 else None)

        CONV = 2 * DC * TAPS
        def conv_steps(n):
            if n < 2 * UPT:
                return 0
            if n < Q0:
                return 14
            if n >= G0:
                return 10
            g, c = unit(n)[1:3]
            return ((6, 6, 14), (0, 1, 14), (3, 3, 10))[g][c]

        CONV_AT = [min(CONV if n >= Q0 else CONV // 2, sum(map(conv_steps, range(n + 1)))) for n in range(UNITS)]
        assert CONV_AT[-1] == CONV

        def turn_bank(i, h):
            return pp[:, h, :] if i % 2 else ap_[h]

        STATE_AT = [Q0 + 1 + 2 * j for j in range(3)]
        K0 = Q0 + 2 * 15 + 10
        SCORE_AT = [K0 + 1 + (UNITS - K0 - 3) * b // (NB - 1) for b in range(NB)]
        k2, q2 = (x[:, 1, :, :] for x in (kT, qT))

        block = ctx.enter_context(nc.Block())

        @block.sync
        def _(eng):
            def load_cache(b):
                if b:
                    eng.wait_ge(c_used, b)
                else:
                    eng.wait_ge(s_ready, sub_no[1, 7, len(sub_batches(1, 7)) - 1] + 1)
                    e = qk_units.index(Q0 + 15 + NT)
                    eng.wait_ge(r_out[e % 3], r_out_count(e))
                eng.dma_start(k2, a["cache_kv_g2"][0, b].rearrange("l w h e -> l w (h e)")[:, 0, :].rearrange("(m r) x -> m r x", r=NS)).then_inc(c_in, 16)
                eng.dma_start(q2, sc["q_smp"][1][NS * b:NS * (b + 1), :].unsqueeze(0).to_broadcast([P, NS, GW])).then_inc(c_in, 16)

            def load_x(i):
                src = a["x_prompt"][0, P * i:P * (i + 1), :] if i < NT else a["x_sample"].rearrange("b s d -> (b s) d")
                eng.dma_start(xt[0:tile_rows(i), i, :], src).then_inc(x_in[i > 0], 16)

            def load_weights(m):
                for col, width, at in w_cols(m):
                    eng.dma_start(wsb[:, m % 2, :, at:at + width], w_v[:, :, col:col + width]).then_inc(w_in[m % 2], 16)

            load_x(0)
            eng.dma_start(rows33[0:TAPS, :], a["conv_w"][0]).then_inc(vec_in, 16)
            eng.dma_start(rows33[TAPS:TAPS + 1, :], a["conv_b"]).then_inc(vec_in, 16)
            eng.dma_start(rows33[TAPS + 1:TAPS + 2, :], a["norm1_w"]).then_inc(vec_in, 16)
            eng.dma_start(cst[:, :], a["consts"]).then_inc(vec_in, 16)
            for i in range(1, UPT):
                load_x(i)
            load_weights(0)
            eng.dma_start(trig[:, :, :], trig_d).then_inc(rope_in, 16)
            eng.dma_start(qkw[:, 0, :], a["q_norm_w"].to_broadcast([P, HD])).then_inc(rope_in, 16)
            eng.dma_start(qkw[:, 1, :], a["k_norm_w"].to_broadcast([P, HD])).then_inc(rope_in, 16)
            load_weights(1)
            for m in range(2, NW + 2):
                for b in range(NB):
                    if SCORE_AT[b] - 1 in range(UPT * (m - 2), UPT * (m - 1)):
                        load_cache(b)
                eng.wait_ge(z_ready, UPT * (m - 1))
                load_weights(m)

        @block.gpsimd
        def _(eng):
            eng.memset(half_m[:, :], -0.5).then_inc(half_ready, 1)
            eng.memset(uT[:, :, 0:PAD], 0.0).then_inc(u_zero, 1)
            eng.wait_ge(half_ready, 1)
            for i in range(UPT):
                n = tile_rows(i)
                eng.wait_ge(sq_done, i + 1)
                eng.tensor_scalar(xss[0:n, i, 1:2], xss[0:n, i, 0:1], 1.0 / D, RMS_EPS, ALU.mult, ALU.add).then_inc(half_ready, 1)
                eng.wait_ge(half_ready, 2 + i)
                eng.tensor_tensor(xss[0:n, i, 2:3], xss[0:n, i, 1:2], half_m[0:n, 0:1], ALU.pow).then_inc(x_var, 1)
                if i < 2:
                    eng.dma_start(cin[0:4 * PAD, i, :], a["state_conv"][0, 4 * i:4 * i + 4].rearrange("b r d -> (b r) d")).then_inc(cin_in, 16)
            own = 1 + UPT
            e = v = 0
            for n in range(Q0, UNITS):
                m, g, c, i = unit(n)
                rows = tile_rows(i)
                if n >= G0:
                    t = n - G0
                    eng.wait_ge(g_ready, t + 1)
                    gm = t // UPT
                    if i < NT:
                        eng.dma_start(sc["gates"][4 * gm + i][:, 0:SEQ], gst[:, t % 2, :]).then_inc(g_out[t % 2], 16)
                    else:
                        eng.dma_start(sc["gates"][4 * gm:4 * gm + 4][:, :, SEQ:TOK].rearrange("c p t -> p c t"),
                                      gst[:, t % 2, 0:4 * SMP].rearrange("p (c t) -> p c t", c=4)).then_inc(g_out[t % 2], 16)
                elif c < 2:
                    eng.wait_ge(z_ss, e + 1)
                    eng.tensor_scalar(ss[0:rows, 1, :], ss[0:rows, 0, :], 1.0 / HD, RMS_EPS, ALU.mult, ALU.add).then_inc(half_ready, 1)
                    own += 1
                    eng.wait_ge(half_ready, own)
                    eng.tensor_tensor(ss[0:rows, 1, :], ss[0:rows, 1, :], half_m[0:rows, :], ALU.pow).then_inc(z_rstd, 1)
                    eng.wait_ge(z_rstd, e + 1)
                    if stored(n):
                        eng.wait_ge(r_ready, e + 1)
                        src = qkr[0:rows, e % 3, :]
                        if i < NT:
                            dst = a[f"kv{g}p"][0, 0].rearrange("t w h e -> t w (h e)")[:, 0, :]
                            dst = dst if g == 0 else order_view(dst, g, i)
                        elif c == 0:
                            dst = sc["q_smp"][g]
                        else:
                            dst = a[f"kv{g}s"][0].rearrange("b s w h e -> (b s) w (h e)")[:, 0, :]
                        eng.dma_start(dst, src).then_inc(r_out[e % 3], 16)
                    e += 1
                else:
                    if g > 0 or i >= NT - 1:
                        eng.wait_ge(v_ready, v + 1)
                        src = vsb[0:rows, g % 2, i, :]
                        if i < NT:
                            dst = a[f"kv{g}p"][0, 0].rearrange("t w h e -> t w (h e)")[:, 1, :]
                            dst = dst if g == 0 else order_view(dst, g, i)
                        else:
                            dst = a[f"kv{g}s"][0].rearrange("b s w h e -> (b s) w (h e)")[:, 1, :]
                        eng.dma_start(dst, src).then_inc(v_out[g % 2], 16)
                    v += 1
                steps = attention_steps(n)
                if steps and steps[3] is not None:
                    g, s = steps[0], steps[3]
                    o = 8 * g + s
                    eng.wait_ge(st_ready, o + 1)
                    dst = order_view(sc["attn"][g][:, (s % 2) * 4 * ACCW:(s % 2 + 1) * 4 * ACCW], g, s // 2)
                    eng.dma_start(dst, st[:, o % 4, :, :].rearrange("p h w -> p (h w)")).then_inc(st_out[o % 4], 16)
                if n in STATE_AT:
                    j = STATE_AT.index(n)
                    eng.wait_ge(sc_ready, 2 * j + 2)
                    if j == 0:
                        eng.dma_start(a["conv_p"][0, 0], state_rows[0:PAD, 0, :]).then_inc(so_out[0], 16)
                    else:
                        eng.dma_start(a["conv_s"][0, 4 * j - 4:4 * j].rearrange("b r d -> (b r) d"), state_rows[0:4 * PAD, j % 2, :]).then_inc(so_out[j % 2], 16)
                if n in SCORE_AT:
                    b = SCORE_AT.index(n)
                    eng.wait_ge(c_in, 32 * (b + 1))
                    eng.tensor_tensor(q2, k2, q2, ALU.mult).then_inc(c_prod, 1)
            eng.wait_ge(so_out[0], 32)
            eng.wait_ge(so_out[1], 16)
            for j in range(2):
                eng.wait_ge(g_out[j], 16 * GATES // 2)
                eng.wait_ge(v_out[j], 16 * sum(2 if g == 0 else UPT for g in range(j, NG, 2)))
            for j in range(3):
                eng.wait_ge(r_out[j], r_out_count(len(qk_units) - 3 + j))
            for j in range(4):
                eng.wait_ge(st_out[j], 16 * 6)

        @block.tensor
        def _(eng):
            eng.wait_ge(vec_in, 16 * VEC_IN)
            for c in range(DC):
                mm = eng.transpose(pp[:, c // 4, (c % 4) * P:(c % 4) * P + VEC], rows33[:, c * P:(c + 1) * P], cst[0:VEC, C_ID:C_ID + VEC])
            mm.then_inc(cp_ready, 1)
            for i in range(UPT):
                n = tile_rows(i)
                eng.wait_ge(h_ready, i + 1)
                if i == 1:
                    eng.wait_ge(cs_ready, 1)
                elif i:
                    eng.wait_ge(hT_ready, i - 1)
                for c in range(DC):
                    mm = eng.transpose(turn_bank(i, c // 4)[:, (c % 4) * P:(c % 4) * P + n], ht[0:n, i % 2, c * P:(c + 1) * P], cst[0:n, C_ID:C_ID + n])
                mm.then_inc(hp_ready, 1)
            eng.wait_ge(hT_ready, UPT)
            t = 0
            o = 0
            for n in range(UNITS):
                m, g, c, i = unit(n)
                if i == 0:
                    eng.wait_ge(w_in[m % 2], w_count(m))
                wait_bank(eng, n)
                z = z_of(n)
                if Q0 <= n < G0:
                    for k in range(DC):
                        tok = hT[:, k, SEQ:TOK] if i == NT else hT[:, k, P * i:P * (i + 1)] if g == 0 else hT[:, k, i:SEQ:NT]
                        mm = eng.matmul(z[0:tile_rows(i), :], tok, wsb[:, m % 2, k, :], start=(k == 0), stop=(k == DC - 1))
                elif i < NT:
                    col = i * P
                    for k in range(DC):
                        mm = eng.matmul(z[:, :], wsb[:, m % 2, k, col:col + P], hT[:, k, 0:SEQ], start=(k == 0), stop=(k == DC - 1))
                else:
                    for j in range(4):
                        for k in range(DC):
                            mm = eng.matmul(z[:, SMP * j:SMP * (j + 1)], wsb[:, m % 2, k, P * j:P * (j + 1)], hT[:, k, SEQ:TOK],
                                            start=(k == 0), stop=(k == DC - 1))
                mm.then_inc(z_ready, 1)
                if n < 2:
                    eng.wait_ge(cin_in, 32)
                    if n:
                        eng.wait_ge(cs_ready, 2)
                    for j in range(DC):
                        mm = eng.transpose(pp[:, j // 4, (j % 4) * P:(j % 4) * P + 4 * PAD], cin[0:4 * PAD, n, j * P:(j + 1) * P],
                                           cst[0:4 * PAD, C_ID:C_ID + 4 * PAD])
                    mm.then_inc(cp_ready, 1)
                if n - 1 in tr_units:
                    e = qk_units.index(n - 1)
                    eng.wait_ge(r_ready, e + 1)
                    if t:
                        eng.wait_ge(tr_out, t)
                    for j in range(4):
                        mm = eng.transpose(tp[:, P * j:P * (j + 1)], qkr[:, e % 3, P * j:P * (j + 1)], ident)
                    mm.then_inc(tr_ready, 1)
                    t += 1
                steps = attention_steps(n)
                if steps:
                    ga, s_, t_, o_ = steps
                    if s_ is not None:
                        ia = s_ // 2
                        eng.wait_ge(tr_out, 8 * (ga + 1))
                        for b, (heads, keys) in enumerate(sub_batches(ga, s_)):
                            q = sub_no[ga, s_, b]
                            if q >= 2:
                                eng.wait_ge(m_ready, q - 1)
                            else:
                                wait_read(eng, max(j for j in range(UNITS) if z_of(j) is ap_[q]))
                            nk = len(keys)
                            for j, h in enumerate(heads):
                                r = (h % 2) * HD
                                mm = eng.matmul(ap_[q % 2][:, j * nk * P:(j + 1) * nk * P], qT[r:r + HD, ga % 2, h // 2, P * ia:P * (ia + 1)],
                                                kT[r:r + HD, ga % 2, h // 2, P * keys[0]:P * (keys[-1] + 1)], start=True, stop=True)
                            mm.then_inc(s_ready, 1)
                    if t_ is not None:
                        for b, (heads, keys) in enumerate(sub_batches(ga, t_)):
                            q = sub_no[ga, t_, b]
                            eng.wait_ge(e_ready, q + 1)
                            if q >= 2:
                                eng.wait_ge(pt_ready, q - 1)
                            elif q == 0:
                                eng.wait_ge(sc_ready, 6)
                            for j in range(len(heads) * len(keys)):
                                mm = eng.transpose(pp[:, q % 2, P * j:P * (j + 1)], s_sb[:, q % 4, P * j:P * (j + 1)], ident)
                            mm.then_inc(p_ready, 1)
                    if o_ is not None:
                        if o:
                            eng.wait_ge(st_ready, o)
                        eng.wait_ge(v_ready, UPT * (ga + 1))
                        for b, (heads, keys) in enumerate(sub_batches(ga, o_)):
                            q = sub_no[ga, o_, b]
                            eng.wait_ge(pt_ready, q + 1)
                            nk = len(keys)
                            for j, h in enumerate(heads):
                                at = (b * len(heads) + j) * HD
                                for x, key in enumerate(keys):
                                    mm = eng.matmul(op[:, at:at + HD], pt[:, q % 4, (j * nk + x) * P:(j * nk + x + 1) * P],
                                                    vsb[:, ga % 2, key, h * HD:(h + 1) * HD], start=(x == 0), stop=(x == nk - 1))
                        mm.then_inc(o_ready, 1)
                        o += 1
                if n in STATE_AT:
                    j = STATE_AT.index(n)
                    eng.wait_ge(u_ready, 3 * 4 + 1)
                    eng.wait_ge(*((sc_ready, 2 * j) if j else (cs_ready, 3)))
                    for c in range(DC):
                        src = uT[:, c, SEQ:SEQ + PAD] if j == 0 else st4[:, c, 4 * j - 4:4 * j, :].rearrange("p b r -> p (b r)")
                        mm = eng.transpose(pp[0:PAD if j == 0 else 4 * PAD, c // 4, (c % 4) * P:(c % 4 + 1) * P], src, ident)
                    mm.then_inc(so_ready, 1)

        @block.scalar
        def _(eng):
            for i in range(UPT):
                n = tile_rows(i)
                eng.wait_ge(x_in[i > 0], 16 * NT if i else 16)
                if i:
                    eng.wait_ge(sq_done, i)
                eng.activation(squares[0:n, :], xt[0:n, i, :], ACT.Square, accum_out=xss[0:n, i, 0:1]).then_inc(sq_done, 1)
            t = e = 0
            for n in range(UNITS):
                m, g, c, i = unit(n)
                rows = tile_rows(i)
                if Q0 <= n < G0 and c < 2:
                    eng.wait_ge(z_ready, n + 1)
                    if e:
                        eng.wait_ge(z_ss, e)
                    eng.activation(sq[0:rows, :], z_of(n)[0:rows, :], ACT.Square).then_inc(z_sq, 1)
                    e += 1
                elif n < Q0:
                    k = n // UPT
                    if i < 2:
                        eng.wait_ge(z_ready, n + 1)
                        if k:
                            eng.wait_ge(u_ready, 3 * k)
                        eng.activation(sg[:, i, :], z_of(n)[:, :], ACT.Sigmoid).then_inc(z_free_a, 1)
                    elif i == NT:
                        eng.wait_ge(z_ready, n + 1)
                        eng.wait_ge(u_ready, 3 * k + 2)
                        eng.activation(sg[:, 0, 0:2 * SMP], z_of(n)[:, 0:2 * SMP], ACT.Sigmoid).then_inc(sg_ready, 1)
                elif n >= G0:
                    k = n - G0
                    w = 512 if i < NT else 4 * SMP
                    eng.wait_ge(z_ready, n + 1)
                    if k >= 2:
                        eng.wait_ge(g_out[k % 2], 16 * (k // 2))
                        eng.wait_ge(g_ready, k - 1)
                    eng.activation(gst[:, k % 2, 0:w], z_of(n)[:, 0:w], ACT.Sigmoid).then_inc(g_ready, 1)
                    eng.wait_ge(g_ready, k + 1)
                    eng.sem_inc(z_free_a, 1)
                if n - 1 in tr_units:
                    gt, ct, it = unit(n - 1)[1:]
                    eng.wait_ge(tr_ready, t + 1)
                    dst = (qT if ct == 0 else kT)[:, gt % 2, :, P * it:P * (it + 1)]
                    if gt == 1 and ct == 0 and it == 0:
                        eng.wait_ge(so_out[0], 32)
                        eng.wait_ge(so_out[1], 16)
                    if gt >= 2:
                        eng.wait_ge(s_ready, sub_no[gt - 2, 7, len(sub_batches(gt - 2, 7)) - 1] + 1)
                    eng.activation(dst, tp[:, :].rearrange("p (a b) -> p a b", a=4), ACT.Copy).then_inc(tr_out, 1)
                    t += 1
                steps = attention_steps(n)
                if steps:
                    ga, s_, t_, o_ = steps
                    if t_ is not None:
                        for b, (heads, keys) in enumerate(sub_batches(ga, t_)):
                            q = sub_no[ga, t_, b]
                            w = P * len(heads) * len(keys)
                            eng.wait_ge(p_ready, q + 1)
                            if ga * 8 + t_ >= 2:
                                eng.wait_ge(o_ready, ga * 8 + t_ - 1)
                            eng.activation(pt[:, q % 4, 0:w], pp[:, q % 2, 0:w], ACT.Copy).then_inc(pt_ready, 1)
                    if s_ is not None:
                        for b, (heads, keys) in enumerate(sub_batches(ga, s_)):
                            q = sub_no[ga, s_, b]
                            slot = (8 * ga + s_) % 4
                            w = P * len(keys)
                            eng.wait_ge(m_ready, q + 1)
                            for j in range(len(heads)):
                                ins = eng.activation(s_sb[:, q % 4, j * w:(j + 1) * w], s_sb[:, q % 4, j * w:(j + 1) * w], ACT.Exp,
                                                     bias=nm[:, q % 4, j:j + 1], accum_out=st[:, slot, b * len(heads) + j, HD + 1:HD + 2])
                            ins.then_inc(e_ready, 1)
                if n in STATE_AT:
                    j = STATE_AT.index(n)
                    w = PAD if j == 0 else 4 * PAD
                    eng.wait_ge(so_ready, j + 1)
                    if j == 2:
                        eng.wait_ge(so_out[0], 16)
                    for b in range(2):
                        eng.activation(state_rows[0:w, j % 2, 512 * b:512 * (b + 1)], pp[0:w, b, :], ACT.Copy).then_inc(sc_ready, 1)

        @block.vector
        def _(eng):
            count = {"chain": 0}

            def link(ins):
                count["chain"] += 1
                ins.then_inc(chain, 1)
                eng.wait_ge(chain, count["chain"])

            def signal(ins, s, n):
                ins.then_inc(s, 1)
                eng.wait_ge(s, n)

            def rotary_tables():
                eng.wait_ge(rope_in, 16 * ROPE_IN)
                for w in range(2):
                    lo, hi = (qkw[:, w, x:x + 32].unsqueeze(1).to_broadcast([P, 9, 32]) for x in (0, 32))
                    link(eng.tensor_tensor(rc[:, w, :, 0:32], trig[:, :, 0:32], lo, ALU.mult))
                    link(eng.tensor_tensor(rc[:, w, :, 32:64], trig[:, :, 0:32], hi, ALU.mult))
                    link(eng.tensor_tensor(rs[:, w, :, 0:32], trig[:, :, 32:64], hi, ALU.mult))
                    link(eng.tensor_tensor(rs[:, w, :, 32:64], trig[:, :, 64:96], lo, ALU.mult))

            def keep_conv_rows(j):
                eng.wait_ge(cp_ready, j + 2)
                for c2 in range(2):
                    src = pp[:, c2, :].rearrange("p (c x) -> p c x", c=4)[:, :, 0:4 * PAD]
                    for c in range(4):
                        ins = eng.tensor_copy(uS[:, 4 * c2 + c, 4 * j:4 * j + 4, 0:PAD], src[:, c, :].rearrange("p (b r) -> p b r", b=4))
                        if c2 == 1 and c == 3:
                            signal(ins, cs_ready, j + 2)
                        else:
                            link(ins)

            def normalise(i):
                n = tile_rows(i)
                eng.wait_ge(x_var, i + 1)
                if i >= 2:
                    eng.wait_ge(hp_ready, i - 1)
                eng.tensor_scalar(ht[0:n, i % 2, :], xt[0:n, i, :], xss[0:n, i, 2:3], None, ALU.mult).then_inc(h_ready, 1)

            eng.wait_ge(cp_ready, 1)
            for b in range(2):
                ins = eng.tensor_copy(vec[:, 4 * b:4 * b + 4, :], pp[:, b, :].rearrange("p (c x) -> p c x", c=4)[:, :, 0:VEC])
                if b:
                    signal(ins, cs_ready, 1)
                else:
                    link(ins)
            normalise(0)
            for i in range(UPT):
                if i + 1 < UPT:
                    normalise(i + 1)
                n = tile_rows(i)
                eng.wait_ge(hp_ready, i + 1)
                for b in range(2):
                    ins = eng.tensor_tensor(hT[:, 4 * b:4 * b + 4, P * i:P * i + n], turn_bank(i, b)[:, :].rearrange("p (c x) -> p c x", c=4)[:, :, 0:n],
                                            n1[:, 4 * b:4 * b + 4].unsqueeze(2).to_broadcast([P, 4, n]), ALU.mult)
                ins.then_inc(hT_ready, 1)
            done = [0]

            def conv_upto(last):
                for step in range(done[0], last):
                    half, rest = divmod(step, 8 * TAPS)
                    tap, (c, smp) = rest // 8, divmod(rest % 8, 2)
                    c += 4 * half
                    if smp:
                        out, src = yT[:, c, SEQ:TOK].rearrange("p (b s) -> p b s", b=NB), uS[:, c, :, tap:tap + NS]
                    else:
                        out, src = yT[:, c, 0:SEQ], uT[:, c, tap:tap + SEQ]
                    if tap:
                        eng.wait_ge(conv_done, step - 7)
                        ins = eng.scalar_tensor_tensor(out=out, in0=src, scalar=cw[:, c, tap:tap + 1], in1=out, op0=ALU.mult, op1=ALU.add)
                    else:
                        ins = eng.tensor_scalar(out, src, cw[:, c, 0:1], cb[:, c:c + 1], ALU.mult, ALU.add)
                    ins.then_inc(conv_done, 1)
                done[0] = max(done[0], last)

            def mask_scores(ga, s_):
                for b, (heads, keys) in enumerate(sub_batches(ga, s_)):
                    q = sub_no[ga, s_, b]
                    so = 8 * ga + s_
                    nh, w = len(heads), P * len(keys)
                    mask = cst[:, C_STRIDE:C_STRIDE + P] if ga == 2 else cst[:, C_DIAG + P - w:C_DIAG + P]
                    eng.wait_ge(s_ready, q + 1)
                    if q >= 4:
                        eng.wait_ge(p_ready, q - 3)
                    if so >= 4:
                        eng.wait_ge(st_out[so % 4], 16 * (so // 4))
                    sv = s_sb[:, q % 4, 0:nh * w].rearrange("p (h k) -> p h k", h=nh)
                    link(eng.scalar_tensor_tensor(out=sv, in0=ap_[q % 2][:, 0:nh * w].rearrange("p (h k) -> p h k", h=nh), scalar=QK_SCALE,
                                                  in1=mask.unsqueeze(1).to_broadcast([P, nh, w]), op0=ALU.mult, op1=ALU.add))
                    mx = st[:, so % 4, b * nh:(b + 1) * nh, HD:HD + 1]
                    link(eng.tensor_reduce(mx, sv, AX, ALU.max))
                    signal(eng.tensor_scalar(nm[:, q % 4, 0:nh], mx.rearrange("p h o -> p (h o)"), -1.0, None, ALU.mult), m_ready, q + 1)

            eng.wait_ge(u_zero, 1)
            e = v = u = o = fv = 0
            for n in range(UNITS):
                m, g, c, i = unit(n)
                rows = tile_rows(i)
                z = z_of(n)
                steps = attention_steps(n)
                slot = steps[:2] if steps and steps[1] is not None else None
                if n < G0:
                    eng.wait_ge(z_ready, n + 1)
                if Q0 <= n < G0 and c < 2:
                    table = 8 if i == NT else i if g == 0 else NT + i
                    eng.wait_ge(z_sq, e + 1)
                    signal(eng.tensor_reduce(ss[0:rows, 0, :], sq[0:rows, :].rearrange("p (h d) -> p h d", h=HG), AX, ALU.add), z_ss, e + 1)
                    if slot is not None:
                        mask_scores(*slot)
                    eng.wait_ge(z_rstd, e + 1)
                    fv += 1
                    signal(eng.tensor_tensor(qn[0:rows, :].rearrange("p (h d) -> p h d", h=HG), z[0:rows, :].rearrange("p (h d) -> p h d", h=HG),
                                             ss[0:rows, 1, :].unsqueeze(2).to_broadcast([rows, HG, HD]), ALU.mult), z_free_v, fv)
                    x = qn[0:rows, :].rearrange("p (h w d) -> p h w d", h=HG, w=2)
                    y = t2[0:rows, :].rearrange("p (h w d) -> p h w d", h=HG, w=2)
                    link(eng.tensor_tensor(t1[0:rows, :].rearrange("p (h d) -> p h d", h=HG), qn[0:rows, :].rearrange("p (h d) -> p h d", h=HG),
                                           rc[0:rows, c, table, :].unsqueeze(1).to_broadcast([rows, HG, HD]), ALU.mult))
                    for w in range(2):
                        link(eng.tensor_tensor(y[:, :, w, :], x[:, :, 1 - w, :],
                                               rs[0:rows, c, table, 32 * w:32 * w + 32].unsqueeze(1).to_broadcast([rows, HG, 32]), ALU.mult))
                    if e >= 3:
                        eng.wait_ge(tr_ready, sum(j in tr_units for j in qk_units[:e - 2]))
                        if r_out_count(e - 3):
                            eng.wait_ge(r_out[e % 3], r_out_count(e - 3))
                    e += 1
                    signal(eng.tensor_tensor(qkr[0:rows, (e - 1) % 3, :], t1[0:rows, :], t2[0:rows, :], ALU.add), r_ready, e)
                elif Q0 <= n < G0:
                    if g >= 2:
                        eng.wait_ge(o_ready, 8 * (g - 1))
                        eng.wait_ge(v_out[g % 2], 16 * 2)
                    v += 1
                    ins = eng.tensor_copy(vsb[0:rows, g % 2, i, :], z[0:rows, :])
                    signal(ins, v_ready, v)
                    fv += 1
                    eng.sem_inc(z_free_v, 1)
                elif n < Q0:
                    k = n // UPT
                    if i in (2, 3):
                        ch = 2 * k + i - 2
                        eng.wait_ge(z_free_a, 2 * k + i - 1)
                        u += 1
                        signal(eng.tensor_tensor(uT[:, ch, PAD:PAD + SEQ], z[:, :], sg[:, i - 2, :], ALU.mult), u_ready, u)
                        fv += 1
                        eng.sem_inc(z_free_v, 1)
                    elif i == NT:
                        eng.wait_ge(sg_ready, k + 1)
                        u += 1
                        for ch in range(2):
                            ins = eng.tensor_tensor(uS[:, 2 * k + ch, :, PAD:PAD + NS], z[:, (2 + ch) * SMP:(3 + ch) * SMP].rearrange("p (b s) -> p b s", b=NB),
                                                    sg[:, 0, ch * SMP:(ch + 1) * SMP].rearrange("p (b s) -> p b s", b=NB), ALU.mult)
                            if ch == 0:
                                link(ins)
                        signal(ins, u_ready, u)
                        fv += 1
                        eng.sem_inc(z_free_v, 1)
                if n < 2:
                    keep_conv_rows(n)
                if n == 2:
                    rotary_tables()
                if n == Q0:
                    for ch in range(DC):
                        ins = eng.tensor_copy(st4[:, ch, :, :], uS[:, ch, :, NS:NS + PAD])
                        if ch < DC - 1:
                            link(ins)
                    u += 1
                    signal(ins, u_ready, u)
                if slot is not None and not (Q0 <= n < G0 and c < 2):
                    mask_scores(*slot)
                conv_upto(CONV_AT[n])
                steps = attention_steps(n)
                if steps:
                    ga, s_, t_, o_ = steps
                    if o_ is not None:
                        eng.wait_ge(o_ready, o + 1)
                        eng.wait_ge(e_ready, sub_no[ga, o_, len(sub_batches(ga, o_)) - 1] + 1)
                        signal(eng.tensor_copy(st[:, o % 4, :, 0:HD], op[:, 0:4 * HD].rearrange("p (h d) -> p h d", h=4)), st_ready, o + 1)
                        o += 1
                if n in SCORE_AT:
                    b = SCORE_AT.index(n)
                    eng.wait_ge(c_prod, b + 1)
                    signal(eng.tensor_reduce(S[:, 1, :, NS * b:NS * (b + 1)].rearrange("p h s -> p s h"), q2.rearrange("p s (h e) -> p s h e", h=HG), AX, ALU.add),
                           c_used, b + 1)
            eng.wait_ge(conv_done, CONV)
    return (w_in[NW % 2], w_count(NW)), (w_in[(NW + 1) % 2], w_count(NW + 1)), NW % 2


def middle(nc, a, sc, cst, yT, hT, mT, wring, w_in, qk, S, late):
    with ExitStack() as ctx:
        def sb(name, shape, dt=F32):
            return ctx.enter_context(nc.sbuf_tensor("m_" + name, shape, dt))

        def sem(name):
            return ctx.enter_context(nc.semaphore("m_" + name))

        wap = sb("wap", [P, 4, D])
        sig = sb("sig", [P, DC, TOK])
        gc = sb("gc", [P, 2, SEQ])
        gcd = sb("gcd", [P, DC, SMP])
        prd = sb("prd", [P, DC, SMP])
        hoT = sb("hoT", [P, 4, TOK])
        stat = sb("stat", [P, 2, TOK])
        sqy = sb("sqy", [P, 2, TOK])
        vec = sb("vec", [P, 2, DC])
        ag = sb("ag", [P, NG, HG, ACCW])
        cg = sb("cg", [P, 8, HG])
        cw = sb("cw", [P, NG, HG])
        ho = sb("ho", [P, 2, GW])
        tmp = sb("tmp", [P, GW])

        kq = qk[:, :, :, :, :].rearrange("p a b c t -> p a (b c t)")
        q1 = kq[:, :, 0:NS * GW].rearrange("p s (r x) -> p s r x", r=NS)
        k1, k3, q3 = (kq[:, :, (NS + x) * GW:(NS + x + 1) * GW] for x in range(3))
        R = kq[0:SMP, 0, 0:NG * HG * P].rearrange("p (j k) -> p j k", k=P)
        newv = kq[0:SMP, 1, 0:6 * GW].rearrange("p (d x) -> p d x", d=6)
        own = kq[:, 1, 6 * GW:8 * GW].rearrange("p (s x) -> p s x", s=2)
        vr = sb("vr", [P, 2, 6, GW])
        vs = [vr[:, 0], vr[:, 1], kq[:, 0, 0:6 * GW].rearrange("p (x c) -> p x c", x=6)]
        newk, qn = vr[0:SMP, 0], vr[0:SMP, 1, 0:NG]
        S3 = sb("S3", [P, HG, NB])
        PT = sb("PT", [P, NB, 6, HG, NS])
        N = sb("N", [SMP, 6, HG])
        hsn = sb("hsn", [SMP, GW])
        mx = sb("mx", [SMP, NG * HG])
        M = sb("M", [SMP, 3, HG])
        den = sb("den", [SMP, 3, HG])

        bank = [ctx.enter_context(nc.psum_tensor(f"m_b{i}", [P, 512], F32)) for i in range(8)]
        bg, bp = bank[0:2], bank[0:4]
        bd = bank[4]
        bs, bsd = bank[5], bank[6]
        bt = bank[7]
        acc = bt[:, 0:4 * SMP].rearrange("p (c t) -> p c t", c=4)

        wcp_in = [sem("wcp_in0"), sem("wcp_in1")]
        late_in = sem("late_in")
        vec_in = sem("vec_in")
        chain = sem("chain")
        z_ready = sem("z_ready")
        sig_ready = sem("sig_ready")
        ag_in = sem("ag_in")
        c_max = sem("c_max")
        c_exp = sem("c_exp")
        ho_ready = sem("ho_ready")
        hp_ready = sem("hp_ready")
        hoT_ready = sem("hoT_ready")
        ysum_ready = sem("ysum_ready")
        sum_ready = sem("sum_ready")
        d_ready = sem("d_ready")
        sq_ready = sem("sq_ready")
        sq_used = sem("sq_used")
        var_ready = sem("var_ready")
        std_ready = sem("std_ready")
        yn_ready = sem("yn_ready")
        y_ready = sem("y_ready")
        gc_in = [sem("gc_in0"), sem("gc_in1")]
        pr_ready = sem("pr_ready")
        mix_ready = sem("mix_ready")
        in1, in3 = ([sem(f"in{g}_{i}") for i in range(2)] for g in (1, 3))
        used1, used3 = sem("used1"), sem("used3")
        p1_ready = sem("p1_ready")
        new_zero = sem("new_zero")
        new_in = sem("new_in")
        pn_ready = sem("pn_ready")
        n_ready = sem("n_ready")
        S_ready = sem("S_ready")
        r_ready = sem("r_ready")
        R_ready = sem("R_ready")
        x_ready = sem("x_ready")
        e_ready = sem("e_ready")
        P_ready = sem("P_ready")
        b_ready = sem("b_ready")
        PT_ready = sem("PT_ready")
        newv_in = sem("newv_in")
        nv_ready = sem("nv_ready")
        hsn_ready = sem("hsn_ready")
        v_in = [sem(f"v_in{i}") for i in range(3)]
        v_used = sem("v_used")
        own_ready = sem("own_ready")
        acc_ready = sem("acc_ready")
        pd_ready = sem("pd_ready")

        def cache(g, b, w):
            rows = a[f"cache_kv_g{g + 1}"][0, b].rearrange("l w h e -> l w (h e)")[:, w, :]
            if g == 1:
                return rows.rearrange("(m r) x -> m r x", r=NS)
            if g == 2:
                return rows.rearrange("(m r) x -> m r x", r=16)[:, 0:NS, :]
            return rows

        new_rows = [a[f"kv{g}s"][0].rearrange("b s w h e -> (b s) w (h e)") for g in range(NG)]
        EXP_AFTER = (3, 5, 7)
        TURN_AFTER = (5, 7)

        def slot(c):
            return (w_in[2] + c // 4) % 2

        block = ctx.enter_context(nc.Block())

        @block.sync
        def _(eng):
            def load_batch(b):
                qrow = [sc["q_smp"][g][NS * b:NS * (b + 1), :] for g in range(NG)]
                s = b % 2
                if b >= 2:
                    eng.wait_ge(used1, b - 1)
                eng.dma_start(k1[:, s], cache(0, b, 0)).then_inc(in1[s], 16)
                eng.dma_start(q1[:, s], qrow[0].unsqueeze(0).to_broadcast([P, NS, GW])).then_inc(in1[s], 16)
                if b >= 2:
                    eng.wait_ge(used3, b - 1)
                eng.dma_start(k3[:, s], cache(2, b, 0)).then_inc(in3[s], 16)
                eng.dma_start(q3[:, s], qrow[2].unsqueeze(0).to_broadcast([P // NS, NS, GW])).then_inc(in3[s], 16)

            def load_values(b):
                eng.dma_start(vs[b % 3][:, 0, :], cache(0, b, 1)).then_inc(v_in[b % 3], 16)
                eng.dma_start(vs[b % 3][:, 1:1 + NS, :], cache(1, b, 1)).then_inc(v_in[b % 3], 16)
                eng.dma_start(vs[b % 3][:, 5, :], cache(2, b, 1)).then_inc(v_in[b % 3], 16)

            def load_gate(c):
                eng.wait_ge(mix_ready, c - 1)
                eng.dma_start(gc[:, c % 2, :], sc["gates"][c][:, 0:SEQ]).then_inc(gc_in[c % 2], 16)

            load_batch(0)
            with nc.allow_non_contiguous_dma("short rows of small inputs"):
                eng.dma_start(vec[:, 0, :], a["conv_ln_g"][0].rearrange("(c p) -> p c", p=P)).then_inc(vec_in, 16)
                eng.dma_start(vec[:, 1, :], a["conv_ln_b"][0].rearrange("(c p) -> p c", p=P)).then_inc(vec_in, 16)
            for g in range(NG):
                eng.dma_start(ag[:, g, :, :].rearrange("p h w -> p (h w)"), sc["attn"][g][0:P, :]).then_inc(ag_in, 16)
            for c in range(2):
                eng.dma_start(gc[:, c, :], sc["gates"][c][:, 0:SEQ]).then_inc(gc_in[c], 16)
            wcp_v = a["w_conv_proj"][0].rearrange("(k p) c -> p k c", p=P)
            for b in range(1, NB):
                if 3 <= b <= NT + 1:
                    i = b - 2
                    eng.wait_ge(ho_ready, i)
                    for g in range(NG):
                        eng.dma_start(ag[:, g, :, :].rearrange("p h w -> p (h w)"), sc["attn"][g][P * i:P * (i + 1), :]).then_inc(ag_in, 16)
                load_batch(b)
                if b in (3, 5):
                    j = (b - 3) // 2
                    eng.wait_ge(z_ready, 4 * (j + 1))
                    eng.dma_start(wring[:, slot(4 * j), :, :], wcp_v[:, :, 512 * j:512 * (j + 1)]).then_inc(wcp_in[j], 16)
                if b == 4:
                    eng.wait_ge(n_ready, 1)
                    load_values(0)
                    load_values(1)
            for c in range(2, 7):
                load_gate(c)
            eng.wait_ge(b_ready, 1)
            load_values(2)
            wo_v = a["w_out"][0].rearrange("(k p) c -> p k c", p=P)
            for b in range(3, NB):
                eng.wait_ge(v_used, b - 2)
                load_values(b)
                if b == 4:
                    load_gate(7)
            eng.wait_ge(pr_ready, 4)
            eng.dma_start(wring[:, slot(0), :, :], wo_v[:, :, 0:512]).then_inc(late["wo_in"][0], 16)
            eng.wait_ge(pr_ready, DC)
            eng.dma_start(wring[:, slot(4), :, :], wo_v[:, :, 512:D]).then_inc(late["wo_in"][1], 16)
            eng.dma_start(rows_of(yT)[:, 0, 0, :], a["x_prompt"][0, 0:P, :]).then_inc(late["x_in"], 16)

        @block.gpsimd
        def _(eng):
            eng.memset(newk[:, 0:NS, :], 0.0).then_inc(new_zero, 1)
            eng.memset(PT[:, :, 1:5, :, :], 0.0).then_inc(new_zero, 1)
            eng.dma_start(wap[:, :, :], a["w_attn_proj"][0].rearrange("(k p) c -> p k c", p=P)).then_inc(late_in, 16)
            eng.wait_ge(new_zero, 1)
            for d in range(NS):
                eng.dma_start(newk[d:SMP, d, :], new_rows[0][0:SMP - d, 0, :]).then_inc(new_in, 16)
            for g in (1, 2):
                eng.dma_start(newk[:, 3 + g, :], new_rows[g][:, 0, :]).then_inc(new_in, 16)
            for g in range(NG):
                eng.dma_start(qn[:, g, :], sc["q_smp"][g]).then_inc(new_in, 16)
            eng.dma_start(gcd[:, :, :], sc["gates"][:, :, SEQ:TOK].rearrange("c p t -> p c t")).then_inc(late_in, 16)
            def products(b):
                s = b % 2
                eng.wait_ge(in1[s], 32 * (b // 2 + 1))
                eng.tensor_tensor(q1[:, s], k1[:, s].unsqueeze(1).to_broadcast([P, NS, GW]), q1[:, s], ALU.mult).then_inc(p1_ready, 1)

            products(0)
            eng.wait_ge(new_in, 16 * 9)
            eng.tensor_tensor(newk[:, 0:NS, :], newk[:, 0:NS, :], qn[:, 0:1, :].to_broadcast([SMP, NS, GW]), ALU.mult)
            eng.tensor_tensor(newk[:, NS:6, :], newk[:, NS:6, :], qn[:, 1:3, :], ALU.mult).then_inc(pn_ready, 1)
            for b in range(1, NB):
                products(b)
            eng.wait_ge(used1, NB)
            eng.wait_ge(used3, NB)
            eng.memset(newv[:, 0:NS, :], 0.0).then_inc(new_zero, 1)
            eng.wait_ge(new_zero, 3)
            for d in range(NS):
                eng.dma_start(newv[d:SMP, d, :], new_rows[0][0:SMP - d, 1, :]).then_inc(newv_in, 16)
            for g in (1, 2):
                eng.dma_start(newv[:, 3 + g, :], new_rows[g][:, 1, :]).then_inc(newv_in, 16)
            eng.wait_ge(newv_in, 16 * 6)
            eng.wait_ge(P_ready, 1)
            eng.tensor_tensor(newv.rearrange("p d (h e) -> p (d h) e", h=HG), newv.rearrange("p d (h e) -> p (d h) e", h=HG),
                              N[:, :, :].rearrange("p d h -> p (d h)").unsqueeze(2).to_broadcast([SMP, 6 * HG, HD]), ALU.mult).then_inc(nv_ready, 1)

        @block.tensor
        def _(eng):
            ident = cst[:, C_ID:C_ID + P]
            ones = cst[:, C_ONE:C_ONE + P]

            def gates(c):
                if c % 4 == 0:
                    eng.wait_ge(*w_in[c // 4])
                if c >= 2:
                    eng.wait_ge(sig_ready, c - 1)
                for k in range(DC):
                    eng.matmul(bg[c % 2][:, :], wring[:, slot(c), k, P * (c % 4):P * (c % 4 + 1)], hT[:, k, 0:SEQ], start=(k == 0), stop=(k == DC - 1))
                for k in range(DC):
                    mm = eng.matmul(bd[:, SMP * c:SMP * (c + 1)], wring[:, slot(c), k, P * (c % 4):P * (c % 4 + 1)], hT[:, k, SEQ:TOK],
                                    start=(k == 0), stop=(k == DC - 1))
                mm.then_inc(z_ready, 1)

            def turn_heads(i):
                eng.wait_ge(ho_ready, i + 1)
                if i:
                    eng.wait_ge(hoT_ready, i)
                for c in range(4):
                    mm = eng.transpose(bt[:, P * c:P * (c + 1)], ho[:, i % 2, P * c:P * (c + 1)], ident)
                mm.then_inc(hp_ready, 1)

            def conv_project(c):
                w = wring[:, slot(c), :, P * (c % 4):P * (c % 4 + 1)]
                if c >= 2:
                    eng.wait_ge(mix_ready, c - 1)
                if c % 4 == 0:
                    eng.wait_ge(wcp_in[c // 4], 16)
                for k in range(DC):
                    eng.matmul(bp[2 * (c % 2)][:, :], w[:, k, :], yT[:, k, 0:SEQ], start=(k == 0), stop=(k == DC - 1))
                for k in range(DC):
                    eng.matmul(bd[:, SMP * c:SMP * (c + 1)], w[:, k, :], yT[:, k, SEQ:TOK], start=(k == 0), stop=(k == DC - 1))

            def attn_project(c):
                for k in range(4):
                    mm = eng.matmul(bp[2 * (c % 2) + 1][:, :], wap[:, k, P * c:P * (c + 1)], hoT[:, k, 0:SEQ], start=(k == 0), stop=(k == 3))
                mm.then_inc(pr_ready, 1)

            def decode_outputs(b):
                eng.wait_ge(v_in[b % 3], 48 * (b // 3 + 1))
                lo = HG * NS * (b % 4)
                for x in range(6):
                    mm = eng.matmul((bs, bsd)[b // 4][lo:lo + HG * NS, :], PT[:, b, x, :, :].rearrange("p h t -> p (h t)"), vs[b % 3][:, x, :],
                                    start=(x == 0), stop=(x == 5))
                mm.then_inc(v_used, 1)

            gates(0)
            eng.wait_ge(ysum_ready, 1)
            eng.matmul(bs[:, :], ones, stat[:, 0, 0:SEQ], start=True, stop=True)
            eng.matmul(bsd[:, 0:SMP], ones, stat[:, 0, SEQ:TOK], start=True, stop=True).then_inc(sum_ready, 1)
            gates(1)
            eng.wait_ge(d_ready, 1)
            for k in range(DC):
                eng.wait_ge(sq_ready, k + 1)
                eng.matmul(bs[:, :], ones, sqy[:, k % 2, 0:SEQ], start=(k == 0), stop=(k == DC - 1))
                eng.matmul(bsd[:, 0:SMP], ones, sqy[:, k % 2, SEQ:TOK], start=(k == 0), stop=(k == DC - 1)).then_inc(sq_used, 1)
            for c in range(2, DC):
                gates(c)
                if c in TURN_AFTER:
                    turn_heads(TURN_AFTER.index(c))
            eng.wait_ge(y_ready, DC)
            eng.wait_ge(sig_ready, DC + 1)
            for c in range(2):
                conv_project(c)
            for i in range(len(TURN_AFTER), NT):
                turn_heads(i)
            eng.wait_ge(hoT_ready, NT)
            eng.wait_ge(late_in, 32)
            for c in range(2):
                attn_project(c)
            for c in range(2, 3):
                conv_project(c)
                attn_project(c)
            eng.wait_ge(S_ready, 1)
            for j in range(6):
                if j >= 2:
                    eng.wait_ge(R_ready, j - 1)
                for x in range(4):
                    mm = eng.transpose((bs, bsd)[j % 2][0:SMP, P * x:P * (x + 1)], S[:, j // 2, 4 * (j % 2) + x, :], ident)
                mm.then_inc(r_ready, 1)
            for c in range(3, 5):
                conv_project(c)
                attn_project(c)
            eng.wait_ge(P_ready, 1)
            for j in range(NG * HG):
                mm = eng.transpose((bs, bsd)[j // 16][:, SMP * (j % 16):SMP * (j % 16 + 1)], R[:, j, :], cst[0:SMP, C_ID:C_ID + SMP])
            mm.then_inc(b_ready, 1)
            eng.wait_ge(PT_ready, 1)
            eng.wait_ge(hoT_ready, NT)
            for b in range(2):
                decode_outputs(b)
            conv_project(5)
            attn_project(5)
            for b in range(2, 5):
                decode_outputs(b)
            conv_project(6)
            attn_project(6)
            for b in range(5, NB):
                decode_outputs(b)
            conv_project(7)
            eng.wait_ge(hsn_ready, 1)
            for half in range(2):
                at = half * SMP // 2
                eng.wait_ge(own_ready, half + 1)
                for c in range(4):
                    out = acc[:, c, at:at + SMP // 2]
                    eng.matmul(out, hsn[:, P * c:P * (c + 1)], cst[0:SMP, C_ID + at:C_ID + at + SMP // 2], start=True, stop=False)
                    mm = eng.matmul(out, own[:, half, P * c:P * (c + 1)], cst[:, C_SUM:C_SUM + SMP // 2], start=False, stop=True)
            mm.then_inc(acc_ready, 1)
            attn_project(7)
            eng.wait_ge(hoT_ready, NT + 1)
            eng.wait_ge(mix_ready, DC - 1)
            for c in range(DC):
                for k in range(4):
                    mm = eng.matmul(bp[0][:, SMP * c:SMP * (c + 1)], wap[:, k, P * c:P * (c + 1)], hoT[:, k, SEQ:TOK], start=(k == 0), stop=(k == 3))
            mm.then_inc(pd_ready, 1)

        @block.scalar
        def _(eng):
            def sigmoid(c):
                eng.wait_ge(z_ready, c + 1)
                eng.activation(sig[:, c, 0:SEQ], bg[c % 2][:, :], ACT.Sigmoid).then_inc(sig_ready, 1)

            def combine_exp(i):
                eng.wait_ge(c_max, i + 1)
                eng.activation(cw[:, :, :], cw[:, :, :], ACT.Exp).then_inc(c_exp, 1)

            def keep_heads(i):
                eng.wait_ge(hp_ready, i + 1)
                eng.activation(hoT[:, :, P * i:P * (i + 1)], bt[:, :].rearrange("p (c t) -> p c t", c=4), ACT.Copy).then_inc(hoT_ready, 1)

            for k in range(DC):
                eng.wait_ge(d_ready, k + 1)
                if k >= 2:
                    eng.wait_ge(sq_used, k - 1)
                eng.activation(sqy[:, k % 2, :], yT[:, k, :], ACT.Square).then_inc(sq_ready, 1)
                if k == 1:
                    for c in range(2):
                        sigmoid(c)
            eng.wait_ge(var_ready, 1)
            eng.activation(stat[:, 1, :], stat[:, 1, :], ACT.Sqrt).then_inc(std_ready, 1)
            sigmoid(2)
            eng.wait_ge(vec_in, 32)
            for k in range(DC):
                eng.wait_ge(yn_ready, k + 1)
                eng.activation(yT[:, k, :], yT[:, k, :], ACT.Silu, scale=vec[:, 0, k:k + 1], bias=vec[:, 1, k:k + 1]).then_inc(y_ready, 1)
            for c in range(3, DC):
                sigmoid(c)
                if c in TURN_AFTER:
                    keep_heads(TURN_AFTER.index(c))
                if c in EXP_AFTER:
                    combine_exp(EXP_AFTER.index(c))
            eng.wait_ge(z_ready, DC)
            eng.activation(sig[:, :, SEQ:TOK], bd[:, 0:DC * SMP].rearrange("p (c t) -> p c t", c=DC), ACT.Sigmoid).then_inc(sig_ready, 1)
            combine_exp(NT - 1)
            for i in range(len(TURN_AFTER), NT):
                keep_heads(i)
            eng.wait_ge(used1, NB)
            eng.wait_ge(used3, NB)
            for j in range(6):
                eng.wait_ge(r_ready, j + 1)
                eng.activation(R[:, 4 * j:4 * j + 4, :], (bs, bsd)[j % 2][0:SMP, :].rearrange("p (a k) -> p a k", a=4), ACT.Copy).then_inc(R_ready, 1)
            eng.wait_ge(x_ready, 1)
            eng.activation(R, R, ACT.Exp).then_inc(e_ready, 1)
            eng.activation(N[:, :, :], N[:, :, :], ACT.Exp).then_inc(e_ready, 1)
            eng.wait_ge(b_ready, 1)
            eng.wait_ge(new_zero, 2)
            for x, b in ((0, bs[:, 0:HG * SMP]), (5, bsd[:, 0:HG * SMP])):
                eng.activation(PT[:, :, x, :, :].rearrange("p b h t -> p h b t"), b.rearrange("p (h b t) -> p h b t", h=HG, t=NS), ACT.Copy)
            for t in range(NS):
                ins = eng.activation(PT[:, :, 1 + t, :, t].rearrange("p b h -> p h b"), bs[:, HG * SMP:2 * HG * SMP].rearrange("p (h b t) -> p h b t", h=HG, t=NS)[:, :, :, t], ACT.Copy)
            ins.then_inc(PT_ready, 1)

        @block.vector
        def _(eng):
            count = [0]

            def link(ins):
                count[0] += 1
                ins.then_inc(chain, 1)
                eng.wait_ge(chain, count[0])

            def signal(ins, s, n):
                ins.then_inc(s, 1)
                eng.wait_ge(s, n)

            def by_head(x):
                return x.rearrange("p s (h e) -> p s h e", h=HG)

            def batch_scores(b):
                s = b % 2
                eng.wait_ge(p1_ready, b + 1)
                signal(eng.tensor_reduce(S[:, 0, :, NS * b:NS * (b + 1)].rearrange("p h s -> p s h"), by_head(q1[:, s]), AX, ALU.add), used1, b + 1)
                eng.wait_ge(in3[s], 32 * (b // 2 + 1))
                link(eng.tensor_tensor(q3[:, s], k3[:, s], q3[:, s], ALU.mult))
                signal(eng.tensor_reduce(S3[:, :, b], q3[:, s].rearrange("p (h e) -> p h e", h=HG), AX, ALU.add), used3, b + 1)

            def group_maxima(i):
                eng.wait_ge(ag_in, 48 * (i + 1))
                mxs = [ag[:, g, :, HD] for g in range(NG)]
                link(eng.tensor_tensor(cg[:, 0, :], mxs[0], mxs[1], ALU.max))
                link(eng.tensor_tensor(cg[:, 0, :], cg[:, 0, :], mxs[2], ALU.max))
                for g in range(NG):
                    ins = eng.tensor_tensor(cw[:, g, :], mxs[g], cg[:, 0, :], ALU.subtract)
                    if g == NG - 1:
                        signal(ins, c_max, i + 1)
                    else:
                        link(ins)

            def combine(i):
                dns = [ag[:, g, :, HD + 1] for g in range(NG)]
                eng.wait_ge(c_exp, i + 1)
                for g in range(NG):
                    link(eng.tensor_tensor(cg[:, 1 + g, :], cw[:, g, :], dns[g], ALU.mult))
                link(eng.tensor_tensor(cg[:, 1, :], cg[:, 1, :], cg[:, 2, :], ALU.add))
                link(eng.tensor_tensor(cg[:, 1, :], cg[:, 1, :], cg[:, 3, :], ALU.add))
                link(eng.reciprocal(cg[:, 4, :], cg[:, 1, :]))
                if i >= 2:
                    eng.wait_ge(hp_ready, i - 1)
                hv = ho[:, i % 2, :].rearrange("p (j w e) -> p w j e", w=2, e=HD)
                tw = tmp[:, :].rearrange("p (j w e) -> p w j e", w=2, e=HD)
                for g in range(NG):
                    link(eng.tensor_tensor(cg[:, 5 + g, :], cw[:, g, :], cg[:, 4, :], ALU.mult))
                    for w in range(2):
                        link(eng.tensor_tensor((tw if g else hv)[:, w, :, :], ag[:, g, 4 * w:4 * w + 4, 0:HD],
                                               cg[:, 5 + g, 4 * w:4 * w + 4].unsqueeze(2).to_broadcast([P, 4, HD]), ALU.mult))
                    if g:
                        ins = eng.tensor_tensor(ho[:, i % 2, :], ho[:, i % 2, :], tmp[:, :], ALU.add)
                        if g == NG - 1:
                            signal(ins, ho_ready, i + 1)
                        else:
                            link(ins)

            def merge(c):
                bc, ba = bp[2 * (c % 2)], bp[2 * (c % 2) + 1]
                eng.wait_ge(pr_ready, c + 1)
                eng.wait_ge(gc_in[c % 2], 16 * (c // 2 + 1))
                link(eng.tensor_tensor(gc[:, c % 2, :], gc[:, c % 2, :], bc[:, :], ALU.mult))
                link(eng.tensor_tensor(sig[:, c, 0:SEQ], sig[:, c, 0:SEQ], ba[:, :], ALU.mult))
                signal(eng.tensor_tensor(mT[:, c, 0:SEQ], gc[:, c % 2, :], sig[:, c, 0:SEQ], ALU.add), mix_ready, c + 1)

            for k in range(1, DC):
                ins = eng.tensor_tensor(stat[:, 0, :], yT[:, 0, :] if k == 1 else stat[:, 0, :], yT[:, k, :], ALU.add)
                if k < DC - 1:
                    link(ins)
            signal(ins, ysum_ready, 1)
            eng.wait_ge(sum_ready, 1)
            link(eng.tensor_scalar(stat[:, 0, 0:SEQ], bs[:, :], 1.0 / D, None, ALU.mult))
            link(eng.tensor_scalar(stat[:, 0, SEQ:TOK], bsd[:, 0:SMP], 1.0 / D, None, ALU.mult))
            for k in range(DC):
                eng.tensor_tensor(yT[:, k, :], yT[:, k, :], stat[:, 0, :], ALU.subtract).then_inc(d_ready, 1)
            batch_scores(0)
            eng.wait_ge(pn_ready, 1)
            signal(eng.tensor_reduce(N[:, :, :], by_head(newk), AX, ALU.add), n_ready, 1)
            link(eng.tensor_scalar(N[:, NS:6, :], N[:, NS:6, :], QK_SCALE, None, ALU.mult))
            link(eng.scalar_tensor_tensor(out=N[:, 0:NS, :], in0=N[:, 0:NS, :], scalar=QK_SCALE,
                                          in1=cst[0:SMP, C_BACK:C_BACK + NS].unsqueeze(2).to_broadcast([SMP, NS, HG]), op0=ALU.mult, op1=ALU.add))
            eng.wait_ge(d_ready, DC)
            eng.wait_ge(sq_used, DC)
            link(eng.tensor_scalar(stat[:, 1, 0:SEQ], bs[:, :], 1.0 / D, LN_EPS, ALU.mult, ALU.add))
            signal(eng.tensor_scalar(stat[:, 1, SEQ:TOK], bsd[:, 0:SMP], 1.0 / D, LN_EPS, ALU.mult, ALU.add), var_ready, 1)
            eng.wait_ge(std_ready, 1)
            link(eng.reciprocal(stat[:, 1, :], stat[:, 1, :]))
            for k in range(DC):
                eng.tensor_tensor(yT[:, k, :], yT[:, k, :], stat[:, 1, :], ALU.mult).then_inc(yn_ready, 1)
            group_maxima(0)
            for b in range(1, NB):
                if b >= NB - 2:
                    merge(b - NB + 2)
                batch_scores(b)
                if b <= NT:
                    if b > 1:
                        group_maxima(b - 1)
                    combine(b - 1)
            hb = [S[:, g, :, :].rearrange("p h (b s) -> p (h b) s", s=NS) for g in range(NG)]

            def rowmask(at, rows=HG * NB):
                return cst[:, at:at + NS].unsqueeze(1).to_broadcast([P, rows, NS])

            link(eng.scalar_tensor_tensor(out=hb[0], in0=hb[0], scalar=QK_SCALE, in1=rowmask(C_NEW1), op0=ALU.mult, op1=ALU.add))
            link(eng.tensor_scalar(S[:, 1, :, :], S[:, 1, :, :], QK_SCALE, None, ALU.mult))
            link(eng.tensor_tensor(hb[2], S3[:, :, :].rearrange("p h b -> p (h b)").unsqueeze(2).to_broadcast([P, HG * NB, NS]), rowmask(C_KEEP), ALU.mult))
            signal(eng.scalar_tensor_tensor(out=hb[2], in0=hb[2], scalar=QK_SCALE, in1=rowmask(C_DROP), op0=ALU.mult, op1=ALU.add), S_ready, 1)
            merge(2)
            eng.wait_ge(R_ready, 6)
            link(eng.tensor_reduce(mx[:, :], R, AX, ALU.max))
            link(eng.tensor_reduce(M[:, 0, :], mx[:, :].rearrange("p (g h) -> p h g", g=NG), AX, ALU.max))
            link(eng.tensor_reduce(M[:, 1, :], N[:, :, :].rearrange("p d h -> p h d"), AX, ALU.max))
            link(eng.tensor_tensor(M[:, 2, :], M[:, 0, :], M[:, 1, :], ALU.max))
            for g in range(NG):
                link(eng.tensor_tensor(R[:, HG * g:HG * (g + 1), :], R[:, HG * g:HG * (g + 1), :], M[:, 2, :].unsqueeze(2).to_broadcast([SMP, HG, P]), ALU.subtract))
            signal(eng.tensor_tensor(N[:, :, :], N[:, :, :], M[:, 2:3, :].to_broadcast([SMP, 6, HG]), ALU.subtract), x_ready, 1)
            merge(3)
            eng.wait_ge(e_ready, 2)
            link(eng.tensor_reduce(mx[:, :], R, AX, ALU.add))
            link(eng.tensor_reduce(den[:, 0, :], mx[:, :].rearrange("p (g h) -> p h g", g=NG), AX, ALU.add))
            link(eng.tensor_reduce(den[:, 1, :], N[:, :, :].rearrange("p d h -> p h d"), AX, ALU.add))
            link(eng.tensor_tensor(den[:, 0, :], den[:, 0, :], den[:, 1, :], ALU.add))
            link(eng.reciprocal(den[:, 2, :], den[:, 0, :]))
            link(eng.tensor_tensor(N[:, :, :], N[:, :, :], den[:, 2:3, :].to_broadcast([SMP, 6, HG]), ALU.mult))
            for g in range(NG):
                ins = eng.tensor_tensor(R[:, HG * g:HG * (g + 1), :], R[:, HG * g:HG * (g + 1), :], den[:, 2, :].unsqueeze(2).to_broadcast([SMP, HG, P]), ALU.mult)
                if g == NG - 1:
                    signal(ins, P_ready, 1)
                else:
                    link(ins)
            for c in range(4, 6):
                merge(c)
            eng.wait_ge(nv_ready, 1)
            signal(eng.tensor_reduce(hsn[:, :], newv.rearrange("p d x -> p x d"), AX, ALU.add), hsn_ready, 1)
            def keep_own(half):
                eng.wait_ge(v_used, 4 * (half + 1))
                signal(eng.tensor_tensor(own[:, half, :].rearrange("p (h e) -> p h e", h=HG), (bs, bsd)[half][:, :].rearrange("p (h e) -> p h e", h=HG),
                                         cst[:, C_HEAD:C_HEAD + HG].unsqueeze(2).to_broadcast([P, HG, HD]), ALU.mult), own_ready, half + 1)

            keep_own(0)
            merge(6)
            keep_own(1)
            eng.wait_ge(acc_ready, 1)
            signal(eng.tensor_copy(hoT[:, :, SEQ:TOK], acc), hoT_ready, NT + 1)
            merge(7)
            def decode_bank(b):
                return b[:, 0:DC * SMP].rearrange("p (c t) -> p c t", c=DC)

            eng.wait_ge(late_in, 32)
            link(eng.tensor_tensor(gcd[:, :, :], gcd[:, :, :], decode_bank(bd), ALU.mult))
            eng.wait_ge(pd_ready, 1)
            link(eng.tensor_tensor(prd[:, :, :], sig[:, :, SEQ:TOK], decode_bank(bp[0]), ALU.mult))
            link(eng.tensor_tensor(mT[:, :, SEQ:TOK], gcd[:, :, :], prd[:, :, :], ALU.add))


def rows_of(yT):
    return yT[:, :, :].rearrange("p c t -> p (c t)")[:, 0:4 * D].rearrange("p (w s d) -> p w s d", w=2, s=2)


def peer(nc, a, cst, yT, mT, wo, late):
    SLOTS = PH * TOPK
    STEPS = NT * SLOTS + SLOTS // 4
    RING = 6
    LOW = -3.0e38
    QUADS = PH // 2

    OUT_AT = (2, 4, 6, 8)
    SUM_AT = 12
    POW_AT = SUM_AT + RING + 4
    NORM_AT = POW_AT + 2
    TURN_AT = NORM_AT + 2

    def quad_at(i, m):
        return TURN_AT + 4 + 18 * m if i else (3, 13)[m - 2]

    def head_at(i, h):
        return quad_at(i, 0) + 14 + 9 * h if i else 1 + 6 * (h - 1)

    def heads_at(tile, k, lag=0):
        return [(i, h) for i in (tile, tile + 1) for h in range(PH)
                if i <= NT and (i == tile + 1 or (i == 0 and h)) and head_at(i, h) + lag == k]

    RETRIEVE_AT = (0, 2, 4, 6)

    def quads_at(tile, k, lag=0):
        return [(i, m) for i in (tile, tile + 1) for m in range(QUADS)
                if i <= NT and (i == tile + 1 or (i == 0 and m >= 2)) and quad_at(i, m) + lag == k]

    with ExitStack() as ctx:
        def sb(name, shape, dt=F32):
            return ctx.enter_context(nc.sbuf_tensor("p_" + name, shape, dt))

        def sem(name):
            return ctx.enter_context(nc.semaphore("p_" + name))

        rows = rows_of(yT)
        y, h2 = rows[:, 0], rows[:, 1]
        h2T = mT
        wq = sb("wq", [P, DC, 2 * PH * HALF])
        skT = sb("skT", [P, 2 * PH, KEYS])
        ring = sb("ring", [P, RING, 2 * D])
        sk = ring[:, 0, :].rearrange("p (j c) -> p j c", j=2 * PH)
        w2 = sb("w2", [P, D])
        rms = sb("rms", [P, 4])
        qp = sb("qp", [P, 4, P])
        sco = sb("sco", [P, 2, 4, KEYS])
        idx = sb("idx", [P, 2, SLOTS], U32)
        gw = sb("gw", [P, 2, SLOTS])
        dots = sb("dots", [P, 4])
        gel = sb("gel", [P, 4])
        wgt = sb("wgt", [P, 4])
        diag = sb("diag", [P, 4, P])
        tv = sb("tv", [P, 2, TOPK])
        ti = sb("ti", [P, 2, TOPK], U32)
        tif = sb("tif", [P, 2, TOPK])
        cand = sb("cand", [P, TOPK, TOPK])
        cv = sb("cv", [P, TOPK])
        ci = sb("ci", [P, TOPK], U32)
        ca = sb("ca", [P, 2, TOPK], U32)
        caf = sb("caf", [P, 2, TOPK])
        eq = cand
        e12 = sb("e12", [P, 2, TOPK])
        nmx = sb("nmx", [P, 1])
        ex = sb("ex", [P, TOPK])
        exs = sb("exs", [P, 2])
        idx4 = sb("idx4", [P, SLOTS // 4], U32)
        gw4 = sb("gw4", [P, SLOTS // 4])
        acc, ob, tb = ([ctx.enter_context(nc.psum_tensor(f"p_{w}{i}", [P, 512], F32)) for i in range(2)] for w in ("acc", "o", "t"))
        qb, kb = (ctx.enter_context(nc.psum_tensor("p_" + w, [P, 512], F32)) for w in ("q", "k"))

        wo_in = late["wo_in"]
        wq_in = [sem(f"wq_in{m}") for m in range(QUADS)]
        sk_in = sem("sk_in")
        kt_ready = sem("kt_ready")
        skT_ready = sem("skT_ready")
        w2_in = sem("w2_in")
        x_in = [late["x_in"], sem("x_in1")]
        o_ready = sem("o_ready")
        x1_ready = sem("x1_ready")
        x1_sq = sem("x1_sq")
        half_ready = sem("half_ready")
        x1_rstd = sem("x1_rstd")
        h2_ready = sem("h2_ready")
        h2_rep = sem("h2_rep")
        ht_ready = sem("ht_ready")
        h2T_ready = sem("h2T_ready")
        q_ready = sem("q_ready")
        qp_ready = sem("qp_ready")
        s_ready = sem("s_ready")
        sco_ready = sem("sco_ready")
        top_ready = sem("top_ready")
        ex_ready = sem("ex_ready")
        idx_ready = sem("idx_ready")
        quad_in = sem("quad_in")
        chain = sem("chain")
        row_in = [sem(f"row_in{i}") for i in range(RING)]
        dot_ready = sem("dot_ready")
        gel_ready = sem("gel_ready")
        wgt_ready = sem("wgt_ready")
        diag_ready = sem("diag_ready")
        v_used = sem("v_used")
        y_ready = sem("y_ready")
        y_out = [sem("y_out0"), sem("y_out1")]

        def step_tile(t):
            return min(t // SLOTS, NT)

        def step_no(t):
            return step_tile(t), t - SLOTS * step_tile(t)

        def end_of(tile):
            return SLOTS * (tile + 1) if tile < NT else STEPS

        block = ctx.enter_context(nc.Block())

        @block.sync
        def _(eng):
            xs, ys = a["x_sample"].rearrange("b s d -> (b s) d"), a["y_s"].rearrange("b s d -> (b s) d")
            wq_v = a["w_peer_q"][0].rearrange("(k p) c -> p k c", p=P)
            eng.dma_start(w2[:, :], a["norm2_w"].to_broadcast([P, D])).then_inc(w2_in, 16)
            eng.dma_start(sk, a["peer_sub_keys"][0].rearrange("h t k c -> k (h t) c")).then_inc(sk_in, 16)
            for m in range(QUADS):
                eng.dma_start(wq[:, :, 512 * m:512 * (m + 1)], wq_v[:, :, 512 * m:512 * (m + 1)]).then_inc(wq_in[m], 16)
            eng.dma_start(y[:, 1, :], a["x_prompt"][0, P:2 * P, :]).then_inc(x_in[1], 16)
            for i in range(NT):
                s = i % 2
                eng.wait_ge(y_ready, i + 1)
                eng.dma_start(a["y_p"][0, P * i:P * (i + 1), :], y[:, s, :]).then_inc(y_out[s], 16)
                if i + 2 <= NT:
                    n = tile_rows(i + 2)
                    eng.wait_ge(y_out[s], 16 * (i // 2 + 1))
                    src = a["x_prompt"][0, P * (i + 2):P * (i + 3), :] if i + 2 < NT else xs
                    eng.dma_start(y[0:n, s, :], src).then_inc(x_in[s], 16)
                if i + 2 == NT:
                    eng.wait_ge(h2_ready, UPT)
                    for r in range(1, 4):
                        eng.dma_start(h2[SMP * r:SMP * (r + 1), NT % 2, :], h2[0:SMP, NT % 2, :]).then_inc(h2_rep, 16)
                    eng.wait_ge(idx_ready, PH * UPT)
                    for r in range(4):
                        for dst, src in ((idx4, idx), (gw4, gw)):
                            eng.dma_start(dst[SMP * r:SMP * (r + 1), :], src[0:SMP, NT % 2, 32 * r:32 * (r + 1)]).then_inc(quad_in, 16)
            eng.wait_ge(y_ready, UPT)
            eng.dma_start(ys, y[0:SMP, NT % 2, :]).then_inc(y_out[0], 16)
            eng.wait_ge(y_out[0], 48)
            eng.wait_ge(y_out[1], 32)

        @block.gpsimd
        def _(eng):
            def rstd(i):
                n = tile_rows(i)
                eng.wait_ge(x1_sq, i + 1)
                eng.tensor_scalar(rms[0:n, 1:2], rms[0:n, 0:1], 1.0 / D, RMS_EPS, ALU.mult, ALU.add).then_inc(half_ready, 1)
                eng.wait_ge(half_ready, 2 + i)
                eng.tensor_tensor(rms[0:n, 2:3], rms[0:n, 1:2], rms[0:n, 3:4], ALU.pow).then_inc(x1_rstd, 1)

            eng.memset(rms[:, 3:4], -0.5).then_inc(half_ready, 1)
            eng.wait_ge(half_ready, 1)
            rstd(0)
            for t in range(STEPS):
                tile, k = step_no(t)
                if tile < NT and k % TOPK == 0:
                    eng.wait_ge(idx_ready, PH * tile + k // TOPK + 1)
                if tile == NT and k == 0:
                    eng.wait_ge(quad_in, 128)
                if t >= RING:
                    eng.wait_ge(v_used, t - RING + 1)
                col = idx[:, tile % 2, k:k + 1] if tile < NT else idx4[:, k:k + 1]
                eng.indirect_dma_start(ring[:, t % RING, :], None, a["expert_uv"], bass.IndirectOffsetOnAxis(col, 0)).then_inc(row_in[t % RING], 16)
                if tile < NT and k == POW_AT:
                    rstd(tile + 1)

        @block.tensor
        def _(eng):
            def out_quarter(i, r):
                n, h, lo = tile_rows(i), r // 2, (r % 2) * 4
                if r == 0 and i:
                    eng.wait_ge(x1_ready, i)
                if lo == 0 and i == 0:
                    eng.wait_ge(wo_in[h], 16)
                for k in range(lo, lo + 4):
                    mm = eng.matmul(ob[h][0:n, :], mT[:, k, P * i:P * i + n], wo[h][:, k, :], start=(k == 0), stop=(k == DC - 1))
                if r == 3:
                    mm.then_inc(o_ready, 1)

            def turn(i):
                n = tile_rows(i)
                eng.wait_ge(h2_ready, i + 1)
                if i:
                    eng.wait_ge(h2T_ready, i)
                for c in range(DC):
                    mm = eng.transpose(tb[c // 4][:, P * (c % 4):P * (c % 4) + n], h2[0:n, i % 2, P * c:P * (c + 1)], cst[0:n, C_ID:C_ID + n])
                mm.then_inc(ht_ready, 1)

            def query(i, m, j):
                n, at = tile_rows(i), 4 * m + j
                if j == 0:
                    eng.wait_ge(h2T_ready, i + 1)
                    eng.wait_ge(wq_in[m], 16)
                    if i or m:
                        eng.wait_ge(qp_ready, QUADS * i + m)
                for k in range(DC):
                    mm = eng.matmul(qb[:, P * j:P * j + n], wq[:, k, P * at:P * (at + 1)], h2T[:, k, P * i:P * i + n], start=(k == 0), stop=(k == DC - 1))
                if j == 3:
                    mm.then_inc(q_ready, 1)

            def scores(i, m):
                n, q = tile_rows(i), QUADS * i + m
                eng.wait_ge(qp_ready, q + 1)
                if q:
                    eng.wait_ge(sco_ready, q)
                for j in range(4):
                    mm = eng.matmul(kb[0:n, P * j:P * (j + 1)], qp[:, j, 0:n], skT[:, 4 * m + j, :], start=True, stop=True)
                mm.then_inc(s_ready, 1)

            for r in range(4):
                out_quarter(0, r)
            eng.wait_ge(sk_in, 16)
            for m, b in enumerate((*acc, qb, kb)):
                for j in range(4):
                    mm = eng.transpose(b[:, P * j:P * (j + 1)], sk[:, 4 * m + j, :], cst[:, C_ID:C_ID + P])
                mm.then_inc(kt_ready, 1)
            turn(0)
            eng.wait_ge(skT_ready, QUADS)
            for m in range(2):
                for j in range(4):
                    query(0, m, j)
                scores(0, m)
            for t in range(STEPS):
                tile, k = step_no(t)
                n = tile_rows(tile)
                eng.wait_ge(row_in[t % RING], 16 * (t // RING + 1))
                if k == 0 and tile:
                    eng.wait_ge(y_ready, tile)
                eng.wait_ge(diag_ready, t + 1)
                for h in range(2):
                    mm = eng.matmul(acc[h][0:n, :], diag[:, t % 4, 0:n], ring[:, t % RING, D + 512 * h:D + 512 * (h + 1)],
                                    start=(k == 0), stop=(t == end_of(tile) - 1))
                mm.then_inc(v_used, 1)
                if tile < NT:
                    if k in OUT_AT:
                        out_quarter(tile + 1, OUT_AT.index(k))
                    if k == TURN_AT:
                        turn(tile + 1)
                    for j in range(4):
                        for i, m in quads_at(tile, k, 2 * j):
                            query(i, m, j)
                    for i, m in quads_at(tile, k, 8):
                        scores(i, m)

        @block.scalar
        def _(eng):
            def square(i):
                n = tile_rows(i)
                eng.wait_ge(x1_ready, i + 1)
                if i >= 2:
                    eng.wait_ge(dot_ready, end_of(i - 2))
                eng.activation(h2[0:n, i % 2, :], y[0:n, i % 2, :], ACT.Square, accum_out=rms[0:n, 0:1]).then_inc(x1_sq, 1)

            def keep_turned(i):
                n = tile_rows(i)
                eng.wait_ge(ht_ready, i + 1)
                for b in range(2):
                    ins = eng.activation(h2T[:, 4 * b:4 * b + 4, P * i:P * i + n], tb[b][:, :].rearrange("p (c t) -> p c t", c=4)[:, :, 0:n], ACT.Copy)
                ins.then_inc(h2T_ready, 1)

            def keep_queries(i, m):
                n, q = tile_rows(i), QUADS * i + m
                eng.wait_ge(q_ready, q + 1)
                if q:
                    eng.wait_ge(s_ready, q)
                eng.activation(qp[:, :, 0:n], qb[:, :].rearrange("p (c t) -> p c t", c=4)[:, :, 0:n], ACT.Copy).then_inc(qp_ready, 1)

            def keep_scores(i, m):
                n, q = tile_rows(i), QUADS * i + m
                eng.wait_ge(s_ready, q + 1)
                if q >= 2:
                    eng.wait_ge(idx_ready, 2 * (q - 1))
                eng.activation(sco[0:n, q % 2, :, :], kb[0:n, :].rearrange("p (c t) -> p c t", c=4), ACT.Copy).then_inc(sco_ready, 1)

            def head_exp(i, h):
                n = tile_rows(i)
                eng.wait_ge(top_ready, PH * i + h + 1)
                eng.activation(ex[0:n, :], cv[0:n, :], ACT.Exp, bias=nmx[0:n, :], accum_out=exs[0:n, 0:1]).then_inc(ex_ready, 1)

            square(0)
            keep_turned(0)
            for m in range(2):
                keep_queries(0, m)
                keep_scores(0, m)
            head_exp(0, 0)
            for t in range(STEPS):
                tile, k = step_no(t)
                n = tile_rows(tile)
                if k == 0 and tile == NT:
                    eng.wait_ge(quad_in, 128)
                w = gw[:, tile % 2, k:k + 1] if tile < NT else gw4[:, k:k + 1]
                shape = cst[:, C_ID:C_ID + P] if tile < NT else cst[:, C_FOLD:C_FOLD + SMP]
                eng.wait_ge(dot_ready, t + 1)
                if t >= 4:
                    eng.wait_ge(v_used, t - 3)
                eng.activation(gel[:, t % 4:t % 4 + 1], dots[:, t % 4:t % 4 + 1], ACT.Gelu).then_inc(gel_ready, 1)
                eng.wait_ge(gel_ready, t + 1)
                eng.activation(wgt[:, t % 4:t % 4 + 1], gel[:, t % 4:t % 4 + 1], ACT.Copy, scale=w).then_inc(wgt_ready, 1)
                eng.wait_ge(wgt_ready, t + 1)
                eng.activation(diag[:, t % 4, 0:n], shape, ACT.Copy, scale=wgt[:, t % 4:t % 4 + 1]).then_inc(diag_ready, 1)
                if tile < NT:
                    if k == SUM_AT:
                        square(tile + 1)
                    if k == TURN_AT:
                        keep_turned(tile + 1)
                    for i, m in quads_at(tile, k, 7):
                        keep_queries(i, m)
                    for i, m in quads_at(tile, k, 9):
                        keep_scores(i, m)
                    for i, h in heads_at(tile, k, RETRIEVE_AT[1]):
                        head_exp(i, h)

        @block.vector
        def _(eng):
            count = [0]

            def link(ins):
                count[0] += 1
                ins.then_inc(chain, 1)
                eng.wait_ge(chain, count[0])

            def signal(ins, s, n):
                ins.then_inc(s, 1)
                eng.wait_ge(s, n)

            def residual(i):
                n, s = tile_rows(i), i % 2
                eng.wait_ge(o_ready, i + 1)
                eng.wait_ge(x_in[s], 16 * (i // 2 + 1))
                for h in range(2):
                    ins = eng.tensor_tensor(y[0:n, s, 512 * h:512 * (h + 1)], y[0:n, s, 512 * h:512 * (h + 1)], ob[h][0:n, :], ALU.add)
                    if h:
                        signal(ins, x1_ready, i + 1)
                    else:
                        link(ins)

            def norm(i):
                n, s = tile_rows(i), i % 2
                eng.wait_ge(x1_rstd, i + 1)
                if i == 0:
                    eng.wait_ge(w2_in, 16)
                signal(eng.scalar_tensor_tensor(out=h2[0:n, s, :], in0=y[0:n, s, :], scalar=rms[0:n, 2:3], in1=w2[0:n, :],
                                                op0=ALU.mult, op1=ALU.mult), h2_ready, i + 1)

            def top16(values, index, x):
                link(eng.max(values[:, 0:8], x))
                link(eng.max_index(index[:, 0:8], values[:, 0:8], x))
                link(eng.match_replace(x, values[:, 0:8], x, LOW))
                link(eng.max(values[:, 8:16], x))
                link(eng.max_index(index[:, 8:16], values[:, 8:16], x))

            def halves(i, h):
                n, q = tile_rows(i), QUADS * i + h // 2
                eng.wait_ge(sco_ready, q + 1)
                for p in range(2):
                    top16(tv[0:n, p, :], ti[0:n, p, :], sco[0:n, q % 2, 2 * (h % 2) + p, :])

            def candidates(i, h):
                n = tile_rows(i)
                link(eng.tensor_copy(tif[0:n, :, :], ti[0:n, :, :]))
                link(eng.tensor_tensor(cand[0:n, :, :], tv[0:n, 0, :].unsqueeze(2).to_broadcast([n, TOPK, TOPK]),
                                       tv[0:n, 1, :].unsqueeze(1).to_broadcast([n, TOPK, TOPK]), ALU.add))
                flat = cand[0:n, :, :].rearrange("p a b -> p (a b)")
                top16(cv[0:n, :], ci[0:n, :], flat)
                signal(eng.tensor_scalar(nmx[0:n, :], cv[0:n, 0:1], -1.0, None, ALU.mult), top_ready, PH * i + h + 1)

            def keys_named(i, p):
                n = tile_rows(i)
                if p == 0:
                    link(eng.tensor_scalar(ca[0:n, 0, :], ci[0:n, :], 4, None, ALU.logical_shift_right))
                    link(eng.tensor_scalar(ca[0:n, 1, :], ci[0:n, :], TOPK - 1, None, ALU.bitwise_and))
                    link(eng.tensor_copy(caf[0:n, :, :], ca[0:n, :, :]))
                link(eng.tensor_tensor(eq[0:n, :, :], caf[0:n, p, :].unsqueeze(2).to_broadcast([n, TOPK, TOPK]),
                                       cst[0:n, C_IOTA:C_IOTA + TOPK].unsqueeze(1).to_broadcast([n, TOPK, TOPK]), ALU.is_equal))
                link(eng.tensor_tensor(eq[0:n, :, :], eq[0:n, :, :], tif[0:n, p, :].unsqueeze(1).to_broadcast([n, TOPK, TOPK]), ALU.mult))
                link(eng.tensor_reduce(e12[0:n, p, :], eq[0:n, :, :], AX, ALU.add))

            def experts(i, h):
                n, s = tile_rows(i), i % 2
                keys_named(i, 1)
                link(eng.scalar_tensor_tensor(out=e12[0:n, 0, :], in0=e12[0:n, 0, :], scalar=float(KEYS), in1=e12[0:n, 1, :], op0=ALU.mult, op1=ALU.add))
                link(eng.tensor_copy(idx[0:n, s, TOPK * h:TOPK * (h + 1)], e12[0:n, 0, :]))
                eng.wait_ge(ex_ready, PH * i + h + 1)
                link(eng.reciprocal(exs[0:n, 1:2], exs[0:n, 0:1]))
                signal(eng.tensor_scalar(gw[0:n, s, TOPK * h:TOPK * (h + 1)], ex[0:n, :], exs[0:n, 1:2], None, ALU.mult), idx_ready, PH * i + h + 1)

            def finish(i):
                n, s = tile_rows(i), i % 2
                eng.wait_ge(v_used, end_of(i))
                for h in range(2):
                    ins = eng.tensor_tensor(y[0:n, s, 512 * h:512 * (h + 1)], y[0:n, s, 512 * h:512 * (h + 1)], acc[h][0:n, :], ALU.add)
                    if h:
                        signal(ins, y_ready, i + 1)
                    else:
                        link(ins)

            residual(0)
            norm(0)
            for m, b in enumerate((*acc, qb, kb)):
                eng.wait_ge(kt_ready, m + 1)
                signal(eng.tensor_copy(skT[:, 4 * m:4 * m + 4, :], b[:, :].rearrange("p (c t) -> p c t", c=4)), skT_ready, m + 1)
            halves(0, 0)
            candidates(0, 0)
            keys_named(0, 0)
            experts(0, 0)
            for t in range(STEPS):
                tile, k = step_no(t)
                if tile == NT and k == 0:
                    eng.wait_ge(h2_rep, 48)
                eng.wait_ge(row_in[t % RING], 16 * (t // RING + 1))
                if t >= 4:
                    eng.wait_ge(gel_ready, t - 3)
                u = ring[:, t % RING, 0:D]
                eng.tensor_tensor_reduce(u, u, h2[:, tile % 2, :], 1.0, 0.0, ALU.mult, ALU.add, dots[:, t % 4:t % 4 + 1]).then_inc(dot_ready, 1)
                if tile and k == 1:
                    finish(tile - 1)
                if tile < NT:
                    if k == SUM_AT:
                        residual(tile + 1)
                    if k == NORM_AT:
                        norm(tile + 1)
                    for i, h in heads_at(tile, k, RETRIEVE_AT[3]):
                        experts(i, h)
                    for i, h in heads_at(tile, k, RETRIEVE_AT[2]):
                        keys_named(i, 0)
                    for i, h in heads_at(tile, k, RETRIEVE_AT[1]):
                        candidates(i, h)
                    for i, h in heads_at(tile, k, RETRIEVE_AT[0]):
                        halves(i, h)
            finish(NT)


_IN = ["x_prompt", "x_sample", "cache_kv_g1", "cache_kv_g2", "cache_kv_g3", "state_conv", "norm1_w", "w_in", "q_norm_w", "k_norm_w",
       "conv_w", "conv_b", "conv_ln_g", "conv_ln_b", "w_conv_proj", "w_attn_proj", "w_out", "norm2_w", "w_peer_q", "peer_sub_keys"]
_OUT = [("y_p", (1, SEQ, D)), ("y_s", (NB, NS, D)),
        ("kv0p", (1, 1, 128, 2, HG, HD)), ("kv1p", (1, 1, SEQ, 2, HG, HD)), ("kv2p", (1, 1, SEQ, 2, HG, HD)), ("conv_p", (1, 1, PAD, D)),
        ("kv0s", (1, NB, NS, 2, HG, HD)), ("kv1s", (1, NB, NS, 2, HG, HD)), ("kv2s", (1, NB, NS, 2, HG, HD)), ("conv_s", (1, NB, PAD, D))]


def program(nc, a):
    def scratch(name, shape):
        return nc.dram_tensor("x_" + name, shape, F32, kind="Internal").ap()

    sc = {"attn": [scratch(f"attn{g}", [SEQ, HG * ACCW]) for g in range(NG)],
          "q_smp": [scratch(f"q{g}", [SMP, GW]) for g in range(NG)],
          "gates": scratch("gates", [DC, P, TOK])}
    with ExitStack() as ctx:
        cst = ctx.enter_context(nc.sbuf_tensor("cst", [P, C_W], F32))
        yT = ctx.enter_context(nc.sbuf_tensor("yT", [P, DC, TOK], F32))
        hT = ctx.enter_context(nc.sbuf_tensor("hT", [P, DC, TOK], F32))
        mT = hT
        w_in = [ctx.enter_context(nc.semaphore(f"w_in{i}")) for i in range(2)]
        wring = ctx.enter_context(nc.sbuf_tensor("wring", [P, 2, DC, 512], F32))
        late = {"wo_in": [ctx.enter_context(nc.semaphore(f"wo_in{i}")) for i in range(2)],
                "x_in": ctx.enter_context(nc.semaphore("x_in0"))}
        with nc.sbuf_tensor("qk", [P, 2, 2, 4, SEQ], F32) as qk, nc.sbuf_tensor("S", [P, NG, HG, SMP], F32) as S:
            gates_in = front(nc, a, sc, cst, yT, hT, wring, w_in, qk, S, a["trig"])
            middle(nc, a, sc, cst, yT, hT, mT, wring, gates_in, qk, S, late)
        first = gates_in[2]
        peer(nc, a, cst, yT, mT, [wring[:, first], wring[:, 1 - first]], late)


def kernel(**inputs):
    import concourse.bacc as _bacc
    from concourse.bass_utils import run_bass_kernel_spmd as _run

    nc = _bacc.Bacc("TRN2", target_bir_lowering=False, num_devices=1)
    arrays = {name: np.ascontiguousarray(inputs[name]) for name in _IN}
    arrays["expert_uv"] = np.concatenate([inputs["expert_u"][0], inputs["expert_v"][0]], axis=1)
    arrays["consts"], arrays["trig"] = shape_constants()
    a = {name: nc.dram_tensor("in_" + name, x.shape, mybir.dt.from_np(x.dtype), kind="ExternalInput").ap() for name, x in arrays.items()}
    a |= {name: nc.dram_tensor("out_" + name, shape, F32, kind="ExternalOutput").ap() for name, shape in _OUT}
    program(nc, a)
    r = _run(nc, [{"in_" + name: x for name, x in arrays.items()}], core_ids=[0])
    return tuple(r.results[0]["out_" + name] for name, _ in _OUT)
```
